# Optimizing a Trainium2 kernel written in Bass

```python
import math
import jax, jax.numpy as jnp
from jax import lax
import numpy as np

D_MODEL = 2048
BATCH = 1
SEQ = 256
DEPTH = 1

HEAD_DIM = 64
Q_CHUNK = 128
A_CONFIGS = ((128, 1), (512, 4), (2048, 16))
N_A_GROUPS = len(A_CONFIGS)
A_HEADS_PER_GROUP = 4
A_HEADS = N_A_GROUPS * A_HEADS_PER_GROUP
A_BLOCK = 128
B_HEADS = 8
MOBA_BLOCK = 256
MOBA_TOPK = 3
C_KV_HEADS = 3
C_GROUP = 4
C_HEADS = C_KV_HEADS * C_GROUP
CMP_STRIDE = 16
CMP_LEN = 2 * CMP_STRIDE
CMP_HIDDEN = 128
SLC_BLOCK = 64
SLC_TOPN = 16
WIN = 512
FORCE_SCORE = 1e9
N_HEADS = A_HEADS + B_HEADS + C_HEADS
MIX_WIDTH = N_HEADS * HEAD_DIM
A_WIDTH = 3 * A_HEADS * HEAD_DIM
B_WIDTH = 3 * B_HEADS * HEAD_DIM
C_Q_WIDTH = C_HEADS * HEAD_DIM
C_KV_WIDTH = 6 * C_KV_HEADS * HEAD_DIM
C_GATE_WIDTH = 3 * C_HEADS
IN_WIDTH = A_WIDTH + B_WIDTH + C_Q_WIDTH + C_KV_WIDTH + C_GATE_WIDTH
D_FF = 5632
CONV_WIDTH = 3
N_BUCKETS = 32
T5_MAX_DIST = 2048
EPS = 1e-6
NEG = -1e30
Q_SCALE = HEAD_DIM ** -0.5


def rmsnorm(x, g):
    x32 = x.astype(jnp.float32)
    y = x32 * lax.rsqrt(jnp.mean(x32 * x32, axis=-1, keepdims=True) + EPS)
    return (y * g.astype(jnp.float32)).astype(x.dtype)

def t5_bucket(dist):
    n = jnp.maximum(dist, 0)
    max_exact = N_BUCKETS // 2
    nf = jnp.maximum(n, 1).astype(jnp.float32)
    large = max_exact + (jnp.log(nf / max_exact) / math.log(T5_MAX_DIST / max_exact)
                         * (N_BUCKETS - max_exact)).astype(jnp.int32)
    large = jnp.minimum(large, N_BUCKETS - 1)
    return jnp.where(n < max_exact, n, large)

def masked_softmax(s, mask):
    s32 = jnp.where(mask, s.astype(jnp.float32), NEG)
    m = jnp.max(s32, axis=-1, keepdims=True)
    e = jnp.where(mask, jnp.exp(s32 - m), 0.0)
    den = jnp.sum(e, axis=-1, keepdims=True)
    p = e / jnp.maximum(den, 1e-30)
    lse = m[..., 0] + jnp.log(jnp.maximum(den[..., 0], 1e-30))
    return p, lse

def dilated_group(q, k, v, window, dilation, tbl):
    B, S, H, dh = q.shape
    L = S // dilation
    nq = -(-L // A_BLOCK)
    Lp = nq * A_BLOCK
    nback = window // dilation

    def to_class(t):
        t = t.reshape(B, L, dilation, H, dh).transpose(0, 2, 3, 1, 4)
        return jnp.pad(t, ((0, 0), (0, 0), (0, 0), (0, Lp - L), (0, 0)))

    def band(t):
        tp = jnp.pad(t, ((0, 0), (0, 0), (0, 0), (A_BLOCK, 0), (0, 0)))
        prev = tp[:, :, :, :Lp].reshape(B, dilation, H, nq, A_BLOCK, dh)
        cur = t.reshape(B, dilation, H, nq, A_BLOCK, dh)
        return jnp.concatenate([prev, cur], axis=4)

    qb = to_class(q).reshape(B, dilation, H, nq, A_BLOCK, dh)
    kb = band(to_class(k))
    vb = band(to_class(v))
    a = jnp.arange(A_BLOCK)[:, None]
    bk = jnp.arange(2 * A_BLOCK)[None, :]
    rel = a + A_BLOCK - bk
    key_idx = jnp.arange(nq)[:, None, None] * A_BLOCK - A_BLOCK + bk[None]
    mask = (rel >= 0)[None] & (rel <= nback)[None] & (key_idx >= 0)
    bias = tbl[:, t5_bucket(rel * dilation)]
    s = jnp.einsum('bdhnqe,bdhnke->bdhnqk', qb, kb) + bias[:, None]
    p, lse = masked_softmax(s, mask)
    o = jnp.einsum('bdhnqk,bdhnke->bdhnqe', p.astype(v.dtype), vb)
    o = o.reshape(B, dilation, H, Lp, dh)[:, :, :, :L].transpose(0, 3, 1, 2, 4).reshape(B, S, H, dh)
    lse = lse.reshape(B, dilation, H, Lp)[:, :, :, :L].transpose(0, 3, 1, 2).reshape(B, S, H)
    return o, lse

def dilated_mixer(pA, tbl_a):
    B, S = pA.shape[:2]
    outs, lses = [], []
    for g, (w, d) in enumerate(A_CONFIGS):
        o, lse = dilated_group(pA[:, :, g, 0] * Q_SCALE, pA[:, :, g, 1], pA[:, :, g, 2], w, d,
                               tbl_a[g * A_HEADS_PER_GROUP:(g + 1) * A_HEADS_PER_GROUP])
        outs.append(o)
        lses.append(lse)
    alpha = jax.nn.softmax(jnp.stack(lses, axis=2), axis=2)
    o = jnp.stack(outs, axis=2) * alpha[..., None].astype(outs[0].dtype)
    return o.reshape(B, S, A_HEADS * HEAD_DIM)

def moba_mixer(q, k, v, tbl):
    B, S, H, dh = q.shape
    q, k, v = (t.transpose(0, 2, 1, 3) for t in (q, k, v))
    nb = -(-S // MOBA_BLOCK)
    Sp = nb * MOBA_BLOCK
    kp = jnp.pad(k, ((0, 0), (0, 0), (0, Sp - S), (0, 0)))
    vp = jnp.pad(v, ((0, 0), (0, 0), (0, Sp - S), (0, 0)))
    kb = kp.reshape(B, H, nb, MOBA_BLOCK, dh)
    vb = vp.reshape(B, H, nb, MOBA_BLOCK, dh)
    kmean = jnp.mean(kb.astype(jnp.float32), axis=3).astype(k.dtype)
    topk = min(MOBA_TOPK, nb)
    ar_b = jnp.arange(B)[:, None, None, None]
    ar_h = jnp.arange(H)[None, :, None, None]
    blk_off = jnp.arange(MOBA_BLOCK)

    def chunk(c):
        start = c * Q_CHUNK
        t = start + jnp.arange(Q_CHUNK)
        ob = start // MOBA_BLOCK
        qc = lax.dynamic_slice_in_dim(q, start, Q_CHUNK, axis=2)
        gate = jnp.einsum('bhqe,bhne->bhqn', qc, kmean).astype(jnp.float32)
        past = jnp.arange(nb) < ob
        gate = jnp.where(past, gate, NEG)
        _, idx = lax.top_k(gate, topk)
        sel_ok = idx < ob
        ks = kb[ar_b, ar_h, idx].reshape(B, H, Q_CHUNK, topk * MOBA_BLOCK, dh)
        vs = vb[ar_b, ar_h, idx].reshape(B, H, Q_CHUNK, topk * MOBA_BLOCK, dh)
        pos_s = (idx[..., None] * MOBA_BLOCK + blk_off).reshape(B, H, Q_CHUNK, topk * MOBA_BLOCK)
        mask_s = jnp.repeat(sel_ok, MOBA_BLOCK, axis=-1)
        ko = lax.dynamic_slice_in_dim(kp, ob * MOBA_BLOCK, MOBA_BLOCK, axis=2)
        vo = lax.dynamic_slice_in_dim(vp, ob * MOBA_BLOCK, MOBA_BLOCK, axis=2)
        pos_o = ob * MOBA_BLOCK + blk_off
        mask_o = jnp.broadcast_to(pos_o[None, :] <= t[:, None], (B, H, Q_CHUNK, MOBA_BLOCK))
        s_s = (jnp.einsum('bhqe,bhqke->bhqk', qc, ks)
               + tbl[ar_h, t5_bucket(t[None, None, :, None] - pos_s)])
        s_o = (jnp.einsum('bhqe,bhke->bhqk', qc, ko)
               + tbl[:, t5_bucket(t[:, None] - pos_o[None, :])][None])
        p, _ = masked_softmax(jnp.concatenate([s_s, s_o], -1), jnp.concatenate([mask_s, mask_o], -1))
        p = p.astype(v.dtype)
        n_sel = topk * MOBA_BLOCK
        return (jnp.einsum('bhqk,bhqke->bhqe', p[..., :n_sel], vs)
                + jnp.einsum('bhqk,bhke->bhqe', p[..., n_sel:], vo))

    outs = lax.map(chunk, jnp.arange(S // Q_CHUNK))
    return outs.transpose(1, 0, 3, 2, 4).reshape(B, S, H * dh)

def nsa_mixer(q, kvC, gates, cmp_w1, cmp_w2, cmp_pe, tbl):
    B, S, _, dh = q.shape
    KV, G = C_KV_HEADS, C_GROUP
    q = q.reshape(B, S, KV, G, dh).transpose(0, 2, 3, 1, 4)
    k_cmp, v_cmp, k_slc, v_slc, k_win, v_win = (kvC[:, :, i].transpose(0, 2, 1, 3) for i in range(6))
    gates = gates.reshape(B, S, KV, G, 3).transpose(0, 2, 3, 1, 4)
    n_cmp = S // CMP_STRIDE - 1
    n_slc = S // SLC_BLOCK
    n_sel = min(SLC_TOPN, n_slc)

    def compress(t, w1, w2, pe):
        sub = t.reshape(B, KV, S // CMP_STRIDE, CMP_STRIDE, dh)
        blocks = jnp.concatenate([sub[:, :, :-1], sub[:, :, 1:]], axis=3) + pe
        return jax.nn.gelu(blocks.reshape(B, KV, n_cmp, CMP_LEN * dh) @ w1) @ w2

    kc = compress(k_cmp, cmp_w1[0], cmp_w2[0], cmp_pe[0])
    vc = compress(v_cmp, cmp_w1[1], cmp_w2[1], cmp_pe[1])
    cmp_end = jnp.arange(n_cmp) * CMP_STRIDE + CMP_LEN - 1
    ci = jnp.arange(n_cmp)[:, None] * CMP_STRIDE
    sj = jnp.arange(n_slc)[None, :] * SLC_BLOCK
    overlap = ((ci < sj + SLC_BLOCK) & (ci + CMP_LEN > sj)).astype(jnp.float32)
    ksb = k_slc.reshape(B, KV, n_slc, SLC_BLOCK, dh)
    vsb = v_slc.reshape(B, KV, n_slc, SLC_BLOCK, dh)
    kwp = jnp.pad(k_win, ((0, 0), (0, 0), (WIN, 0), (0, 0)))
    vwp = jnp.pad(v_win, ((0, 0), (0, 0), (WIN, 0), (0, 0)))
    tbl_kgn = tbl.reshape(KV, G, N_BUCKETS)
    tbl_kng = tbl_kgn.transpose(0, 2, 1)
    ar_b = jnp.arange(B)[:, None, None, None]
    ar_kv = jnp.arange(KV)[None, :, None, None]
    slc_off = jnp.arange(SLC_BLOCK)
    jj = jnp.arange(n_slc)[None, :]

    def chunk(c):
        start = c * Q_CHUNK
        t = start + jnp.arange(Q_CHUNK)
        qc = lax.dynamic_slice_in_dim(q, start, Q_CHUNK, axis=3)
        s_c = jnp.einsum('bkgqe,bkne->bkgqn', qc, kc)
        p_c, _ = masked_softmax(s_c, cmp_end[None, :] <= t[:, None])
        o_c = jnp.einsum('bkgqn,bkne->bkgqe', p_c.astype(v_cmp.dtype), vc)
        imp = jnp.einsum('bkgqn,nj->bkqj', p_c, overlap)
        own = (t // SLC_BLOCK)[:, None]
        valid = jj <= own
        forced = (jj == 0) | (jj == own) | (jj == own - 1)
        score = jnp.where(valid, jnp.where(forced, FORCE_SCORE, imp), -1.0)
        _, idx = lax.top_k(score, n_sel)
        ks = ksb[ar_b, ar_kv, idx].reshape(B, KV, Q_CHUNK, n_sel * SLC_BLOCK, dh)
        vs = vsb[ar_b, ar_kv, idx].reshape(B, KV, Q_CHUNK, n_sel * SLC_BLOCK, dh)
        pos = (idx[..., None] * SLC_BLOCK + slc_off).reshape(B, KV, Q_CHUNK, n_sel * SLC_BLOCK)
        dist = t[None, None, :, None] - pos
        bias_s = tbl_kng[ar_kv, t5_bucket(dist)].transpose(0, 1, 4, 2, 3)
        s_s = jnp.einsum('bkgqe,bkqse->bkgqs', qc, ks) + bias_s
        p_s, _ = masked_softmax(s_s, (dist >= 0)[:, :, None])
        o_s = jnp.einsum('bkgqs,bkqse->bkgqe', p_s.astype(v_slc.dtype), vs)
        kw = lax.dynamic_slice_in_dim(kwp, start, Q_CHUNK + WIN, axis=2)
        vw = lax.dynamic_slice_in_dim(vwp, start, Q_CHUNK + WIN, axis=2)
        pos_w = start - WIN + jnp.arange(Q_CHUNK + WIN)
        dist_w = t[:, None] - pos_w[None, :]
        mask_w = (dist_w >= 0) & (dist_w < WIN) & (pos_w[None, :] >= 0)
        s_w = jnp.einsum('bkgqe,bkse->bkgqs', qc, kw) + tbl_kgn[:, :, t5_bucket(dist_w)]
        p_w, _ = masked_softmax(s_w, mask_w)
        o_w = jnp.einsum('bkgqs,bkse->bkgqe', p_w.astype(v_win.dtype), vw)
        g = lax.dynamic_slice_in_dim(gates, start, Q_CHUNK, axis=3).astype(o_c.dtype)
        return g[..., 0:1] * o_c + g[..., 1:2] * o_s + g[..., 2:3] * o_w

    outs = lax.map(chunk, jnp.arange(S // Q_CHUNK))
    return outs.transpose(1, 0, 4, 2, 3, 5).reshape(B, S, C_HEADS * dh)

def conv_ffn(h, w_up, conv_w, conv_b, w_down):
    S = h.shape[1]
    u = h @ w_up
    up = jnp.pad(u, ((0, 0), (CONV_WIDTH - 1, 0), (0, 0)))
    acc = conv_b
    for j in range(CONV_WIDTH):
        acc = acc + conv_w[j] * up[:, CONV_WIDTH - 1 - j:CONV_WIDTH - 1 - j + S]
    a, g = jnp.split(acc, 2, axis=-1)
    return (jax.nn.silu(g) * a) @ w_down

def first_inputs(seed: int = 0) -> dict:
    key = jax.random.key(seed)
    ks = jax.random.split(key, 14)
    nrm = jax.random.normal
    f32 = jnp.float32
    return {
        "x": nrm(ks[0], (BATCH, SEQ, D_MODEL), f32),
        "rel_table": 0.5 * nrm(ks[1], (N_HEADS, N_BUCKETS), f32),
        "w_in": nrm(ks[2], (DEPTH, D_MODEL, IN_WIDTH), f32) * D_MODEL ** -0.5,
        "w_out": nrm(ks[3], (DEPTH, MIX_WIDTH, D_MODEL), f32) * MIX_WIDTH ** -0.5,
        "cmp_w1": nrm(ks[4], (DEPTH, 2, CMP_LEN * HEAD_DIM, CMP_HIDDEN), f32) * (CMP_LEN * HEAD_DIM) ** -0.5,
        "cmp_w2": nrm(ks[5], (DEPTH, 2, CMP_HIDDEN, HEAD_DIM), f32) * CMP_HIDDEN ** -0.5,
        "cmp_pe": 0.5 * nrm(ks[6], (DEPTH, 2, CMP_LEN, HEAD_DIM), f32),
        "norm_attn": 1.0 + 0.05 * nrm(ks[7], (DEPTH, D_MODEL), f32),
        "norm_mlp": 1.0 + 0.05 * nrm(ks[8], (DEPTH, D_MODEL), f32),
        "w_up": nrm(ks[9], (DEPTH, D_MODEL, 2 * D_FF), f32) * D_MODEL ** -0.5,
        "conv_w": nrm(ks[10], (DEPTH, CONV_WIDTH, 2 * D_FF), f32) * CONV_WIDTH ** -0.5,
        "conv_b": 0.02 * nrm(ks[11], (DEPTH, 2 * D_FF), f32),
        "w_down": nrm(ks[12], (DEPTH, D_FF, D_MODEL), f32) * D_FF ** -0.5,
        "norm_final": 1.0 + 0.05 * nrm(ks[13], (D_MODEL,), f32),
    }

def first_block(x, rel_table, w_in, w_out, cmp_w1, cmp_w2, cmp_pe, norm_attn, norm_mlp,
              w_up, conv_w, conv_b, w_down, norm_final):
    B, S, _ = x.shape
    tbl_a = rel_table[:A_HEADS]
    tbl_b = rel_table[A_HEADS:A_HEADS + B_HEADS]
    tbl_c = rel_table[A_HEADS + B_HEADS:]
    for l in range(DEPTH):
        h = rmsnorm(x, norm_attn[l])
        proj = h @ w_in[l]
        pA = proj[..., :A_WIDTH].reshape(B, S, N_A_GROUPS, 3, A_HEADS_PER_GROUP, HEAD_DIM)
        pB = proj[..., A_WIDTH:A_WIDTH + B_WIDTH].reshape(B, S, 3, B_HEADS, HEAD_DIM)
        pC = proj[..., A_WIDTH + B_WIDTH:]
        o_a = dilated_mixer(pA, tbl_a)
        o_b = moba_mixer(pB[:, :, 0] * Q_SCALE, pB[:, :, 1], pB[:, :, 2], tbl_b)
        q_c = pC[..., :C_Q_WIDTH].reshape(B, S, C_HEADS, HEAD_DIM) * Q_SCALE
        kv_c = pC[..., C_Q_WIDTH:C_Q_WIDTH + C_KV_WIDTH].reshape(B, S, 6, C_KV_HEADS, HEAD_DIM)
        g_c = jax.nn.sigmoid(pC[..., C_Q_WIDTH + C_KV_WIDTH:].reshape(B, S, C_HEADS, 3))
        o_c = nsa_mixer(q_c, kv_c, g_c, cmp_w1[l], cmp_w2[l], cmp_pe[l], tbl_c)
        x = x + jnp.concatenate([o_a, o_b, o_c], axis=-1) @ w_out[l]
        h = rmsnorm(x, norm_mlp[l])
        x = x + conv_ffn(h, w_up[l], conv_w[l], conv_b[l], w_down[l])
    return rmsnorm(x, norm_final)


PLE_DIM = 256
RMS_EPS = 1e-6
N_HEADS_2 = 16
QK_NOPE_DIM = 128
QK_ROPE_DIM = 64
V_HEAD_DIM = 128
QK_HEAD_DIM = QK_NOPE_DIM + QK_ROPE_DIM
Q_LORA_RANK = 768
KV_LORA_RANK = 512
ROPE_THETA = 10000.0
Q_BLOCK = 128
D_RNN = D_MODEL
RNN_BLOCKS = 16
RNN_BLOCK_DIM = D_RNN // RNN_BLOCKS
CONV_WIDTH_2 = 4
LRU_C = 8.0
PEER_HEADS = 8
N_KEYS = 128
N_EXPERTS = N_KEYS * N_KEYS
PEER_QUERY_DIM = 256
PEER_HALF = PEER_QUERY_DIM // 2
PEER_TOPK = 16
PEER_CHUNK = 128
IN_SPLITS = (Q_LORA_RANK, KV_LORA_RANK, QK_ROPE_DIM, D_RNN, D_RNN, D_MODEL, D_MODEL)
IN_WIDTH_2 = Q_LORA_RANK + KV_LORA_RANK + QK_ROPE_DIM + 2 * D_RNN + 2 * D_MODEL


def rms_norm(x, g):
    xf = x.astype(jnp.float32)
    y = xf * lax.rsqrt(jnp.mean(xf * xf, axis=-1, keepdims=True) + RMS_EPS)
    return (y * g.astype(jnp.float32)).astype(x.dtype)

def rope(x, pos):
    half = QK_ROPE_DIM // 2
    inv_freq = 1.0 / (ROPE_THETA ** (jnp.arange(half, dtype=jnp.float32) / half))
    ang = pos.astype(jnp.float32)[:, None] * inv_freq[None, :]
    cos = jnp.cos(ang)[:, None, :]
    sin = jnp.sin(ang)[:, None, :]
    xf = x.astype(jnp.float32)
    x1, x2 = xf[..., :half], xf[..., half:]
    return jnp.concatenate([x1 * cos - x2 * sin, x2 * cos + x1 * sin], axis=-1).astype(x.dtype)

def split_columns(z):
    offs, acc = [], 0
    for w in IN_SPLITS[:-1]:
        acc += w
        offs.append(acc)
    return jnp.split(z, offs, axis=-1)

def mla_branch(c_q, c_kv, k_r, q_norm, w_uq, kv_norm, w_ukv, w_attn_o):
    B, S, _ = c_q.shape
    pos = jnp.arange(S)
    q = (rms_norm(c_q, q_norm) @ w_uq).reshape(B, S, N_HEADS_2, QK_HEAD_DIM)
    q_nope = q[..., :QK_NOPE_DIM]
    q_pe = rope(q[..., QK_NOPE_DIM:], pos)
    kv = (rms_norm(c_kv, kv_norm) @ w_ukv).reshape(B, S, N_HEADS_2, QK_NOPE_DIM + V_HEAD_DIM)
    k_nope, v = kv[..., :QK_NOPE_DIM], kv[..., QK_NOPE_DIM:]
    k_pe = rope(k_r[:, :, None, :], pos)[:, :, 0, :]
    scale = QK_HEAD_DIM ** -0.5
    n_blk = S // Q_BLOCK

    def to_blocks(t):
        return t.reshape(B, n_blk, Q_BLOCK, *t.shape[2:]).swapaxes(0, 1)

    def attend(args):
        qn, qp, blk = args
        s = (jnp.einsum('bqhd,bkhd->bhqk', qn, k_nope, preferred_element_type=jnp.float32)
             + jnp.einsum('bqhd,bkd->bhqk', qp, k_pe, preferred_element_type=jnp.float32))
        q_pos = blk * Q_BLOCK + jnp.arange(Q_BLOCK)
        s = jnp.where(pos[None, :] <= q_pos[:, None], s * scale, -jnp.inf)
        prob = jax.nn.softmax(s, axis=-1)
        return jnp.einsum('bhqk,bkhd->bqhd', prob.astype(v.dtype), v)

    o = lax.map(attend, (to_blocks(q_nope), to_blocks(q_pe), jnp.arange(n_blk)))
    o = o.swapaxes(0, 1).reshape(B, S, N_HEADS_2 * V_HEAD_DIM)
    return o @ w_attn_o

def rglru_branch(x_r, y_r, conv_w, conv_b, w_rg_a, b_rg_a, w_rg_x, b_rg_x, lru_lambda, w_rnn_o):
    B, S, C = x_r.shape
    xc = lax.conv_general_dilated(x_r, conv_w[:, None, :], window_strides=(1,),
                                  padding=[(CONV_WIDTH_2 - 1, 0)],
                                  dimension_numbers=('NWC', 'WIO', 'NWC'),
                                  feature_group_count=C) + conv_b
    xb = xc.reshape(B, S, RNN_BLOCKS, RNN_BLOCK_DIM)
    r = jax.nn.sigmoid(jnp.einsum('bshi,hij->bshj', xb, w_rg_a) + b_rg_a).reshape(B, S, C)
    i = jax.nn.sigmoid(jnp.einsum('bshi,hij->bshj', xb, w_rg_x) + b_rg_x).reshape(B, S, C)
    log_a = -LRU_C * r.astype(jnp.float32) * jax.nn.softplus(-lru_lambda.astype(jnp.float32))
    a = jnp.exp(log_a)
    mult = jnp.sqrt(-jnp.expm1(2.0 * log_a))
    mult = jnp.where((jnp.arange(S) == 0)[None, :, None], 1.0, mult)
    b = mult * (i * xc).astype(jnp.float32)

    def combine(left, right):
        a1, b1 = left
        a2, b2 = right
        return a1 * a2, a2 * b1 + b2

    _, h = lax.associative_scan(combine, (a, b), axis=1)
    y = h.astype(x_r.dtype) * jax.nn.gelu(y_r)
    return y @ w_rnn_o

def peer_ffn(x, w_peer_q, peer_subkeys, peer_u, peer_v):
    B, S, D = x.shape
    q = (x @ w_peer_q).reshape(B, S, PEER_HEADS, 2, PEER_HALF)
    s = jnp.einsum('bshcd,hcnd->bshcn', q, peer_subkeys, preferred_element_type=jnp.float32)
    top_s, top_i = lax.top_k(s, PEER_TOPK)
    cand = top_s[..., 0, :, None] + top_s[..., 1, None, :]
    cand = cand.reshape(B, S, PEER_HEADS, PEER_TOPK * PEER_TOPK)
    best_s, best_c = lax.top_k(cand, PEER_TOPK)
    i1 = jnp.take_along_axis(top_i[..., 0, :], best_c // PEER_TOPK, axis=-1)
    i2 = jnp.take_along_axis(top_i[..., 1, :], best_c % PEER_TOPK, axis=-1)
    experts = i1 * N_KEYS + i2
    gates = jax.nn.softmax(best_s, axis=-1).astype(x.dtype)
    T = B * S
    HK = PEER_HEADS * PEER_TOPK
    xs = x.reshape(T // PEER_CHUNK, PEER_CHUNK, D)
    es = experts.reshape(T // PEER_CHUNK, PEER_CHUNK, HK)
    gs = gates.reshape(T // PEER_CHUNK, PEER_CHUNK, HK)

    def chunk(args):
        xc, ec, gc = args
        u = peer_u[ec]
        act = jax.nn.gelu(jnp.einsum('tkd,td->tk', u, xc))
        return jnp.einsum('tk,tkd->td', gc * act, peer_v[ec])

    return lax.map(chunk, (xs, es, gs)).reshape(B, S, D)

def second_inputs(seed: int = 0) -> dict:
    key = jax.random.key(seed)
    ks = iter(jax.random.split(key, 40))
    f32 = jnp.float32

    def nrm(shape, scale):
        return jax.random.normal(next(ks), shape, f32) * scale

    def gain(shape):
        return 1.0 + nrm(shape, 0.05)

    L = DEPTH
    u = jax.random.uniform(next(ks), (L, D_RNN), f32, 0.9, 0.999)
    s_root = u ** (1.0 / LRU_C)
    lru_lambda = jnp.log(s_root) - jnp.log1p(-s_root)
    return {
        'x': nrm((BATCH, SEQ, D_MODEL), 1.0),
        'p': nrm((DEPTH, BATCH, SEQ, PLE_DIM), 1.0),
        'attn_norm': gain((L, D_MODEL)),
        'w_in': nrm((L, D_MODEL, IN_WIDTH_2), D_MODEL ** -0.5),
        'b_gate': nrm((L, 2 * D_MODEL), 0.01),
        'q_norm': gain((L, Q_LORA_RANK)),
        'w_uq': nrm((L, Q_LORA_RANK, N_HEADS_2 * QK_HEAD_DIM), Q_LORA_RANK ** -0.5),
        'kv_norm': gain((L, KV_LORA_RANK)),
        'w_ukv': nrm((L, KV_LORA_RANK, N_HEADS_2 * (QK_NOPE_DIM + V_HEAD_DIM)), KV_LORA_RANK ** -0.5),
        'w_attn_o': nrm((L, N_HEADS_2 * V_HEAD_DIM, D_MODEL), (N_HEADS_2 * V_HEAD_DIM) ** -0.5),
        'conv_w': nrm((L, CONV_WIDTH_2, D_RNN), CONV_WIDTH_2 ** -0.5),
        'conv_b': nrm((L, D_RNN), 0.01),
        'w_rg_a': nrm((L, RNN_BLOCKS, RNN_BLOCK_DIM, RNN_BLOCK_DIM), RNN_BLOCK_DIM ** -0.5),
        'b_rg_a': nrm((L, RNN_BLOCKS, RNN_BLOCK_DIM), 0.01),
        'w_rg_x': nrm((L, RNN_BLOCKS, RNN_BLOCK_DIM, RNN_BLOCK_DIM), RNN_BLOCK_DIM ** -0.5),
        'b_rg_x': nrm((L, RNN_BLOCKS, RNN_BLOCK_DIM), 0.01),
        'lru_lambda': lru_lambda,
        'w_rnn_o': nrm((L, D_RNN, D_MODEL), D_RNN ** -0.5),
        'w_out': nrm((L, D_MODEL, D_MODEL), D_MODEL ** -0.5),
        'ffn_norm': gain((L, D_MODEL)),
        'w_peer_q': nrm((L, D_MODEL, PEER_HEADS * PEER_QUERY_DIM), D_MODEL ** -0.5),
        'peer_subkeys': nrm((L, PEER_HEADS, 2, N_KEYS, PEER_HALF), PEER_HALF ** -0.5),
        'peer_u': nrm((L, N_EXPERTS, D_MODEL), D_MODEL ** -0.5),
        'peer_v': nrm((L, N_EXPERTS, D_MODEL), PEER_HEADS ** -0.5),
        'ple_norm': gain((L, D_MODEL)),
        'w_ple_gate': nrm((L, D_MODEL, D_MODEL), D_MODEL ** -0.5),
        'w_ple_proj': nrm((L, PLE_DIM, D_MODEL), PLE_DIM ** -0.5),
        'final_norm': gain((D_MODEL,)),
    }

def second_block(x, p, attn_norm, w_in, b_gate, q_norm, w_uq, kv_norm, w_ukv, w_attn_o,
              conv_w, conv_b, w_rg_a, b_rg_a, w_rg_x, b_rg_x, lru_lambda, w_rnn_o, w_out,
              ffn_norm, w_peer_q, peer_subkeys, peer_u, peer_v, ple_norm, w_ple_gate,
              w_ple_proj, final_norm):
    h = x
    for l in range(DEPTH):
        n = rms_norm(h, attn_norm[l])
        c_q, c_kv, k_r, x_r, y_r, ga, gr = split_columns(n @ w_in[l])
        g_attn = jax.nn.sigmoid(ga + b_gate[l, :D_MODEL])
        g_rnn = jax.nn.sigmoid(gr + b_gate[l, D_MODEL:])
        y_attn = mla_branch(c_q, c_kv, k_r, q_norm[l], w_uq[l], kv_norm[l], w_ukv[l], w_attn_o[l])
        y_rnn = rglru_branch(x_r, y_r, conv_w[l], conv_b[l], w_rg_a[l], b_rg_a[l],
                             w_rg_x[l], b_rg_x[l], lru_lambda[l], w_rnn_o[l])
        h = h + (g_attn * y_attn + g_rnn * y_rnn) @ w_out[l]
        h = h + peer_ffn(rms_norm(h, ffn_norm[l]), w_peer_q[l], peer_subkeys[l], peer_u[l], peer_v[l])
        gate = jax.nn.sigmoid(rms_norm(h, ple_norm[l]) @ w_ple_gate[l])
        h = h + gate * (p[l] @ w_ple_proj[l])
    return rms_norm(h, final_norm)


def setup_inputs(seed=0):
    out = dict(first_inputs(seed))
    for name, value in second_inputs(seed + 1).items():
        if name != "x":
            out[name + "_2"] = value
    return out


def reference(
    x, rel_table, w_in, w_out, cmp_w1, cmp_w2, cmp_pe, norm_attn, norm_mlp, w_up, conv_w,
    conv_b, w_down, norm_final, p_2, attn_norm_2, w_in_2, b_gate_2, q_norm_2, w_uq_2, kv_norm_2,
    w_ukv_2, w_attn_o_2, conv_w_2, conv_b_2, w_rg_a_2, b_rg_a_2, w_rg_x_2, b_rg_x_2,
    lru_lambda_2, w_rnn_o_2, w_out_2, ffn_norm_2, w_peer_q_2, peer_subkeys_2, peer_u_2,
    peer_v_2, ple_norm_2, w_ple_gate_2, w_ple_proj_2, final_norm_2,
):
    x = first_block(
        x, rel_table, w_in, w_out, cmp_w1, cmp_w2, cmp_pe, norm_attn, norm_mlp, w_up, conv_w,
        conv_b, w_down, norm_final,
    )
    return second_block(
        x, p_2, attn_norm_2, w_in_2, b_gate_2, q_norm_2, w_uq_2, kv_norm_2, w_ukv_2, w_attn_o_2,
        conv_w_2, conv_b_2, w_rg_a_2, b_rg_a_2, w_rg_x_2, b_rg_x_2, lru_lambda_2, w_rnn_o_2,
        w_out_2, ffn_norm_2, w_peer_q_2, peer_subkeys_2, peer_u_2, peer_v_2, ple_norm_2,
        w_ple_gate_2, w_ple_proj_2, final_norm_2,
    )


_drawn_inputs = setup_inputs


def setup_inputs(seed=0):
    import zlib

    import numpy as np

    out = dict(_drawn_inputs(seed))
    spreads = {}
    factors = {'b_gate_2': 8.0,
     'q_norm_2': 4.885,
     'kv_norm_2': 3.661,
     'b_rg_a_2': 64.0,
     'b_rg_x_2': 63.598,
     'ple_norm_2': 25.015,
     'conv_b_2': 5.594,
     'ffn_norm_2': 2.708}
    for name, (base, spread) in spreads.items():
        noise = np.random.default_rng([zlib.crc32(name.encode()), seed]).standard_normal(out[name].shape)
        drawn = base * np.exp(spread * noise) if base else spread * noise
        out[name] = __import__('jax').numpy.asarray(drawn.astype(out[name].dtype))
    for name, factor in factors.items():
        out[name] = (out[name] * factor).astype(out[name].dtype)
    return out
```

```python
import concourse.bass as bass
from concourse import mybir
from contextlib import ExitStack

S = 256
NSLOT = 7
SLOT = 2048
NEG = -1e30
LOW = -3.0e38

VEC = [("norm_attn", 16), ("norm_mlp", 16), ("norm_final", 16), ("attn_norm_2", 16), ("q_norm_2", 6),
       ("kv_norm_2", 4), ("ffn_norm_2", 16), ("ple_norm_2", 16), ("final_norm_2", 16), ("conv_w", 264),
       ("conv_b", 88), ("conv_w_2", 64), ("conv_b_2", 16), ("b_rg_a_2", 16), ("b_rg_x_2", 16),
       ("lru_lambda_2", 16), ("b_gate_2", 32)]
CST = [("ident", 128), ("exch", 128), ("mask", 256), ("cos", 256), ("sin", 256), ("cmp01", 30), ("cmpneg", 30), ("iota", 16)]


def offsets(table):
    at, out = 0, {}
    for name, n in table:
        out[name] = (at, at + n)
        at += n
    return out, at


VOFF, NVEC = offsets(VEC)
COFF, NCST = offsets(CST)


class Engine:

    def __init__(self, sem):
        self.sem, self.q, self.n, self.seen = sem, [], 0, {}

    def __call__(self, fn, waits=(), sig=True):
        self.q.append((self.fresh(waits), fn, (self.sem, 1) if sig else None))
        self.n += 1 if sig else 0
        return (self.sem, self.n) if sig else None

    def dma(self, fn, chan, waits=()):
        chan.n += 16
        self.q.append((self.fresh(waits), fn, (chan.sem, 16)))
        return (chan.sem, chan.n)

    def wait(self, waits):
        self.q.append((self.fresh(waits), None, None))

    def fresh(self, waits):
        out = []
        for t in waits:
            if t is not None and self.seen.get(id(t[0]), 0) < t[1]:
                self.seen[id(t[0])] = t[1]
                out.append(t)
        return out

    def last(self):
        return (self.sem, self.n) if self.n else None

    def play(self, eng):
        for waits, fn, inc in self.q:
            for sem, val in waits:
                eng.wait_ge(sem, val)
            if fn is not None:
                ins = fn(eng)
                if inc is not None:
                    ins.then_inc(*inc)


class Chan:

    def __init__(self, sem):
        self.sem, self.n = sem, 0


class Buf:

    def __init__(self, ap, chan=None):
        self.ap, self.chan, self.free = ap, chan, []


class Ring:
    def __init__(self, bufs):
        self.bufs, self.i = bufs, 0

    def next(self):
        b = self.bufs[self.i % len(self.bufs)]
        self.i += 1
        return b


def program(nc, D, out):
    fp32, u32, i32 = mybir.dt.float32, mybir.dt.uint32, mybir.dt.int32
    ALU, ACT, AX = mybir.AluOpType, mybir.ActivationFunctionType, mybir.AxisListType.X
    ctx = ExitStack()
    with ctx:
        def sb(name, cols, parts=128):
            return ctx.enter_context(nc.sbuf_tensor(name, [parts, cols], fp32))

        def sem(name):
            return ctx.enter_context(nc.semaphore(name))

        XT = sb("XT", 16 * S)[:, :].rearrange("p (k t) -> p k t", t=S)
        HT = sb("HT", 16 * S)[:, :].rearrange("p (k t) -> p k t", t=S)
        ring_sb = sb("ring", NSLOT * SLOT)
        vec = sb("vec", NVEC)
        cst = sb("cst", NCST)
        ones = sb("ones", 128)
        nrm = sb("nrm", 3 * S)
        NAR = 27648
        arena = sb("arena", NAR)
        banks = [ctx.enter_context(nc.psum_tensor(f"ps{i}", [128, 512], fp32)) for i in range(8)]

        P, A, V, G, SP = (Engine(sem(f"s_{n}")) for n in ("pe", "act", "dve", "pool", "sp"))
        ring = Ring([Buf(ring_sb[:, i * SLOT:(i + 1) * SLOT], Chan(sem(f"s_w{i}"))) for i in range(NSLOT)])
        rows = Ring([Buf(ring_sb[:, i * SLOT:(i + 1) * SLOT], Chan(sem(f"s_g{i}"))) for i in range(NSLOT)])
        PP = Ring([Buf(b[:, :]) for b in banks[0:3]])
        PT = Ring([Buf(b[:, :]) for b in banks[3:5]])
        PO = Ring([Buf(b[:, :]) for b in banks[5:8]])

        def vcol(name, i=0, n=1):
            a = VOFF[name][0] + i
            return vec[:, a:a + n]

        def cc(name):
            a, b = COFF[name]
            return cst[:, a:b]

        class Arena:
            def __init__(self):
                self.at = 0

            def __call__(self, cols):
                a = self.at
                self.at += cols
                assert self.at <= NAR, self.at
                return arena[:, a:a + cols]

        def fence():
            ends = [e.last() for e in (P, A, V, G)]
            for e in (P, A, V, G):
                e.wait(ends)

        def mm(o, l, r, start, stop, waits=(), sig=False):
            return P(lambda e: e.matmul(o, lhsT=l, rhs=r, start=start, stop=stop), waits, sig)

        def tr(o, i, waits=(), sig=False):
            idn = cc("ident")
            return P(lambda e: e.transpose(o, i, idn), waits, sig)

        def act(o, i, f, waits=(), **kw):
            return A(lambda e: e.activation(o, i, f, **kw), waits)

        def tt(o, a, b, op, waits=()):
            return V(lambda e: e.tensor_tensor(o, a, b, op), waits)

        def ts(o, a, s1, s2, op0, op1=None, waits=()):
            if op1 is None:
                return V(lambda e: e.tensor_scalar(o, a, s1, None, op0), waits)
            return V(lambda e: e.tensor_scalar(o, a, s1, s2, op0, op1), waits)

        def stt(o, a, s, b, op0, op1, waits=()):
            return V(lambda e: e.scalar_tensor_tensor(out=o, in0=a, scalar=s, in1=b, op0=op0, op1=op1), waits)

        def red(o, i, op, waits=(), **kw):
            return V(lambda e: e.tensor_reduce(o, i, AX, op, **kw), waits)

        def recip(o, i, waits=()):
            return V(lambda e: e.reciprocal(o, i), waits)

        def vcopy(o, i, waits=()):
            return V(lambda e: e.tensor_copy(o, i), waits)

        def vset(o, v, waits=()):
            return V(lambda e: e.memset(o, v), waits)

        def load(src, cols, parts=128):
            s = ring.next()
            dst = s.ap[0:parts, 0:cols]
            tok = SP.dma(lambda e: e.dma_start(dst, src), s.chan, s.free)
            s.free = []
            return s, tok

        def linT(w, n, rhs, rhs_toks, evac, m=128, pieces=1):
            kt = w.shape[2] // m
            ps = PP.next()
            step = kt // pieces
            o = ps.ap[0:m, 0:S]
            tok = None
            for p in range(pieces):
                s, ld = load(w[n, :, p * step * m:(p + 1) * step * m], step * m)
                for j in range(step):
                    k = p * step + j
                    tok = mm(o, s.ap[:, j * m:(j + 1) * m], rhs[:, k, :], k == 0, k == kt - 1,
                             [ld, rhs_toks[k]] + (ps.free if k == 0 else []), j == step - 1)
                s.free = [tok]
            ps.free = evac(n, o, tok)

        def linN(s, ld, lhs, lhs_toks, cols, c0, width, evac):
            kt = lhs.shape[1]
            for i in range(2):
                ps = PP.next()
                for k in range(kt):
                    tok = mm(ps.ap[:, 0:cols], lhs[:, k, i * 128:(i + 1) * 128],
                             s.ap[:, k * width + c0:k * width + c0 + cols], k == 0, k == kt - 1,
                             [ld, lhs_toks[k]] + (ps.free if k == 0 else []), k == kt - 1)
                ps.free = evac(i, ps.ap[:, 0:cols], tok)
            s.free = [tok]

        flip = [0]

        def copy(o, i, waits):
            flip[0] ^= 1
            if flip[0]:
                return act(o, i, ACT.Copy, waits)
            return vcopy(o, i, waits)

        def rmsnorm(src, gain, scratch, dst, nkt, toks):
            ps = PP.next()
            for k in range(nkt):
                t = act(scratch[:, k, :], src[:, k, :], ACT.Square, [toks[k]])
                t = mm(ps.ap[:, 0:S], ones[:, :], scratch[:, k, :], k == 0, k == nkt - 1,
                       [t, t_ones] + (ps.free if k == 0 else []), k == nkt - 1)
            var, dev, inv = (nrm[:, i * S:(i + 1) * S] for i in range(3))
            t = ts(var, ps.ap[:, 0:S], 1.0 / (nkt * 128), 1e-6, ALU.mult, ALU.add, [t])
            ps.free = [t]
            t = act(dev, var, ACT.Sqrt, [t])
            t = recip(inv, dev, [t])
            return [stt(dst[:, k, :], src[:, k, :], vcol(gain, k), inv, ALU.mult, ALU.mult, [t, toks[k], t_vec])
                    for k in range(nkt)]

        def residual(n, o, tok):
            t = tt(XT[:, n, :], o, XT[:, n, :], ALU.add, [tok])
            xt[n] = t
            return [t]

        class Smalls:
            def __init__(self, tile, n):
                self.ring = Ring([Buf(tile[:, 8 * i:8 * i + 8]) for i in range(n)])

        def softmax(job, SB, small):
            nk = (job["i"] + 1) * 128
            c = small.ring.next()
            parts, scale = job["parts"], job.get("scale", 1.0)
            free = c.free
            for n, u in enumerate(parts):
                ps = PP.next()
                for j, (l, r) in enumerate(u["qk"]):
                    tok = mm(ps.ap[:, 0:nk], l, r, j == 0, j == len(u["qk"]) - 1,
                             u["toks"] + (ps.free if j == 0 else []), j == len(u["qk"]) - 1)
                b = u["buf"] = SB.next()
                o, i0, i1, ac = b.ap[:, 0:nk], ps.ap[:, 0:nk], u["bias"], c.ap[:, n:n + 1]
                t = V(lambda e, o=o, i0=i0, i1=i1, ac=ac: e.tensor_tensor_reduce(
                    out=o, in0=i0, in1=i1, scale=1.0, scalar=LOW, op0=ALU.add, op1=ALU.max, accum_out=ac),
                    [tok] + u["btoks"] + b.free + free)
                ps.free = [t]
            if len(parts) == 1:
                t = ts(c.ap[:, 3:4], c.ap[:, 0:1], -scale, None, ALU.mult, waits=[t])
            else:
                t = red(c.ap[:, 3:4], c.ap[:, 0:len(parts)], ALU.max, [t], negate=True)
            for n, u in enumerate(parts):
                o = u["buf"].ap[:, 0:nk]
                t2 = act(o, o, ACT.Exp, [t], bias=c.ap[:, 3:4], scale=scale, accum_out=c.ap[:, 4 + n:5 + n])
            if len(parts) > 1:
                t2 = red(c.ap[:, 7:8], c.ap[:, 4:4 + len(parts)], ALU.add, [t2])
                t2 = recip(c.ap[:, 7:8], c.ap[:, 7:8], [t2])
            else:
                t2 = recip(c.ap[:, 7:8], c.ap[:, 4:5], [t2])
            for u in parts:
                o = u["buf"].ap[:, 0:nk]
                if job.get("gate") is not None:
                    u["p"] = ts(o, o, c.ap[:, 7:8], job["gate"], ALU.mult, ALU.mult, [t2] + job["gtoks"])
                else:
                    u["p"] = ts(o, o, c.ap[:, 7:8], None, ALU.mult, waits=[t2])
            c.free = [u["p"]]

        def attend(job, PB):
            i = job["i"]
            for u in job["parts"]:
                pt = PT.next()
                for b in range(i + 1):
                    tok = tr(pt.ap[:, b * 128:(b + 1) * 128], u["buf"].ap[:, b * 128:(b + 1) * 128],
                             [u["p"]] + pt.free, b == i)
                u["buf"].free = [tok]
                pb = PB.next()
                t = copy(pb.ap[:, 0:(i + 1) * 128], pt.ap[:, 0:(i + 1) * 128], [tok] + pb.free)
                pt.free = [t]
                o = u["out"]
                for b in range(i + 1):
                    tok = mm(o, u["v"](b), pb.ap[:, b * 128:(b + 1) * 128], u["start"] and b == 0,
                             u["stop"] and b == i, [t] + u["vtoks"] + u["ofree"], b == i)
                pb.free = [tok]
            if job.get("done"):
                job["done"](tok)

        ch_c = Chan(sem("s_c"))
        ch_v = Chan(sem("s_v"))
        ch_x = Chan(sem("s_x"))
        t_x = SP.dma(lambda e: e.dma_start(XT, D["xT"].rearrange("(k p) t -> p k t", p=128)), ch_x)
        t_cst = SP.dma(lambda e: e.dma_start(cst[:, :], D["cst"]), ch_c)
        t_vec = SP.dma(lambda e: e.dma_start(vec[:, :], D["vec"]), ch_v)
        t_ones = vset(ones[:, :], 1.0)
        xt = [t_x] * 16

        ar = Arena()
        qT = ar(16 * S).rearrange("p (k t) -> p k t", t=S)
        kT = ar(16 * S).rearrange("p (k t) -> p k t", t=S)
        vN = ar(2 * 1664).rearrange("p (i c) -> p i c", i=2)
        gts = ar(72).rearrange("p (i c) -> p i c", i=2)
        bias = ar(32 * S).rearrange("p (h t) -> p h t", t=S)
        SB = Ring([Buf(ar(S)) for _ in range(10)])
        PB = Ring([Buf(ar(S)) for _ in range(4)])
        small = Smalls(ar(64), 8)
        tpe = ar(32 * 45).rearrange("p (l k n) -> p l k n", l=32, k=3)
        peT = ar(64).rearrange("p (b l) -> p b l", b=2)
        hid = ar(45)
        hidR = ar(3 * 128).rearrange("p (k g n) -> p k g n", k=3, g=4)
        kcT = ar(45)
        vcR = ar(3 * 64).rearrange("p (k d) -> p k d", k=3)
        w2 = ar(128).rearrange("p (b d) -> p b d", b=2)
        pcs = ar(1536)
        Pc = pcs[:, 0:768].rearrange("p (i h n) -> p i h n", i=2, h=12)
        PcT = pcs[:, 768:1536].rearrange("p (k i t) -> p k i t", k=3, i=2)
        csm = ar(64)
        relT = ar(32)
        oneh = kT[:, 10:16, :].rearrange("p k t -> p (k t)").rearrange("p (v j) -> p v j", v=4)
        toe = pcs.rearrange("p (v j) -> p v j", v=4)
        oT = HT
        ch_b = Chan(sem("s_b"))
        ch_t = Chan(sem("s_t"))
        t = SP.dma(lambda e: e.dma_start(oneh[0:33], D["oneh"].rearrange("b (v j) -> b v j", v=4)), ch_b)
        t = SP.dma(lambda e: e.dma_start(relT[0:33, :], D["relT"]), ch_b)
        t = SP.dma(lambda e: e.dma_start(peT[0:64], D["peT"].rearrange("d (b l) -> d b l", b=2)), ch_b)
        t_b = SP.dma(lambda e: e.dma_start(w2[:, :, :], D["cw2"].rearrange("p (b d) -> p b d", b=2)), ch_b)
        groups = [(0, 4), (4, 8), (8, 12), (12, 32)]
        for v, (a, b) in enumerate(groups):
            ps = PP.next()
            tok = mm(ps.ap[0:b - a, 0:384], relT[0:33, a:b], oneh[0:33, v, :], True, True, [t_b] + ps.free, True)
            t = vcopy(toe[0:b - a, v, :], ps.ap[0:b - a, 0:384], [tok])
            ps.free = [t]
            td = SP.dma(lambda e, v=v, a=a, b=b: e.dma_start(D["toe"][a:b, :], toe[0:b - a, v, :]), ch_t, [t])
        tb = [None] * 32

        def make_bias(q):
            src = bass.AP(D["toe"].tensor, 8 * q * 384, [[1, 128], [384, 8], [1, 256]])
            s = ring.next()
            dst = s.ap.rearrange("p (h t) -> p h t", h=8)
            ld = SP.dma(lambda e: e.dma_start(dst, src), s.chan, s.free + [td])
            for c in range(4):
                ps = PP.next()
                tok = mm(ps.ap, cc("exch"), s.ap[:, 512 * c:512 * c + 512], True, True,
                         [ld, t_cst] + ps.free, True)
                h = 8 * q + 2 * c
                t = copy(bias[:, h:h + 2, :].rearrange("p h t -> p (h t)"), ps.ap, [tok])
                tb[h] = tb[h + 1] = t
                ps.free = [t]
            s.free = [tok]

        ht = rmsnorm(XT, "norm_attn", HT, HT, 16, xt)

        tq, tk = [None] * 16, [None] * 16

        def to_q(n, slot):
            def f(_, o, tok):
                tq[slot] = act(qT[:, slot, :], o, ACT.Copy, [tok], scale=0.125)
                return [tq[slot]]
            linT(D["w_in"], n, HT, ht, f)

        def to_k(n, slot):
            def f(_, o, tok):
                tk[slot] = vcopy(kT[:, slot, :], o, [tok])
                return [tk[slot]]
            linT(D["w_in"], n, HT, ht, f)

        tv = {}

        def to_v(s, ld, c0, cols, at):
            def f(i, o, tok):
                tv[at, i] = copy(vN[:, i, at:at + cols], o, [tok])
                return [tv[at, i]]
            linN(s, ld, HT, ht, cols, c0, 128, f)

        def v_tile(n, at):
            s, ld = load(D["w_in"][n], SLOT)
            to_v(s, ld, 0, 128, at)

        for g in range(3):
            for j in range(2):
                to_q(6 * g + j, 2 * g + j)
                to_k(6 * g + 2 + j, 2 * g + j)
            for j in range(2):
                v_tile(6 * g + 4 + j, g * 256 + j * 128)
        for q in range(4):
            make_bias(q)
        for j in range(4):
            to_q(18 + j, 6 + j)
            to_k(22 + j, 6 + j)
            v_tile(26 + j, 768 + 128 * j)
        for j in range(6):
            to_q(30 + j, 10 + j)

        tpe_free = []
        unit_t = {}

        def unit(s, ld, h, what):
            nonlocal tpe_free
            wu = s.ap.rearrange("p (k c) -> p k c", c=128)[:, :, 64 * h:64 * h + 64]
            kind, kv = what // 3, what % 3
            if kind in (3, 5):
                at = 1280 + (0 if kind == 3 else 192) + 64 * kv

                def f(i, o, tok):
                    tv[at, i] = copy(vN[:, i, at:at + 64], o, [tok])
                    return [tv[at, i]]
                linN(s, ld, HT, ht, 64, 64 * h, 128, f)
                return
            ps = PP.next()
            reps = (0, 64) if kind in (2, 4) else (0,)
            for b in reps:
                for k in range(16):
                    tok = mm(ps.ap[b:b + 64, 0:S], wu[:, k, :], HT[:, k, :], k == 0, k == 15,
                             [ld, ht[k]] + (ps.free if k == 0 else []), k == 15)
            s.free = [tok]
            if kind in (2, 4):
                slot = 10 + (0 if kind == 2 else 3) + kv
                tk[slot] = vcopy(kT[:, slot, :], ps.ap[:, 0:S], [tok])
                ps.free = [tk[slot]]
                return
            src = ps.ap[0:64, 0:S].rearrange("p (n r) -> p r n", r=16)
            for a in range(2):
                pe = peT[0:64, kind, 16 * a:16 * a + 16].unsqueeze(2).to_broadcast([64, 16, 15])
                t = tt(tpe[0:64, 16 * a:16 * a + 16, kv, :], src[:, :, a:a + 15], pe, ALU.add,
                       [tok, t_b] + tpe_free)
            ps.free = [t]
            unit_t[what] = t

        cmp_t = {}

        def compress(br):
            nonlocal tpe_free
            ps = PP.next()
            for p in range(2):
                s, ld = load(D["cw1"][br, p], SLOT, 64)
                for l in range(16):
                    tok = mm(ps.ap[:, 0:45], s.ap[0:64, l * 128:(l + 1) * 128],
                             tpe[0:64, 16 * p + l].rearrange("p k n -> p (k n)"), p + l == 0, p == 1 and l == 15,
                             [ld] + [unit_t[3 * br + kv] for kv in range(3)] + ps.free, l == 15)
                s.free = [tok]
            tpe_free = [tok]
            t = act(hid[:, :], ps.ap[:, 0:45], ACT.Gelu_apprx_tanh, [tok] + cmp_t.get("hid", []))
            ps.free = [t]
            po = PP.next()
            if br == 0:
                for b in (0, 64):
                    tok = mm(po.ap[b:b + 64, 0:45], w2[:, 0, :], hid[:, :], True, True, [t, t_b] + po.free, True)
                cmp_t["hid"] = [tok]
                cmp_t["k"] = vcopy(kcT[:, :], po.ap[:, 0:45], [tok])
                po.free = [cmp_t["k"]]
            else:
                t0 = vset(hidR[:, :, :, :], 0.0)
                h3 = hid.rearrange("p (k n) -> p k n", k=3)
                for g in range(4):
                    t1 = vcopy(hidR[:, :, g, 0:15], h3, [t, t0])
                for kv in range(3):
                    tok = mm(po.ap[:, 64 * kv:64 * kv + 64], hidR[:, kv, :, :].rearrange("p g n -> p (g n)"),
                             w2[:, 1, :], True, True, [t1] + po.free, kv == 2)
                cmp_t["v"] = vcopy(vcR[:, :, :].rearrange("p k d -> p (k d)"), po.ap[:, 0:192], [tok])
                po.free = [cmp_t["v"]]

        for n in range(9):
            s, ld = load(D["w_in"][36 + n], SLOT)
            for h in range(2):
                unit(s, ld, h, 2 * n + h)
                if 2 * n + h in (2, 5):
                    compress(n - 1)
        s, ld = load(D["w_gate"], 16 * 36)
        tg = [None, None]

        def f_gate(i, o, tok):
            tg[i] = act(gts[:, i, :], o, ACT.Sigmoid, [tok])
            return [tg[i]]
        linN(s, ld, HT, ht, 36, 0, 36, f_gate)

        t_pz = vset(Pc[:, :, :, :], 0.0, [td])
        for i in range(2):
            pc = Pc[:, i, :, 0:15]
            ng = cc("cmpneg")[:, 15 * i:15 * i + 15].unsqueeze(1).to_broadcast([128, 6, 15])
            ok = cc("cmp01")[:, 15 * i:15 * i + 15].unsqueeze(1).to_broadcast([128, 12, 15])
            for odd in range(2):
                ps = PP.next()
                sc = ps.ap[:, 0:192].rearrange("p (h n) -> p h n", h=6)[:, :, 0:15]
                for m in range(6):
                    b, h = 64 * odd, 2 * m + odd
                    tok = mm(ps.ap[:, 32 * m:32 * m + 15], qT[b:b + 64, 10 + m, i * 128:(i + 1) * 128],
                             kcT[b:b + 64, 15 * (h // 4):15 * (h // 4) + 15], True, True,
                             [tq[10 + m], cmp_t["k"]] + ps.free, m == 5)
                t = tt(pc[:, odd:12:2, :], sc, ng, ALU.add, [tok, t_cst, t_pz])
                ps.free = [t]
            mx, dn = csm[:, 24 * i:24 * i + 12], csm[:, 24 * i + 12:24 * i + 24]
            t = red(mx, pc, ALU.max, [t])
            t = tt(pc, pc, mx.unsqueeze(2).to_broadcast([128, 12, 15]), ALU.subtract, [t])
            t = act(pc, pc, ACT.Exp, [t])
            t = tt(pc, pc, ok, ALU.mult, [t])
            t = red(dn, pc, ALU.add, [t])
            t = ts(dn, dn, 1e-30, None, ALU.max, waits=[t])
            t = recip(dn, dn, [t])
            t = tt(dn, dn, gts[:, i, 0:36].rearrange("p (h b) -> p h b", b=3)[:, :, 0], ALU.mult, [t, tg[i]])
            t = tt(pc, pc, dn.unsqueeze(2).to_broadcast([128, 12, 15]), ALU.mult, [t])
            pt = PT.next()
            for kv in range(3):
                tok = tr(pt.ap[:, kv * 128:(kv + 1) * 128],
                         Pc[:, i, 4 * kv:4 * kv + 4, :].rearrange("p h n -> p (h n)"), [t, t_cst] + pt.free, kv == 2)
            t = vcopy(PcT[:, :, i, :], pt.ap[:, 0:384].rearrange("p (k t) -> p k t", k=3), [tok])
            pt.free = [t]
        t_pct = t

        ot = [None] * 16
        ht_read = P.last()

        def unit_of(q, k, base, i, bi, v, vtoks, o, start=True, stop=True, ofree=()):
            nk = (i + 1) * 128
            return {"qk": [(qT[base:base + 64, q, i * 128:(i + 1) * 128], kT[base:base + 64, k, 0:nk])],
                    "toks": [tq[q], tk[k]], "bias": bias[:, bi, 128 - 128 * i:S], "btoks": [tb[bi]],
                    "v": v, "vtoks": vtoks, "out": o, "start": start, "stop": stop, "ofree": list(ofree)}

        def vcols(at):
            return lambda b: vN[:, b, at:at + 64]

        jobs = []
        for jp in range(2):
            ps = [PO.next() for _ in range(3)]
            for j in (2 * jp, 2 * jp + 1):
                base = 64 * (j % 2)
                for i in range(2):
                    jobs.append({"i": i, "ps": ps, "tiles": [2 * g + jp for g in range(3)], "parts": [
                        (2 * g + jp, 2 * g + jp, base, i, 4 * g + j, g * 256 + 64 * j, g) for g in range(3)]})
            jobs[-1]["last"] = True
        for hp in range(4):
            ps = [PO.next()]
            for h in (2 * hp, 2 * hp + 1):
                for i in range(2):
                    jobs.append({"i": i, "ps": ps, "tiles": [6 + hp],
                                 "parts": [(6 + hp, 6 + hp, 64 * (h % 2), i, 12 + h, 768 + 64 * h, 0)]})
            jobs[-1]["last"] = True
        for hp in range(6):
            ps = [PO.next()]
            for h in (2 * hp, 2 * hp + 1):
                kv = h // 4
                for i in range(2):
                    for br in range(2):
                        jobs.append({"i": i, "ps": ps, "tiles": [10 + hp], "c": (h, br),
                                     "gate": gts[:, i, 3 * h + 1 + br:3 * h + 2 + br], "gtoks": [tg[i]],
                                     "parts": [(10 + hp, 10 + 3 * br + kv, 64 * (h % 2), i, 20 + h,
                                                1280 + 192 * br + 64 * kv, 0)]})
            jobs[-1]["last"] = True

        def vtok(at):
            if at < 1280:
                at = at // 128 * 128
            return [tv[at, 0], tv[at, 1]]

        def front(job):
            job["parts"] = [unit_of(q, k, base, i, bi, vcols(at), vtok(at),
                                    job["ps"][n].ap[base:base + 64, i * 128:(i + 1) * 128])
                            for q, k, base, i, bi, at, n in job["parts"]]
            softmax(job, SB, small)

        def back(job):
            i = job["i"]
            for n, u in enumerate(job["parts"]):
                u["ofree"] = job["ps"][n].free
            if "c" in job:
                h, br = job["c"]
                u = job["parts"][0]
                if br == 0:
                    g = h % 4
                    mm(u["out"], vcR[32 * g:32 * g + 32, h // 4, :], PcT[32 * g:32 * g + 32, h // 4, i, :],
                       True, False, [t_pct, cmp_t["v"]] + u["ofree"])
                    u["start"], u["stop"] = False, False
                else:
                    u["start"] = False

            def done(tok):
                for n, tile in enumerate(job["tiles"]):
                    ot[tile] = copy(oT[:, tile, :], job["ps"][n].ap[:, 0:S], [tok, ht_read])
                    job["ps"][n].free = [ot[tile]]
            if job.get("last"):
                job["done"] = done
            attend(job, PB)

        for n in range(len(jobs) + 2):
            if n < len(jobs):
                front(jobs[n])
            if n >= 2:
                back(jobs[n - 2])
            if n == 7:
                pass

        for n in range(16):
            linT(D["w_out"], n, oT, ot, residual)

        fence()
        ar = Arena()
        ff = ar(44 * S).rearrange("p (k t) -> p k t", t=S)
        CA = Ring([Buf(ar(S)) for _ in range(6)])
        h2 = rmsnorm(XT, "norm_mlp", HT, HT, 16, xt)
        ft = [None] * 44

        def conv3(n, o, tok):
            b = CA.next()
            t = act(b.ap, o, ACT.Identity, [tok, t_vec] + b.free, bias=vcol("conv_b", n), scale=vcol("conv_w", n))
            for j in (1, 2):
                t = stt(b.ap[:, j:S], o[:, 0:S - j], vcol("conv_w", 88 * j + n), b.ap[:, j:S], ALU.mult, ALU.add, [t])
            return b, t

        for n in range(44):
            got = []

            def f_up(m, o, tok):
                got.append(conv3(m, o, tok))
                return [got[-1][1]]
            linT(D["w_up"], n, HT, h2, f_up)
            linT(D["w_up"], 44 + n, HT, h2, f_up)
            (ba, ta), (bg, tgg) = got
            t = act(bg.ap, bg.ap, ACT.Silu, [tgg])
            ft[n] = tt(ff[:, n, :], ba.ap, bg.ap, ALU.mult, [t, ta])
            ba.free = bg.free = [ft[n]]
        for n in range(16):
            linT(D["w_down"], n, ff, ft, residual, pieces=4)
        xt = rmsnorm(XT, "norm_final", HT, XT, 16, xt)

        fence()
        ar = Arena()
        qn = ar(16 * S).rearrange("p (k t) -> p k t", t=S)
        qp = ar(8 * S).rearrange("p (k t) -> p k t", t=S)
        kn = ar(16 * S).rearrange("p (k t) -> p k t", t=S)
        kp = ar(S)
        mv = ar(2 * 2048).rearrange("p (i c) -> p i c", i=2)
        lat = ar(10 * S).rearrange("p (k t) -> p k t", t=S)
        Y = ar(16 * S).rearrange("p (k t) -> p k t", t=S)
        SB = Ring([Buf(ar(S)) for _ in range(4)])
        PB = Ring([Buf(ar(S)) for _ in range(4)])
        small = Smalls(ar(64), 8)
        RW = Ring([Buf(ar(S), Chan(sem(f"s_r{i}"))) for i in range(2)])
        RS = Ring([Buf([ar(S) for _ in range(4)]) for i in range(2)])
        RO = Ring([Buf(ar(S)) for _ in range(2)])
        GB = Ring([Buf(ar(S)) for _ in range(2)])
        sp = [ar(16) for _ in range(4)]
        n4 = rmsnorm(XT, "attn_norm_2", HT, HT, 16, xt)
        lt = [None] * 10

        def f_lat(base):
            def f(n, o, tok):
                lt[base + n] = copy(lat[:, base + n, :], o, [tok])
                return [lt[base + n]]
            return f
        for n in range(6):
            linT(D["w_cq"], n, HT, n4, f_lat(0))
        for n in range(4):
            linT(D["w_ckv"], n, HT, n4, f_lat(6))

        def rope(o, dst, parts, tok):
            sw = RO.next()
            for b in range(0, parts, 64):
                for x, y in ((b, b + 32), (b + 32, b)):
                    t = act(sw.ap[x:x + 32, :], o[y:y + 32, :], ACT.Copy, [tok] + sw.free)
            t2 = tt(dst, o, cc("cos")[0:parts, :], ALU.mult, [t, t_cst])
            t = tt(sw.ap[0:parts, :], sw.ap[0:parts, :], cc("sin")[0:parts, :], ALU.mult, [t])
            t = tt(dst, dst, sw.ap[0:parts, :], ALU.add, [t, t2])
            sw.free = [t]
            return t

        kpt = []

        def f_kr(_, o, tok):
            t = rope(o, kp[0:64, :], 64, tok)
            kpt.append(vcopy(kp[64:128, :], kp[0:64, :], [t]))
            return [t]
        linT(D["w_kr"], 0, HT, n4, f_kr, m=64)
        lq = rmsnorm(lat[:, 0:6, :], "q_norm_2", qn[:, 0:6, :], lat[:, 0:6, :], 6, lt[0:6])
        lk = rmsnorm(lat[:, 6:10, :], "kv_norm_2", kn[:, 0:4, :], lat[:, 6:10, :], 4, lt[6:10])

        lam = vcol("lru_lambda_2", 0, 16)
        t = act(sp[0], lam, ACT.Abs, [t_vec])
        t = act(sp[0], sp[0], ACT.Exp, [t], scale=-1.0)
        t1 = ts(sp[1], sp[0], 2.0, None, ALU.add, waits=[t])
        t1 = recip(sp[1], sp[1], [t1])
        t1 = tt(sp[1], sp[1], sp[0], ALU.mult, [t1])
        t2 = tt(sp[2], sp[1], sp[1], ALU.mult, [t1])
        t2 = ts(sp[3], sp[2], 1.0 / 19, 1.0 / 17, ALU.mult, ALU.add, [t2])
        for d in (15, 13, 11, 9, 7, 5, 3, 1):
            t2 = tt(sp[3], sp[3], sp[2], ALU.mult, [t2])
            t2 = ts(sp[3], sp[3], 1.0 / d, None, ALU.add, waits=[t2])
        t2 = tt(sp[3], sp[3], sp[1], ALU.mult, [t2])
        t2 = ts(sp[3], sp[3], 16.0, None, ALU.mult, waits=[t2])
        t2 = ts(sp[0], lam, -1.0, 0.0, ALU.mult, ALU.max, [t2])
        t2 = stt(sp[3], sp[0], 8.0, sp[3], ALU.mult, ALU.add, [t2])
        t_sp = ts(sp[2], sp[3], -1.0, None, ALU.mult, waits=[t2])

        yt = [None] * 16

        def recurrent(j):
            st = RS.next()
            xc, r, w, z = st.ap
            rw = RW.next()
            t_rw = SP.dma(lambda e: e.dma_start(rw.ap, D["w_rg"][j]), rw.chan, rw.free)
            got = []

            def f_x(n, o, tok):
                t = act(xc, o, ACT.Identity, [tok, t_vec] + st.free, bias=vcol("conv_b_2", n),
                        scale=vcol("conv_w_2", 48 + n))
                for k in (1, 2, 3):
                    t = stt(xc[:, k:S], o[:, 0:S - k], vcol("conv_w_2", 16 * (3 - k) + n), xc[:, k:S],
                            ALU.mult, ALU.add, [t])
                got.append(t)
                return [t]

            def f_y(n, o, tok):
                got.append(act(Y[:, n, :], o, ACT.Gelu_apprx_tanh, [tok]))
                return [got[-1]]
            linT(D["w_xr"], j, HT, n4, f_x)
            linT(D["w_yr"], j, HT, n4, f_y)
            t_xc, t_y = got
            ps = PP.next()
            mm(ps.ap[:, 0:S], rw.ap[:, 0:128], xc, True, True, [t_rw, t_xc] + ps.free)
            tok = mm(ps.ap[:, S:2 * S], rw.ap[:, 128:256], xc, True, True, [], True)
            rw.free = [tok]
            t_i = act(w, ps.ap[:, S:2 * S], ACT.Sigmoid, [tok] + st.free, bias=vcol("b_rg_x_2", j))
            t_r = act(r, ps.ap[:, 0:S], ACT.Sigmoid, [], bias=vcol("b_rg_a_2", j))
            ps.free = [t_r]
            t_g = tt(xc, xc, w, ALU.mult, [t_i, tok])
            t_t = act(w, r, ACT.Tanh, [t_r, t_g, t_sp], scale=sp[3][:, j:j + 1])
            t_a = act(r, r, ACT.Exp, [t_t], scale=sp[2][:, j:j + 1])
            t = ts(z, w, 1.0, None, ALU.add, waits=[t_t])
            t = recip(z, z, [t])
            t = stt(w, w, 2.0, z, ALU.mult, ALU.mult, [t])
            t = act(w, w, ACT.Sqrt, [t])
            t = vset(w[:, 0:1], 1.0, [t])
            t = tt(w, w, xc, ALU.mult, [t])
            t = V(lambda e: e.tensor_tensor_scan(z, r, w, 0.0, ALU.mult, ALU.add), [t, t_a])
            yt[j] = tt(Y[:, j, :], Y[:, j, :], z, ALU.mult, [t, t_y])
            st.free = [yt[j]]

        for j in range(8):
            recurrent(j)
        tqn, tqp, tkn, tmv = [None] * 16, [None] * 8, [None] * 16, {}

        def f_qn(n, o, tok):
            tqn[n] = copy(qn[:, n, :], o, [tok, lq[0]])
            return [tqn[n]]

        def f_kn(n, o, tok):
            tkn[n] = copy(kn[:, n, :], o, [tok, lk[0]])
            return [tkn[n]]

        def f_qp(n, o, tok):
            tqp[n] = rope(o, qp[:, n, :], 128, tok)
            return [tqp[n]]
        for n in range(16):
            linT(D["w_qn"], n, lat[:, 0:6, :], lq, f_qn)
        for n in range(8):
            linT(D["w_qp"], n, lat[:, 0:6, :], lq, f_qp)
        for n in range(16):
            linT(D["w_kn"], n, lat[:, 6:10, :], lk, f_kn)
        for c in range(4):
            s, ld = load(D["w_v"][c], SLOT)

            def f_v(i, o, tok, c=c):
                tmv[c, i] = copy(mv[:, i, 512 * c:512 * c + 512], o, [tok])
                return [tmv[c, i]]
            linN(s, ld, lat[:, 6:10, :], lk, 512, 0, 512, f_v)

        jobs = []
        to = [None] * 16
        for h in range(16):
            ps = PO.next()
            for i in range(2):
                jobs.append((h, i, ps))

        def mla_front(h, i, ps):
            b, nk = 64 * (h % 2), (i + 1) * 128
            u = {"qk": [(qn[:, h, i * 128:(i + 1) * 128], kn[:, h, 0:nk]),
                        (qp[b:b + 64, h // 2, i * 128:(i + 1) * 128], kp[b:b + 64, 0:nk])],
                 "toks": [tqn[h], tkn[h], tqp[h // 2], kpt[0]], "bias": cc("mask")[:, 128 - 128 * i:S],
                 "btoks": [t_cst], "v": lambda b, h=h: mv[:, b, 128 * h:128 * h + 128],
                 "vtoks": [tmv[h // 4, 0], tmv[h // 4, 1]], "out": ps.ap[:, i * 128:(i + 1) * 128],
                 "start": True, "stop": True, "ofree": []}
            job = {"i": i, "parts": [u], "scale": 192.0 ** -0.5}
            softmax(job, SB, small)
            return job

        def mla_back(job, h, i, ps):
            job["parts"][0]["ofree"] = ps.free

            def done(tok):
                to[h] = copy(qn[:, h, :], ps.ap[:, 0:S], [tok])
                ps.free = [to[h]]
            if i == 1:
                job["done"] = done
            attend(job, PB)

        live = []
        for n in range(len(jobs) + 2):
            if n < len(jobs):
                live.append(mla_front(*jobs[n]))
            if n >= 2:
                mla_back(live[n - 2], *jobs[n - 2])
            if n % 4 == 3 and n < len(jobs):
                recurrent(8 + n // 4)

        mT = kn
        tm = [None] * 16
        kn_read = P.last()
        for n in range(16):
            g = GB.next()

            def f_g(m, o, tok):
                g.free = [act(g.ap, o, ACT.Sigmoid, [tok, t_vec] + g.free, bias=vcol("b_gate_2", m))]
                return g.free

            def f_o(m, o, tok):
                tm[m] = tt(mT[:, m, :], o, g.ap, ALU.mult, [tok, kn_read] + g.free)
                g.free = [tm[m]]
                return [tm[m]]
            linT(D["w_ga"], n, HT, n4, f_g)
            linT(D["w_attn_o"], n, qn, to, f_o)
        for n in range(16):
            g = GB.next()

            def f_g2(m, o, tok):
                g.free = [act(g.ap, o, ACT.Sigmoid, [tok, t_vec] + g.free, bias=vcol("b_gate_2", 16 + m))]
                return g.free

            def f_o2(m, o, tok):
                t = tt(g.ap, o, g.ap, ALU.mult, [tok] + g.free)
                tm[m] = tt(mT[:, m, :], mT[:, m, :], g.ap, ALU.add, [t, tm[m]])
                g.free = [tm[m]]
                return [t]
            linT(D["w_gr"], n, HT, n4, f_g2)
            linT(D["w_rnn_o"], n, Y, yt, f_o2)
        for n in range(16):
            linT(D["w_out_2"], n, mT, tm, residual)

        fence()
        ar = Arena()
        pq = ar(16 * S).rearrange("p (k t) -> p k t", t=S)
        xn = ar(2 * 2048).rearrange("p (i c) -> p i c", i=2)
        acc = ar(2 * 2048).rearrange("p (i c) -> p i c", i=2)
        scr = ar(2048)
        s2 = Ring([Buf(ar(256)) for _ in range(2)])
        tv_ = ar(256).rearrange("p (c k) -> p c k", c=16)
        ti_ = ar(256).bitcast(u32).rearrange("p (c k) -> p c k", c=16)
        tf_ = ar(256).rearrange("p (c k) -> p c k", c=16)
        cand = ar(2048).rearrange("p (h a b) -> p h a b", h=8, a=16)
        bv = ar(128).rearrange("p (h k) -> p h k", h=8)
        bc = ar(128).bitcast(u32).rearrange("p (h k) -> p h k", h=8)
        bd = ar(128).bitcast(u32).rearrange("p (h k) -> p h k", h=8)
        pf = [ar(128).rearrange("p (h k) -> p h k", h=8) for _ in range(2)]
        pe_ = [ar(128).rearrange("p (h k) -> p h k", h=8) for _ in range(2)]
        eidx = ar(256).bitcast(i32).rearrange("p (i k) -> p i k", i=2)
        gat = ar(256).rearrange("p (i h k) -> p i h k", i=2, h=8)
        hsm = ar(16)
        actv = ar(256).rearrange("p (i k) -> p i k", i=2)
        pleb = ar(2 * S)
        ppT = ar(2 * S).rearrange("p (k t) -> p k t", t=S)
        n5 = rmsnorm(XT, "ffn_norm_2", HT, HT, 16, xt)
        tpq = [None] * 16

        def f_pq(n, o, tok):
            tpq[n] = copy(pq[:, n, :], o, [tok])
            return [tpq[n]]
        for n in range(16):
            linT(D["w_peer_q"], n, HT, n5, f_pq)
        txn = [None, None]
        for i in range(2):
            for c in range(4):
                pt = PT.next()
                for k in range(4):
                    tok = tr(pt.ap[:, k * 128:(k + 1) * 128], HT[:, 4 * c + k, i * 128:(i + 1) * 128],
                             [n5[4 * c + k]] + pt.free, k == 3)
                txn[i] = vcopy(xn[:, i, 512 * c:512 * c + 512], pt.ap, [tok])
                pt.free = [txn[i]]
        sk, ld_sk = load(D["subkeys"], SLOT)

        def top16(vals, idx, src, n, tok):
            b = s2.next()
            w = b.ap[:, 0:n]
            t = V(lambda e: e.max(vals[:, 0:8], src), [tok])
            V(lambda e: e.max_index(idx[:, 0:8], vals[:, 0:8], src), [t])
            t = V(lambda e: e.match_replace(w, vals[:, 0:8], src, LOW), [t] + b.free)
            t = V(lambda e: e.max(vals[:, 8:16], w), [t])
            t = V(lambda e: e.max_index(idx[:, 8:16], vals[:, 8:16], w), [t])
            b.free = [t]
            return t

        tga, tei = [None, None], [None, None]

        def select(i):
            for c in range(4):
                ps = PP.next()
                for k in range(4):
                    n = 4 * c + k
                    tok = mm(ps.ap[:, k * 128:(k + 1) * 128], pq[:, n, i * 128:(i + 1) * 128],
                             sk.ap[:, n * 128:(n + 1) * 128], True, True, [tpq[n], ld_sk] + ps.free, k == 3)
                t = act(scr[:, 512 * c:512 * c + 512], ps.ap, ACT.Copy, [tok, V.last()])
                ps.free = [t]
                for k in range(4):
                    n = 4 * c + k
                    t_top = top16(tv_[:, n, :], ti_[:, n, :], scr[:, n * 128:(n + 1) * 128], 128, t)
            t = vcopy(tf_, ti_, [t_top])
            v4 = tv_.rearrange("p (h c) k -> p h c k", c=2)
            f4 = tf_.rearrange("p (h c) k -> p h c k", c=2)
            for h in range(8):
                t2 = tt(cand[:, h], v4[:, h, 0, :].unsqueeze(2).to_broadcast([128, 16, 16]),
                        v4[:, h, 1, :].unsqueeze(1).to_broadcast([128, 16, 16]), ALU.add, [t])
                t2 = top16(bv[:, h, :], bc[:, h, :], cand[:, h].rearrange("p a b -> p (a b)"), 256, t2)
            for c, (op, k) in enumerate(((ALU.logical_shift_right, 4), (ALU.bitwise_and, 15))):
                t = ts(bd, bc, k, None, op, waits=[t2])
                t = vcopy(pf[c], bd, [t])
                for h in range(8):
                    oh = cand[:, h]
                    a = tt(oh, pf[c][:, h, :].unsqueeze(2).to_broadcast([128, 16, 16]),
                           cc("iota").unsqueeze(1).to_broadcast([128, 16, 16]), ALU.is_equal, [t, t_cst])
                    a = tt(oh, oh, f4[:, h, c, :].unsqueeze(1).to_broadcast([128, 16, 16]), ALU.mult, [a])
                    t2 = red(pe_[c][:, h, :], oh, ALU.add, [a])
            t = stt(pe_[0], pe_[0], 128.0, pe_[1], ALU.mult, ALU.add, [t2])
            tei[i] = vcopy(eidx[:, i, :].rearrange("p (h k) -> p h k", h=8), pe_[0], [t])
            g = gat[:, i]
            t = tt(g, bv, bv[:, :, 0:1].to_broadcast([128, 8, 16]), ALU.subtract, [t2])
            t = act(g, g, ACT.Exp, [t])
            t = red(hsm[:, 0:8], g, ALU.add, [t])
            t = recip(hsm[:, 0:8], hsm[:, 0:8], [t])
            tga[i] = tt(g, g, hsm[:, 0:8].unsqueeze(2).to_broadcast([128, 8, 16]), ALU.mult, [t])

        def gather(table, i, k):
            s = rows.next()
            ix = eidx[:, i, k:k + 1]
            tok = G.dma(lambda e: e.indirect_dma_start(
                out=s.ap, out_offset=None, in_=D[table],
                in_offset=bass.IndirectOffsetOnAxis(ap=ix, axis=0)), s.chan, [tei[i]] + s.free)
            s.free = []
            return s, tok

        def experts_in(i):
            for k in range(128):
                s, ld = gather("peer_u", i, k)
                a, x, ac = s.ap, xn[:, i, :], actv[:, i, k:k + 1]
                t = V(lambda e, a=a, x=x, ac=ac: e.tensor_tensor_reduce(
                    out=a, in0=a, in1=x, scale=1.0, scalar=0.0, op0=ALU.mult, op1=ALU.add, accum_out=ac),
                    [ld, txn[i]])
                s.free = [t]
            t = act(actv[:, i, :], actv[:, i, :], ACT.Gelu_apprx_tanh, [t])
            return tt(actv[:, i, :], actv[:, i, :], gat[:, i].rearrange("p h k -> p (h k)"), ALU.mult, [t, tga[i]])

        def experts_out(i, t):
            o = acc[:, i, :]
            for k in range(128):
                s, ld = gather("peer_v", i, k)
                c = actv[:, i, k:k + 1]
                if k == 0:
                    t = ts(o, s.ap, c, None, ALU.mult, waits=[t, ld])
                else:
                    t = stt(o, s.ap, c, o, ALU.mult, ALU.add, [t, ld])
                s.free = [t]
            return t

        select(0)
        select(1)
        sk.free = [P.last()]
        for r, b in zip(rows.bufs, ring.bufs):
            r.free = list(b.free)
        t_co = experts_in(0)
        t_acc = [experts_out(0, t_co)]
        t_co = experts_in(1)
        t_acc.append(experts_out(1, t_co))
        for r, b in zip(rows.bufs, ring.bufs):
            b.free = list(r.free)
        xt = [None] * 16
        for c in range(16):
            pt = PT.next()
            for i in range(2):
                tok = tr(pt.ap[:, i * 128:(i + 1) * 128], acc[:, i, c * 128:(c + 1) * 128],
                         [t_acc[i]] + pt.free, i == 1)
            xt[c] = tt(XT[:, c, :], pt.ap[:, 0:S], XT[:, c, :], ALU.add, [tok])
            pt.free = [xt[c]]

        ch_p = Chan(sem("s_p"))
        t_pp = SP.dma(lambda e: e.dma_start(ppT, D["pT"].rearrange("(k p) t -> p k t", p=128)), ch_p, [V.last()])
        n6 = rmsnorm(XT, "ple_norm_2", HT, HT, 16, xt)
        GB2 = Ring([Buf(pleb[:, i * S:(i + 1) * S]) for i in range(2)])
        for n in range(16):
            g = GB2.next()

            def f_pg(m, o, tok):
                g.free = [act(g.ap, o, ACT.Sigmoid, [tok] + g.free)]
                return g.free

            def f_pp(m, o, tok):
                t = tt(g.ap, o, g.ap, ALU.mult, [tok] + g.free)
                xt[m] = tt(XT[:, m, :], XT[:, m, :], g.ap, ALU.add, [t])
                g.free = [xt[m]]
                return [t]
            linT(D["w_ple_gate"], n, HT, n6, f_pg)
            linT(D["w_ple_proj"], n, ppT, [t_pp] * 2, f_pp)
        fin = rmsnorm(XT, "final_norm_2", HT, HT, 16, xt)
        ch_o = Chan(sem("s_out"))
        for c in range(4):
            t = SP.dma(lambda e, c=c: e.dma_start(
                out[512 * c:512 * c + 512, :].rearrange("(k p) t -> p k t", p=128), HT[:, 4 * c:4 * c + 4, :]),
                ch_o, [fin[4 * c + 3]])
        SP.wait([t])

        block = ctx.enter_context(nc.Block())

        @block.sync
        def _(eng):
            SP.play(eng)

        @block.tensor
        def _(eng):
            P.play(eng)

        @block.scalar
        def _(eng):
            A.play(eng)

        @block.vector
        def _(eng):
            V.play(eng)

        @block.gpsimd
        def _(eng):
            G.play(eng)


def constants():
    import numpy as np
    import math
    f = np.float32
    p = np.arange(128)
    ident = np.eye(128, dtype=f)
    mask = np.where(np.arange(256)[None, :] <= 128 + p[:, None], 0.0, NEG).astype(f)
    half = 32
    inv = (1.0 / (np.float32(10000.0) ** (np.arange(half, dtype=f) / f(half)))).astype(f)
    ang = np.arange(256, dtype=f)[:, None] * inv[None, :]
    cos, sin = np.cos(ang).astype(f).T, np.sin(ang).astype(f).T
    cos4 = np.concatenate([cos] * 4, 0)
    sin4 = np.concatenate([-sin, sin, -sin, sin], 0)
    end = np.arange(15) * 16 + 31
    ok = np.stack([(end[None, :] <= (128 * i + p)[:, None]) for i in range(2)], 1).reshape(128, 30)
    iota = np.broadcast_to(np.arange(16, dtype=f), (128, 16))
    cst = np.concatenate([ident, ident[:, ::-1], mask, cos4, sin4, ok.astype(f), np.where(ok, 0.0, NEG).astype(f), iota], 1)
    dist = 255 - np.arange(384)
    n = np.maximum(dist, 0)
    nf = np.maximum(n, 1).astype(f)
    large = 16 + (np.log(nf / f(16)) / f(math.log(2048 / 16)) * f(16)).astype(np.int32)
    bucket = np.where(n < 16, n, np.minimum(large, 31))
    oneh = np.zeros((33, 4, 384), f)
    for v, (d, far) in enumerate(((1, 128), (4, 512), (16, 2048), (1, 10 ** 6))):
        good = (dist >= 0) & (dist % d == 0) & (dist <= far)
        oneh[bucket, v, np.arange(384)] = good
        oneh[32, v] = np.where(good, 0.0, NEG)
    return np.ascontiguousarray(cst.astype(f)), np.ascontiguousarray(oneh.reshape(33, 4 * 384))


def layout(inp):
    import numpy as np
    g = {k: np.asarray(v) for k, v in inp.items()}

    def tiles(w, c=128):
        k, n = w.shape
        return np.ascontiguousarray(w.reshape(k // 128, 128, n // c, c).transpose(2, 1, 0, 3)).reshape(
            n // c, 128, (k // 128) * c)

    def cols(v):
        v = v.reshape(-1, v.shape[-1])
        return v.reshape(v.shape[0], -1, 128).transpose(2, 0, 1).reshape(128, -1)

    d = {}
    x = g["x"][0]
    d["xT"] = np.ascontiguousarray(x.T)
    d["pT"] = np.ascontiguousarray(g["p_2"][0, 0].T)
    d["vec"] = np.ascontiguousarray(np.concatenate([cols(g[n]) for n, _ in VEC], 1))
    d["cst"], d["oneh"] = constants()
    d["relT"] = np.ascontiguousarray(np.concatenate(
        [g["rel_table"].T, np.ones((1, 32), np.float32)], 0))
    d["peT"] = np.ascontiguousarray(g["cmp_pe"][0].transpose(2, 0, 1)).reshape(64, 64)
    d["cw2"] = np.ascontiguousarray(g["cmp_w2"][0].transpose(1, 0, 2)).reshape(128, 128)
    d["cw1"] = np.ascontiguousarray(
        g["cmp_w1"][0].reshape(2, 2, 16, 64, 128).transpose(0, 1, 3, 2, 4)).reshape(2, 2, 64, 2048)
    w = g["w_in"][0]
    d["w_in"] = tiles(w[:, :5760])
    d["w_gate"] = tiles(w[:, 5760:], 36)[0]
    d["w_out"] = tiles(g["w_out"][0])
    d["w_up"] = tiles(g["w_up"][0])
    d["w_down"] = tiles(g["w_down"][0])
    w = g["w_in_2"][0]
    at = 0
    for name, n, c in (("w_cq", 768, 128), ("w_ckv", 512, 128), ("w_kr", 64, 64), ("w_xr", 2048, 128),
                       ("w_yr", 2048, 128), ("w_ga", 2048, 128), ("w_gr", 2048, 128)):
        d[name] = tiles(w[:, at:at + n], c)
        at += n
    w = g["w_uq_2"][0].reshape(768, 16, 192)
    d["w_qn"] = tiles(np.ascontiguousarray(w[:, :, :128]).reshape(768, 2048))
    d["w_qp"] = tiles(np.ascontiguousarray(w[:, :, 128:]).reshape(768, 1024))
    w = g["w_ukv_2"][0].reshape(512, 16, 256)
    d["w_kn"] = tiles(np.ascontiguousarray(w[:, :, :128]).reshape(512, 2048))
    d["w_v"] = tiles(np.ascontiguousarray(w[:, :, 128:]).reshape(512, 2048), 512)
    d["w_rg"] = np.ascontiguousarray(np.concatenate([g["w_rg_a_2"][0], g["w_rg_x_2"][0]], 2))
    for name in ("w_attn_o", "w_rnn_o", "w_out", "w_peer_q", "w_ple_gate", "w_ple_proj"):
        d[name + ("_2" if name == "w_out" else "")] = tiles(g[name + "_2"][0])
    d["subkeys"] = np.ascontiguousarray(
        g["peer_subkeys_2"][0].reshape(16, 128, 128).transpose(2, 0, 1)).reshape(128, 2048)
    d["peer_u"] = g["peer_u_2"][0]
    d["peer_v"] = g["peer_v_2"][0]
    return d


def kernel(**inputs):
    import numpy as np
    import concourse.bacc as bacc
    from concourse.bass_utils import run_bass_kernel_spmd as run

    nc = bacc.Bacc("TRN2", target_bir_lowering=False, num_devices=1)
    arrays = {f"in_{k}": np.ascontiguousarray(v) for k, v in layout(inputs).items()}
    D = {k[3:]: nc.dram_tensor(k, v.shape, mybir.dt.from_np(v.dtype), kind="ExternalInput").ap()
         for k, v in arrays.items()}
    D["toe"] = nc.dram_tensor("toe_scratch", (32, 384), mybir.dt.float32).ap()
    out = nc.dram_tensor("out_0", (2048, S), mybir.dt.float32, kind="ExternalOutput").ap()
    program(nc, D, out)
    r = run(nc, [arrays], core_ids=[0])
    return np.ascontiguousarray(r.results[0]["out_0"].T)[None]
```

```python
import concourse.bass as bass
from concourse import mybir
from contextlib import ExitStack

S = 256
NRAW = 5
NSPL = 4
COLS = 1024
NEG = -1e30
LOW = -3.0e38

VEC = [("norm_attn", 16), ("norm_mlp", 16), ("norm_final", 16), ("attn_norm_2", 16), ("q_norm_2", 6),
       ("kv_norm_2", 4), ("ffn_norm_2", 16), ("ple_norm_2", 16), ("final_norm_2", 16), ("conv_w", 264),
       ("conv_b", 88), ("conv_w_2", 64), ("conv_b_2", 16), ("b_rg_a_2", 16), ("b_rg_x_2", 16),
       ("lru_lambda_2", 16), ("b_gate_2", 32)]
CST = [("ident", 128), ("exch", 128), ("mask", 256), ("cos", 256), ("sin", 256), ("cmp01", 30), ("cmpneg", 30), ("iota", 16)]


def offsets(table):
    at, out = 0, {}
    for name, n in table:
        out[name] = (at, at + n)
        at += n
    return out, at


VOFF, NVEC = offsets(VEC)
COFF, NCST = offsets(CST)


class Engine:

    def __init__(self, sem):
        self.sem, self.q, self.n, self.seen = sem, [], 0, {}

    def __call__(self, fn, waits=(), sig=True):
        self.q.append((self.fresh(waits), fn, (self.sem, 1) if sig else None))
        self.n += 1 if sig else 0
        return (self.sem, self.n) if sig else None

    def dma(self, fn, chan, waits=()):
        chan.n += 16
        self.q.append((self.fresh(waits), fn, (chan.sem, 16)))
        return (chan.sem, chan.n)

    def wait(self, waits):
        self.q.append((self.fresh(waits), None, None))

    def fresh(self, waits):
        out = []
        for t in waits:
            if t is not None and self.seen.get(id(t[0]), 0) < t[1]:
                self.seen[id(t[0])] = t[1]
                out.append(t)
        return out

    def last(self):
        return (self.sem, self.n) if self.n else None

    def play(self, eng):
        for waits, fn, inc in self.q:
            for sem, val in waits:
                eng.wait_ge(sem, val)
            if fn is not None:
                ins = fn(eng)
                if inc is not None:
                    ins.then_inc(*inc)


class Chan:

    def __init__(self, sem):
        self.sem, self.n = sem, 0


class Buf:

    def __init__(self, ap, chan=None):
        self.ap, self.chan, self.free, self.busy = ap, chan, [], False


class Ring:
    def __init__(self, bufs):
        self.bufs, self.i = bufs, 0

    def next(self):
        b = self.bufs[self.i % len(self.bufs)]
        self.i += 1
        return b


def program(nc, D, out):
    fp32, f32r = mybir.dt.float32, mybir.dt.float32r
    u32, i32 = mybir.dt.uint32, mybir.dt.int32
    ALU, ACT, AX = mybir.AluOpType, mybir.ActivationFunctionType, mybir.AxisListType.X
    base = ExitStack()

    def keep(name, cols, dt=fp32):
        return base.enter_context(nc.sbuf_tensor(name, [128, cols], dt))

    def tiled(t):
        return t[:, :].rearrange("p (k t) -> p k t", t=S)

    XT = tiled(keep("XT", 16 * S))
    HH, HL = tiled(keep("HH", 16 * S, f32r)), tiled(keep("HL", 16 * S, f32r))
    raw_sb = keep("raw", NRAW * COLS)
    sph, spl = keep("sph", NSPL * COLS, f32r), keep("spl", NSPL * COLS, f32r)
    vec, cst, ones, nrm = keep("vec", NVEC), keep("cst", NCST), keep("ones", 128), keep("nrm", 3 * S)
    banks = [base.enter_context(nc.psum_tensor(f"ps{i}", [128, 512], fp32)) for i in range(8)]
    sems = {}

    def sem(name):
        if name not in sems:
            sems[name] = base.enter_context(nc.semaphore(name))
        return sems[name]

    def walk(plan, run):
        P, A, V, G, SP = (Engine(sem(f"s_{n}")) for n in ("pe", "act", "dve", "pool", "sp"))
        raw = Ring([Buf(raw_sb[:, i * COLS:(i + 1) * COLS], Chan(sem(f"s_w{i}"))) for i in range(NRAW)])
        spr = Ring([Buf((sph[:, i * COLS:(i + 1) * COLS], spl[:, i * COLS:(i + 1) * COLS]))
                    for i in range(NSPL)])
        bank = [Buf(b[:, :]) for b in banks]
        PP, PS, PT, PO = Ring(bank[0:2]), Ring(bank[2:4]), Ring(bank[4:6]), Ring(bank[6:8])
        names = [0]

        def share(pp, sc, pt):
            for ring, a, b in ((PP, 0, pp), (PS, pp, pp + sc), (PT, pp + sc, pp + sc + pt), (PO, pp + sc + pt, 8)):
                ring.bufs, ring.i = bank[a:b], 0

        def vcol(name, i=0, n=1):
            a = VOFF[name][0] + i
            return vec[:, a:a + n]

        def cc(name):
            a, b = COFF[name]
            return cst[:, a:b]

        def allocator(stack):
            def alloc(cols, dt=fp32):
                names[0] += 1
                t = stack.enter_context(nc.sbuf_tensor(f"t{run}_{names[0]}", [128, cols], dt))
                return t[:, :]
            return alloc

        def tiles(ap):
            return ap.rearrange("p (k t) -> p k t", t=S)

        def fence():
            ends = [e.last() for e in (P, A, V, G)]
            for e in (P, A, V, G):
                e.wait(ends)
            return ends

        def mm(o, l, r, start, stop, waits=(), sig=False):
            return P(lambda e: e.matmul(o, lhsT=l, rhs=r, start=start, stop=stop), waits, sig)

        def tr(o, i, waits=(), sig=False):
            idn = cc("ident")
            return P(lambda e: e.transpose(o, i, idn), waits, sig)

        def act(o, i, f, waits=(), **kw):
            return A(lambda e: e.activation(o, i, f, **kw), waits)

        def tt(o, a, b, op, waits=()):
            return V(lambda e: e.tensor_tensor(o, a, b, op), waits)

        def ts(o, a, s1, s2, op0, op1=None, waits=()):
            if op1 is None:
                return V(lambda e: e.tensor_scalar(o, a, s1, None, op0), waits)
            return V(lambda e: e.tensor_scalar(o, a, s1, s2, op0, op1), waits)

        def stt(o, a, s, b, op0, op1, waits=()):
            return V(lambda e: e.scalar_tensor_tensor(out=o, in0=a, scalar=s, in1=b, op0=op0, op1=op1), waits)

        def red(o, i, op, waits=(), **kw):
            return V(lambda e: e.tensor_reduce(o, i, AX, op, **kw), waits)

        def recip(o, i, waits=()):
            return V(lambda e: e.reciprocal(o, i), waits)

        def vcopy(o, i, waits=()):
            return V(lambda e: e.tensor_copy(o, i), waits)

        def vset(o, v, waits=()):
            return V(lambda e: e.memset(o, v), waits)

        flip = [0]

        def copy(o, i, waits):
            flip[0] ^= 1
            if flip[0]:
                return act(o, i, ACT.Copy, waits)
            return vcopy(o, i, waits)

        def halves(hi, lo, src, waits):
            t = act(hi, src, ACT.Copy, waits)
            return tt(lo, src, hi.bitcast(fp32), ALU.subtract, [t])

        listed, ready = [], []
        at = {"use": 0, "dma": 0, "split": 0}

        def pump():
            if plan is None:
                return
            moved = True
            while moved:
                moved = False
                if at["dma"] < len(plan):
                    r = raw.bufs[at["dma"] % NRAW]
                    if not r.busy:
                        src, view, after, cut = plan[at["dma"]]
                        dst = view(r.ap)
                        tok = SP.dma(lambda e, d=dst, s=src: e.dma_start(d, s), r.chan, r.free + after)
                        r.busy = True
                        ready.append((r, tok))
                        at["dma"] += 1
                        moved = True
                if at["split"] < at["dma"]:
                    r, tok = ready[at["split"]]
                    cut = plan[at["split"]][3]
                    if not cut:
                        at["split"] += 1
                        moved = True
                    elif not spr.bufs[spr.i % NSPL].busy:
                        b = spr.next()
                        b.busy = True
                        n = plan[at["split"]][0].free_size()
                        t = halves(b.ap[0][:, 0:n], b.ap[1][:, 0:n], r.ap[:, 0:n], [tok] + b.free)
                        r.free, r.busy = [t], False
                        ready[at["split"]] = (b, t)
                        at["split"] += 1
                        moved = True

        def piece(src, cut=True, view=None, after=()):
            n = src.free_size()
            parts = src.shape[0]
            listed.append((src, view or (lambda ap: ap[0:parts, 0:n]), list(after), cut))
            if plan is None:
                return (spr.bufs[0] if cut else raw.bufs[0]), None
            if at["split"] <= at["use"]:
                pump()
            got = ready[at["use"]]
            at["use"] += 1
            return got

        def done(buf, tok):
            pump()
            buf.free, buf.busy = [tok], False

        THREE = ((0, 0), (0, 1), (1, 0))

        def go(gen):
            for _ in gen:
                pass

        def linT(srcs, rhs, rhs_toks, n, evac, ks=None):
            ps = PP.next()
            o = ps.ap[:, 0:S]
            kt = sum(s.free_size() // 128 for s in srcs)
            ks = ks or range(kt)
            k = 0
            for src in srcs:
                b, ld = piece(src)
                for j in range(src.free_size() // 128):
                    last = j == src.free_size() // 128 - 1
                    for a, c in THREE:
                        end = last and (a, c) == THREE[-1]
                        tok = mm(o, b.ap[a][:, j * 128:(j + 1) * 128], rhs[c][:, ks[k], :], k == 0 and a + c == 0,
                                 k == kt - 1 and (a, c) == THREE[-1],
                                 [ld, rhs_toks[ks[k]]] + (ps.free if k == 0 else []), end)
                    k += 1
                done(b, tok)
                if k == kt:
                    ps.free = evac(n, o, tok)
                yield

        def linN(srcs, lhs, lhs_toks, cols, evac):
            pss = [PP.next(), PP.next()]
            kt = sum(s.free_size() // cols for s in srcs)
            k0 = 0
            for src in srcs:
                b, ld = piece(src)
                nk = src.free_size() // cols
                for i in range(2):
                    ps = pss[i]
                    for j in range(nk):
                        k = k0 + j
                        for a, c in THREE:
                            tok = mm(ps.ap[:, 0:cols], lhs[c][:, k, i * 128:(i + 1) * 128],
                                     b.ap[a][:, j * cols:(j + 1) * cols], k == 0 and a + c == 0,
                                     k == kt - 1 and (a, c) == THREE[-1],
                                     [ld, lhs_toks[k]] + (ps.free if k == 0 else []),
                                     j == nk - 1 and (a, c) == THREE[-1])
                    if k0 + nk == kt:
                        ps.free = evac(i, ps.ap[:, 0:cols], tok)
                k0 += nk
                done(b, tok)
                yield

        def two(w, n):
            h = w.shape[2] // 2
            return [w[n, :, 0:h], w[n, :, h:2 * h]]

        def rmsnorm(src, gain, nkt, toks, NT, pair=None, dst=None, after=()):
            ps = PP.next()
            for k in range(nkt):
                b = NT.next()
                t = act(b.ap, src[:, k, :], ACT.Square, [toks[k]] + b.free)
                t = mm(ps.ap[:, 0:S], ones[:, :], b.ap, k == 0, k == nkt - 1,
                       [t, t_ones] + (ps.free if k == 0 else []), True)
                b.free = [t]
            var, dev, inv = (nrm[:, i * S:(i + 1) * S] for i in range(3))
            t = ts(var, ps.ap[:, 0:S], 1.0 / (nkt * 128), 1e-6, ALU.mult, ALU.add, [t])
            ps.free = [t]
            t = act(dev, var, ACT.Sqrt, [t])
            t = recip(inv, dev, [t])
            out_t = []
            for k in range(nkt):
                if dst is not None:
                    o, free = dst[:, k, :], []
                else:
                    b = NT.next()
                    o, free = b.ap, b.free
                t1 = stt(o, src[:, k, :], vcol(gain, k), inv, ALU.mult, ALU.mult, [t, toks[k], t_vec] + free)
                if pair is not None:
                    t1 = halves(pair[0][:, k, :], pair[1][:, k, :], o, [t1] + list(after))
                if dst is None:
                    b.free = [t1]
                out_t.append(t1)
            return out_t

        def residual(n, o, tok):
            xt[n] = tt(XT[:, n, :], o, XT[:, n, :], ALU.add, [tok, xt[n]])
            return [xt[n]]

        def smalls(tile, n):
            return Ring([Buf(tile[:, 8 * i:8 * i + 8]) for i in range(n)])

        def softmax(job, SB, small):
            nk = (job["i"] + 1) * 128
            c = small.next()
            parts, scale = job["parts"], job.get("scale", 1.0)
            for n, u in enumerate(parts):
                ps = PS.next()
                for j, (l, r) in enumerate(u["qk"]):
                    tok = mm(ps.ap[:, 0:nk], l, r, j == 0, j == len(u["qk"]) - 1,
                             u["toks"] + (ps.free if j == 0 else []), j == len(u["qk"]) - 1)
                b = u["buf"] = SB.next()
                o, i0, i1, ac = b.ap[:, 0:nk], ps.ap[:, 0:nk], u["bias"], c.ap[:, n:n + 1]
                t = V(lambda e, o=o, i0=i0, i1=i1, ac=ac: e.tensor_tensor_reduce(
                    out=o, in0=i0, in1=i1, scale=1.0, scalar=LOW, op0=ALU.add, op1=ALU.max, accum_out=ac),
                    [tok] + u["btoks"] + b.free + c.free)
                ps.free = [t]
            if len(parts) == 1:
                t = ts(c.ap[:, 3:4], c.ap[:, 0:1], -scale, None, ALU.mult, waits=[t])
            else:
                t = red(c.ap[:, 3:4], c.ap[:, 0:len(parts)], ALU.max, [t], negate=True)
            for n, u in enumerate(parts):
                o = u["buf"].ap[:, 0:nk]
                t2 = act(o, o, ACT.Exp, [t], bias=c.ap[:, 3:4], scale=scale, accum_out=c.ap[:, 4 + n:5 + n])
            if len(parts) > 1:
                t2 = red(c.ap[:, 7:8], c.ap[:, 4:4 + len(parts)], ALU.add, [t2])
                t2 = recip(c.ap[:, 7:8], c.ap[:, 7:8], [t2])
            else:
                t2 = recip(c.ap[:, 7:8], c.ap[:, 4:5], [t2])
            for u in parts:
                o = u["buf"].ap[:, 0:nk]
                if job.get("gate") is not None:
                    u["p"] = ts(o, o, c.ap[:, 7:8], job["gate"], ALU.mult, ALU.mult, [t2] + job["gtoks"])
                else:
                    u["p"] = ts(o, o, c.ap[:, 7:8], None, ALU.mult, waits=[t2])
            c.free = [u["p"]]

        def transposed(job, PB):
            i = job["i"]
            for u in job["parts"]:
                pt = PT.next()
                for b in range(i + 1):
                    tok = tr(pt.ap[:, b * 128:(b + 1) * 128], u["buf"].ap[:, b * 128:(b + 1) * 128],
                             [u["p"]] + pt.free, b == i)
                u["buf"].free = [tok]
                pb = u["pb"] = PB.next()
                u["pT"] = copy(pb.ap[:, 0:(i + 1) * 128], pt.ap[:, 0:(i + 1) * 128], [tok] + pb.free)
                pt.free = [u["pT"]]

        def attend(job):
            i = job["i"]
            for u in job["parts"]:
                pb, o = u["pb"], u["out"]
                for b in range(i + 1):
                    tok = mm(o, u["v"](b), pb.ap[:, b * 128:(b + 1) * 128], u["start"] and b == 0,
                             u["stop"] and b == i, [u["pT"]] + u["vtoks"] + u["ofree"], b == i)
                pb.free = [tok]
            if job.get("done"):
                job["done"](tok)

        def weave(jobs, front, back, PB, fillers, lag=2):
            todo = [list(f) + [0, None][len(f) - 2:] for f in fillers]
            steps = len(jobs) + lag + 1
            now = [None]

            def advance(n, most, due):
                while most > 0 and (todo or now[0]):
                    if now[0] is None:
                        free = [f for f in todo if f[2] <= n]
                        if not free:
                            return
                        soon = [f for f in free if f[3] is not None]
                        now[0] = soon[0] if soon and (due or soon[0][3] <= n + 8) else free[0]
                        todo.remove(now[0])
                    if next(now[0][0], True):
                        now[0] = None
                    else:
                        now[0][1] -= 1
                        most -= 1
            for n in range(steps):
                if n > lag:
                    back(jobs[n - lag - 1])
                if lag <= n < len(jobs) + lag:
                    transposed(jobs[n - lag], PB)
                if n < len(jobs):
                    while any(f[3] is not None and f[3] <= n for f in todo + [now[0]] * (now[0] is not None)):
                        advance(n, 1, True)
                    front(jobs[n])
                left = sum(f[1] for f in todo) + (now[0][1] if now[0] else 0)
                advance(n, -(-left // (steps - n)), False)
            while todo or now[0]:
                advance(steps, 1, False)

        ch_c, ch_v, ch_x, ch_b, ch_t = (Chan(sem(f"s_{n}")) for n in ("c", "v", "x", "b", "t"))
        t_x = SP.dma(lambda e: e.dma_start(XT, D["xT"].rearrange("(k p) t -> p k t", p=128)), ch_x)
        t_cst = SP.dma(lambda e: e.dma_start(cst[:, :], D["cst"]), ch_c)
        t_vec = SP.dma(lambda e: e.dma_start(vec[:, :], D["vec"]), ch_v)
        t_ones = vset(ones[:, :], 1.0)
        xt = [t_x] * 16
        H = (HH, HL)

        st = ExitStack()
        al = allocator(st)
        share(2, 1, 2)
        qT, kT = tiles(al(12 * S)), tiles(al(12 * S))
        vN = al(2 * 1280).rearrange("p (i c) -> p i c", i=2)
        gts = al(72).rearrange("p (i c) -> p i c", i=2)
        bias = tiles(al(24 * S))
        ots = al(16 * S)
        oT = tiles(ots)
        SB = Ring([Buf(al(S)) for _ in range(7)])
        PB = Ring([Buf(al(S)) for _ in range(3)])
        NT = Ring(PB.bufs + SB.bufs[0:2])
        small = smalls(al(64), 8)
        peT = al(64).rearrange("p (b l) -> p b l", b=2)
        hid = al(45)
        hidR = al(3 * 128).rearrange("p (k g n) -> p k g n", k=3, g=4)
        kcT = al(45)
        vcR = al(3 * 64).rearrange("p (k d) -> p k d", k=3)
        w2 = al(128).rearrange("p (b d) -> p b d", b=2)
        pcs = al(1536)
        Pc = pcs[:, 0:768].rearrange("p (i h n) -> p i h n", i=2, h=12)
        PcT = pcs[:, 768:1536].rearrange("p (k i t) -> p k i t", k=3, i=2)
        csm = al(64)
        relT = al(32)
        oneh = ots[:, 0:1536].rearrange("p (v j) -> p v j", v=4)
        toe = pcs.rearrange("p (v j) -> p v j", v=4)
        tpe = ots[:, 1536:1536 + 1440].rearrange("p (l k n) -> p l k n", l=32, k=3)
        kst = ots[:, 3072:3072 + S]

        SP.dma(lambda e: e.dma_start(oneh[0:33], D["oneh"].rearrange("b (v j) -> b v j", v=4)), ch_b)
        SP.dma(lambda e: e.dma_start(relT[0:33, :], D["relT"]), ch_b)
        SP.dma(lambda e: e.dma_start(peT[0:64], D["peT"].rearrange("d (b l) -> d b l", b=2)), ch_b)
        t_b = SP.dma(lambda e: e.dma_start(w2[:, :, :], D["cw2"].rearrange("p (b d) -> p b d", b=2)), ch_b)
        for v, (a, b) in enumerate([(0, 4), (4, 8), (8, 12), (12, 32)]):
            ps = PP.next()
            tok = mm(ps.ap[0:b - a, 0:384], relT[0:33, a:b], oneh[0:33, v, :], True, True, [t_b] + ps.free, True)
            t = vcopy(toe[0:b - a, v, :], ps.ap[0:b - a, 0:384], [tok])
            ps.free = [t]
            td = SP.dma(lambda e, v=v, a=a, b=b: e.dma_start(D["toe"][a:b, :], toe[0:b - a, v, :]), ch_t, [t])
        tb = [None] * 24

        def make_bias(head, slot, after=()):
            src = bass.AP(D["toe"].tensor, head * 384, [[1, 128], [384, 4], [1, 256]])
            s, ld = piece(src, False, lambda ap: ap.rearrange("p (h t) -> p h t", h=4), [td])
            for c in range(2):
                ps = PP.next()
                tok = mm(ps.ap, cc("exch"), s.ap[:, 512 * c:512 * c + 512], True, True,
                         [ld, t_cst] + ps.free, True)
                h = slot + 2 * c
                t = copy(bias[:, h:h + 2, :].rearrange("p h t -> p (h t)"), ps.ap, [tok] + list(after))
                tb[h] = tb[h + 1] = t
                ps.free = [t]
            done(s, tok)
            yield

        ht = rmsnorm(XT, "norm_attn", 16, xt, NT, pair=H)
        tq, tk, tv = [None] * 12, [None] * 12, {}

        def to_q(n, slot, after=()):
            def f(_, o, tok):
                tq[slot] = act(qT[:, slot, :], o, ACT.Copy, [tok] + list(after), scale=0.125)
                return [tq[slot]]
            return linT(two(D["w_in"], n), H, ht, 0, f)

        def to_k(w, n, slot, after=()):
            def f(_, o, tok):
                tk[slot] = vcopy(kT[:, slot, :], o, [tok] + list(after))
                return [tk[slot]]
            return linT(two(w, n), H, ht, 0, f)

        def to_v(w, n, at, after=()):
            def f(i, o, tok):
                tv[at, i] = copy(vN[:, i, at:at + 128], o, [tok] + list(after))
                return [tv[at, i]]
            return linN(two(w, n), H, ht, 128, f)

        for j in range(6):
            go(to_q(30 + j, j))
        unit_t = {}
        tpe_free, hid_free, kst_free = [], [], []
        cmp_t = {}

        def window(what, src, tok):
            kind, kv = what // 3, what % 3
            v = src.rearrange("p (n r) -> p r n", r=16)
            for a in range(2):
                pe = peT[0:64, kind, 16 * a:16 * a + 16].unsqueeze(2).to_broadcast([64, 16, 15])
                t = tt(tpe[0:64, 16 * a:16 * a + 16, kv, :], v[:, :, a:a + 15], pe, ALU.add, [tok, t_b] + tpe_free)
            unit_t[what] = t
            return t

        def compress(br):
            ps = PP.next()
            for p in range(4):
                s, ld = piece(D["cw1"][br, p], False)
                for l in range(8):
                    tok = mm(ps.ap[:, 0:45], s.ap[0:64, l * 128:(l + 1) * 128],
                             tpe[0:64, 8 * p + l].rearrange("p k n -> p (k n)"), p + l == 0, p == 3 and l == 7,
                             [ld] + [unit_t[3 * br + kv] for kv in range(3)] + (ps.free if p + l == 0 else []),
                             l == 7)
                done(s, tok)
            tpe_free[:] = [tok]
            t = act(hid[:, :], ps.ap[:, 0:45], ACT.Gelu_apprx_tanh, [tok] + hid_free)
            ps.free = [t]
            po = PP.next()
            if br == 0:
                for b in (0, 64):
                    tok = mm(po.ap[b:b + 64, 0:45], w2[:, 0, :], hid[:, :], True, True, [t, t_b] + po.free, True)
                hid_free[:] = [tok]
                cmp_t["k"] = vcopy(kcT[:, :], po.ap[:, 0:45], [tok])
                po.free = [cmp_t["k"]]
            else:
                t0 = vset(hidR[:, :, :, :], 0.0)
                h3 = hid.rearrange("p (k n) -> p k n", k=3)
                for g in range(4):
                    t1 = vcopy(hidR[:, :, g, 0:15], h3, [t, t0])
                for kv in range(3):
                    tok = mm(po.ap[:, 64 * kv:64 * kv + 64], hidR[:, kv, :, :].rearrange("p g n -> p (g n)"),
                             w2[:, 1, :], True, True, [t1, t_b] + po.free, kv == 2)
                cmp_t["v"] = vcopy(vcR[:, :, :].rearrange("p k d -> p (k d)"), po.ap[:, 0:192], [tok])
                po.free = [cmp_t["v"]]

        for n in range(3):
            def f_kv(n, o, tok):
                t = window(2 * n, o[0:64, :], tok)
                t2 = act(kst[0:64, :], o[64:128, :], ACT.Copy, [t] + kst_free)
                if n == 1:
                    late.append(t2)
                else:
                    kst_free[:] = [window(2 * n + 1, kst[0:64, :], t2)]
                return [t2]
            late = []
            go(linT(two(D["w_cmp"], n), H, ht, n, f_kv))
            if n == 1:
                compress(0)
                kst_free[:] = [window(3, kst[0:64, :], late[0])]
        for q in range(3):
            go(make_bias(20 + 4 * q, 4 * q))
        for j in range(6):
            go(to_k(D["w_kdup"], j, j))
        compress(1)
        for j in range(3):
            go(to_v(D["w_vc"], j, 128 * j))
        tg = [None, None]

        def f_gate(i, o, tok):
            tg[i] = act(gts[:, i, :], o, ACT.Sigmoid, [tok])
            return [tg[i]]
        go(linN([D["w_gate"]], H, ht, 36, f_gate))

        t_pz = vset(Pc[:, :, :, :], 0.0, [td])

        def compressed(i):
            pc = Pc[:, i, :, 0:15]
            ng = cc("cmpneg")[:, 15 * i:15 * i + 15].unsqueeze(1).to_broadcast([128, 6, 15])
            ok = cc("cmp01")[:, 15 * i:15 * i + 15].unsqueeze(1).to_broadcast([128, 12, 15])
            for odd in range(2):
                ps = PP.next()
                sc = ps.ap[:, 0:192].rearrange("p (h n) -> p h n", h=6)[:, :, 0:15]
                for m in range(6):
                    b, h = 64 * odd, 2 * m + odd
                    tok = mm(ps.ap[:, 32 * m:32 * m + 15], qT[b:b + 64, m, i * 128:(i + 1) * 128],
                             kcT[b:b + 64, 15 * (h // 4):15 * (h // 4) + 15], True, True,
                             [tq[m], cmp_t["k"]] + ps.free, m == 5)
                t = tt(pc[:, odd:12:2, :], sc, ng, ALU.add, [tok, t_cst, t_pz])
                ps.free = [t]
            mx, dn = csm[:, 24 * i:24 * i + 12], csm[:, 24 * i + 12:24 * i + 24]
            t = red(mx, pc, ALU.max, [t])
            t = tt(pc, pc, mx.unsqueeze(2).to_broadcast([128, 12, 15]), ALU.subtract, [t])
            t = act(pc, pc, ACT.Exp, [t])
            t = tt(pc, pc, ok, ALU.mult, [t])
            t = red(dn, pc, ALU.add, [t])
            t = ts(dn, dn, 1e-30, None, ALU.max, waits=[t])
            t = recip(dn, dn, [t])
            t = tt(dn, dn, gts[:, i, 0:36].rearrange("p (h b) -> p h b", b=3)[:, :, 0], ALU.mult, [t, tg[i]])
            return tt(pc, pc, dn.unsqueeze(2).to_broadcast([128, 12, 15]), ALU.mult, [t])

        def compressed_T(i, t):
            pt = PT.next()
            for kv in range(3):
                tok = tr(pt.ap[:, kv * 128:(kv + 1) * 128],
                         Pc[:, i, 4 * kv:4 * kv + 4, :].rearrange("p h n -> p (h n)"), [t, t_cst] + pt.free, kv == 2)
            t = vcopy(PcT[:, :, i, :], pt.ap[:, 0:384].rearrange("p (k t) -> p k t", k=3), [tok])
            pt.free = [t]
            return t

        tcp = [compressed(0), compressed(1)]
        for j in range(2):
            go(to_q(j, 6 + j))
        t_pct = [compressed_T(i, tcp[i]) for i in range(2)]
        ot = [None] * 16

        def front(job):
            i, nk = job["i"], (job["i"] + 1) * 128
            parts = []
            for q, k, base, bi, at, n in job["parts"]:
                a = at // 128 * 128
                parts.append({
                    "qk": [(qT[base:base + 64, q, i * 128:(i + 1) * 128], kT[base:base + 64, k, 0:nk])],
                    "toks": [tq[q], tk[k]], "bias": bias[:, bi, 128 - 128 * i:S], "btoks": [tb[bi]],
                    "v": lambda b, at=at: vN[:, b, at:at + 64], "vtoks": [tv[a, 0], tv[a, 1]],
                    "out": job["ps"][n].ap[base:base + 64, i * 128:(i + 1) * 128], "start": True, "stop": True})
            job["parts"] = parts
            softmax(job, SB, small)

        def back(job):
            i = job["i"]
            for n, u in enumerate(job["parts"]):
                u["ofree"] = job["ps"][n].free
            if "c" in job:
                h, br = job["c"]
                u = job["parts"][0]
                if br == 0:
                    g = h % 4
                    mm(u["out"], vcR[32 * g:32 * g + 32, h // 4, :], PcT[32 * g:32 * g + 32, h // 4, i, :],
                       True, False, [t_pct[i], cmp_t["v"]] + u["ofree"])
                    u["start"], u["stop"] = False, False
                else:
                    u["start"] = False

            def finish(tok):
                for n, tile in enumerate(job["tiles"]):
                    ot[tile] = copy(oT[:, tile, :], job["ps"][n].ap[:, 0:S], [tok])
                    job["ps"][n].free = [ot[tile]]
                    if job.get("split"):
                        job["split"](tile)
            if job.get("last"):
                job["done"] = finish
            attend(job)

        jobs = []
        for hp in range(6):
            ps = [PO.next()]
            for h in (2 * hp, 2 * hp + 1):
                kv = h // 4
                for i in range(2):
                    for br in range(2):
                        jobs.append({"i": i, "ps": ps, "tiles": [10 + hp], "c": (h, br),
                                     "gate": gts[:, i, 3 * h + 1 + br:3 * h + 2 + br], "gtoks": [tg[i]],
                                     "parts": [(hp, 3 * br + kv, 64 * (h % 2), h, 192 * br + 64 * kv, 0)]})
            jobs[-1]["last"] = True
        todo = []
        for g in range(3):
            for j in range(2):
                if g:
                    todo.append((to_q(6 * g + j, 6 + 2 * g + j), 2))
                todo.append((to_k(D["w_in"], 6 * g + 2 + j, 6 + 2 * g + j), 2))
                todo.append((to_v(D["w_in"], 6 * g + 4 + j, 512 + g * 256 + j * 128), 2))
            todo.append((make_bias(4 * g, 12 + 4 * g), 1))
        weave(jobs, front, back, PB, todo, 3)
        jobs = []
        for jp in range(2):
            ps = [PO.next() for _ in range(3)]
            for j in (2 * jp, 2 * jp + 1):
                for i in range(2):
                    jobs.append({"i": i, "ps": ps, "tiles": [2 * g + jp for g in range(3)], "parts": [
                        (6 + 2 * g + jp, 6 + 2 * g + jp, 64 * (j % 2), 12 + 4 * g + j, 512 + g * 256 + 64 * j, g)
                        for g in range(3)]})
            jobs[-1]["last"] = True
        room = [P.last(), V.last()]
        todo = [(make_bias(12 + 4 * q, 4 * q, room), 1) for q in range(2)]
        for j in range(4):
            todo.append((to_q(18 + j, j, room), 2))
            todo.append((to_k(D["w_in"], 22 + j, j, room), 2))
            todo.append((to_v(D["w_in"], 26 + j, 128 * j, room), 2))
        weave(jobs, front, back, PB, todo, 1)
        h_read = [P.last()]
        os_ = [None] * 16

        def split_o(tile):
            os_[tile] = halves(HH[:, tile, :], HL[:, tile, :], oT[:, tile, :], [ot[tile]] + h_read)
        jobs = []
        for hp in range(4):
            ps = [PO.next()]
            for h in (2 * hp, 2 * hp + 1):
                for i in range(2):
                    jobs.append({"i": i, "ps": ps, "tiles": [6 + hp], "split": split_o,
                                 "parts": [(hp, hp, 64 * (h % 2), h, 64 * h, 0)]})
            jobs[-1]["last"] = True
        early = (0, 1, 2, 3, 4, 5, 10, 11, 12, 13, 14, 15)
        for n in early:
            split_o(n)
        todo = [(linT([D["w_out"][n, :, 0:768], D["w_out"][n, :, 1280:2048]], H, os_, n, residual, early), 2)
                for n in range(16)]
        weave(jobs, front, back, PB, todo, 3)
        for n in range(16):
            go(linT([D["w_out"][n, :, 768:1280]], H, os_, n, residual, (6, 7, 8, 9)))
        fence()
        st.close()

        st = ExitStack()
        al = allocator(st)
        share(6, 1, 1)
        FF = Ring([Buf((tiles(al(8 * S, f32r)), tiles(al(8 * S, f32r)))) for _ in range(2)])
        CA = Ring([Buf(al(S)) for _ in range(6)])
        NT = Ring([Buf(al(S)) for _ in range(5)])
        h2 = rmsnorm(XT, "norm_mlp", 16, xt, NT, pair=H)

        def conv3(n, o, tok):
            b = CA.next()
            t = act(b.ap, o, ACT.Identity, [tok, t_vec] + b.free, bias=vcol("conv_b", n), scale=vcol("conv_w", n))
            for j in (1, 2):
                t = stt(b.ap[:, j:S], o[:, 0:S - j], vcol("conv_w", 88 * j + n), b.ap[:, j:S], ALU.mult, ALU.add, [t])
            return b, t

        def up(n, ffb, k, ft):
            got = []

            def f_up(m, o, tok):
                got.append(conv3(m, o, tok))
                return [got[-1][1]]
            go(linT(two(D["w_up"], n), H, h2, n, f_up))
            go(linT(two(D["w_up"], 44 + n), H, h2, 44 + n, f_up))
            (ba, ta), (bg, tgg) = got
            t = act(bg.ap, bg.ap, ACT.Silu, [tgg])
            t = tt(ba.ap, ba.ap, bg.ap, ALU.mult, [t, ta])
            bg.free = [t]
            ft.append(halves(ffb.ap[0][:, k, :], ffb.ap[1][:, k, :], ba.ap, [t] + ffb.free))
            ba.free = [ft[-1]]

        def down(c, ffb, ft):
            m = len(ft)
            for n in range(16):
                go(linT([D["w_down"][n, :, c * COLS:c * COLS + m * 128]], ffb.ap, ft, n, residual))
            ffb.free = [P.last()]

        before = None
        for c in range(6):
            ffb, ft = FF.next(), []
            for k in range(8 if c < 5 else 4):
                up(8 * c + k, ffb, k, ft)
                if k == 1 and before:
                    down(*before)
            before = (c, ffb, ft)
        down(*before)
        xt = rmsnorm(XT, "norm_final", 16, xt, NT, dst=XT)
        ends = fence()
        st.close()

        st = ExitStack()
        al = allocator(st)
        ots = al(16 * S)
        share(3, 1, 2)
        o2, Y = tiles(ots), tiles(al(16 * S))
        st2 = ExitStack()
        al = allocator(st2)
        LH, LL = tiles(al(10 * S, f32r)), tiles(al(10 * S, f32r))
        lat = o2
        HB = Ring([Buf([tiles(al(2 * S)), tiles(al(2 * S)), al(S),
                        al(512).rearrange("p (i c) -> p i c", i=2)]) for _ in range(3)])
        kp = al(S)
        SB = Ring([Buf(al(S)) for _ in range(4)])
        PB = Ring([Buf(al(S)) for _ in range(3)])
        small = smalls(al(64), 8)
        RW = Ring([Buf(al(S), Chan(sem(f"s_r{i}"))) for i in range(2)])
        for b in RW.bufs:
            b.free = ends
        RS = Ring([Buf([al(S) for _ in range(4)]) for i in range(2)])
        RO = Ring([Buf(al(S)) for _ in range(2)])
        NT = Ring([Buf(Y[:, i, :]) for i in range(10, 16)])
        sp = [al(16) for _ in range(4)]
        n4 = rmsnorm(XT, "attn_norm_2", 16, xt, NT, pair=H)
        lt = [None] * 10

        def f_lat(base):
            def f(n, o, tok):
                lt[base + n] = copy(lat[:, base + n, :], o, [tok])
                return [lt[base + n]]
            return f
        for n in range(6):
            go(linT(two(D["w_cq"], n), H, n4, n, f_lat(0)))
        for n in range(4):
            go(linT(two(D["w_ckv"], n), H, n4, n, f_lat(6)))

        def rope(o, dst, waits):
            sw = RO.next()
            for b in (0, 64):
                for x, y in ((b, b + 32), (b + 32, b)):
                    t = act(sw.ap[x:x + 32, :], o[y:y + 32, :], ACT.Copy, waits + sw.free)
            t2 = tt(dst, o, cc("cos"), ALU.mult, [t, t_cst])
            t = tt(sw.ap, sw.ap, cc("sin"), ALU.mult, [t])
            t = tt(dst, dst, sw.ap, ALU.add, [t, t2])
            sw.free = [t]
            return t

        kpt = []

        def f_kr(_, o, tok):
            kpt.append(rope(o, kp, [tok]))
            return [kpt[0]]
        go(linT(two(D["w_kr"], 0), H, n4, 0, f_kr))
        Lq, Lk = (LH[:, 0:6, :], LL[:, 0:6, :]), (LH[:, 6:10, :], LL[:, 6:10, :])

        lam = vcol("lru_lambda_2", 0, 16)
        t = act(sp[0], lam, ACT.Abs, [t_vec])
        t = act(sp[0], sp[0], ACT.Exp, [t], scale=-1.0)
        t1 = ts(sp[1], sp[0], 2.0, None, ALU.add, waits=[t])
        t1 = recip(sp[1], sp[1], [t1])
        t1 = tt(sp[1], sp[1], sp[0], ALU.mult, [t1])
        t2 = tt(sp[2], sp[1], sp[1], ALU.mult, [t1])
        t2 = ts(sp[3], sp[2], 1.0 / 19, 1.0 / 17, ALU.mult, ALU.add, [t2])
        for d in (15, 13, 11, 9, 7, 5, 3, 1):
            t2 = tt(sp[3], sp[3], sp[2], ALU.mult, [t2])
            t2 = ts(sp[3], sp[3], 1.0 / d, None, ALU.add, waits=[t2])
        t2 = tt(sp[3], sp[3], sp[1], ALU.mult, [t2])
        t2 = ts(sp[3], sp[3], 16.0, None, ALU.mult, waits=[t2])
        t2 = ts(sp[0], lam, -1.0, 0.0, ALU.mult, ALU.max, [t2])
        t2 = stt(sp[3], sp[0], 8.0, sp[3], ALU.mult, ALU.add, [t2])
        t_sp = ts(sp[2], sp[3], -1.0, None, ALU.mult, waits=[t2])

        yt = [None] * 16

        def recurrent(j):
            sr = RS.next()
            xc, r, w, z = sr.ap
            rw = RW.next()
            t_rw = SP.dma(lambda e: e.dma_start(rw.ap, D["w_rg"][j]), rw.chan, rw.free)
            got = []

            def f_x(n, o, tok):
                t = act(xc, o, ACT.Identity, [tok, t_vec] + sr.free, bias=vcol("conv_b_2", n),
                        scale=vcol("conv_w_2", 48 + n))
                for k in (1, 2, 3):
                    t = stt(xc[:, k:S], o[:, 0:S - k], vcol("conv_w_2", 16 * (3 - k) + n), xc[:, k:S],
                            ALU.mult, ALU.add, [t])
                got.append(t)
                return [t]

            def f_y(n, o, tok):
                got.append(act(Y[:, n, :], o, ACT.Gelu_apprx_tanh, [tok] + nt_read))
                return [got[-1]]
            yield from linT(two(D["w_xr"], j), H, n4, j, f_x)
            yield from linT(two(D["w_yr"], j), H, n4, j, f_y)
            t_xc, t_y = got
            ps = PP.next()
            mm(ps.ap[:, 0:S], rw.ap[:, 0:128], xc, True, True, [t_rw, t_xc] + ps.free)
            tok = mm(ps.ap[:, S:2 * S], rw.ap[:, 128:256], xc, True, True, [], True)
            rw.free = [tok]
            t_i = act(w, ps.ap[:, S:2 * S], ACT.Sigmoid, [tok] + sr.free, bias=vcol("b_rg_x_2", j))
            t_r = act(r, ps.ap[:, 0:S], ACT.Sigmoid, [], bias=vcol("b_rg_a_2", j))
            ps.free = [t_r]
            t_g = tt(xc, xc, w, ALU.mult, [t_i, tok])
            t_t = act(w, r, ACT.Tanh, [t_r, t_g, t_sp], scale=sp[3][:, j:j + 1])
            t_a = act(r, r, ACT.Exp, [t_t], scale=sp[2][:, j:j + 1])
            t = ts(z, w, 1.0, None, ALU.add, waits=[t_t])
            t = recip(z, z, [t])
            t = stt(w, w, 2.0, z, ALU.mult, ALU.mult, [t])
            t = act(w, w, ACT.Sqrt, [t])
            t = vset(w[:, 0:1], 1.0, [t])
            t = tt(w, w, xc, ALU.mult, [t])
            t = V(lambda e: e.tensor_tensor_scan(z, r, w, 0.0, ALU.mult, ALU.add), [t, t_a])
            yt[j] = tt(Y[:, j, :], Y[:, j, :], z, ALU.mult, [t, t_y])
            sr.free = [yt[j]]

        nt_read = []
        go(recurrent(0))
        lq = rmsnorm(lat[:, 0:6, :], "q_norm_2", 6, lt[0:6], NT, pair=Lq)
        go(recurrent(1))
        lk = rmsnorm(lat[:, 6:10, :], "kv_norm_2", 4, lt[6:10], NT, pair=Lk)
        nt_read = [P.last(), V.last()]
        go(recurrent(2))
        to = [None] * 16
        heads = {}

        def project(p):
            hb = HB.next()
            qn, kn, qp, mv = hb.ap
            d = {"hb": hb, "t": []}

            def put(dst):
                def f(_, o, tok):
                    d["t"].append(copy(dst, o, [tok] + hb.free))
                    return [d["t"][-1]]
                return f

            def f_qp(_, o, tok):
                d["t"].append(rope(o, qp, [tok] + hb.free))
                return [d["t"][-1]]

            def f_v(i, o, tok):
                d["t"].append(copy(mv[:, i, :], o, [tok] + hb.free))
                return [d["t"][-1]]
            for j in range(2):
                yield from linT([D["w_qn"][2 * p + j]], Lq, lq, 0, put(qn[:, j, :]))
            yield from linT([D["w_qp"][p]], Lq, lq, 0, f_qp)
            for j in range(2):
                yield from linT([D["w_kn"][2 * p + j]], Lk, lk, 0, put(kn[:, j, :]))
            yield from linN([D["w_v"][p]], Lk, lk, 256, f_v)
            heads[p] = d

        def mla_front(job):
            h, i = job["h"], job["i"]
            d = heads[h // 2]
            qn, kn, qp, mv = d["hb"].ap
            j, b, nk = h % 2, 64 * (h % 2), (i + 1) * 128
            job["parts"] = [{
                "qk": [(qn[:, j, i * 128:(i + 1) * 128], kn[:, j, 0:nk]),
                       (qp[b:b + 64, i * 128:(i + 1) * 128], kp[b:b + 64, 0:nk])],
                "toks": d["t"] + [kpt[0]], "bias": cc("mask")[:, 128 - 128 * i:S], "btoks": [t_cst],
                "v": lambda b, j=j, mv=mv: mv[:, b, 128 * j:128 * j + 128], "vtoks": d["t"],
                "out": job["ps"].ap[:, i * 128:(i + 1) * 128], "start": True, "stop": True}]
            softmax(job, SB, small)

        def mla_back(job):
            h, ps = job["h"], job["ps"]
            job["parts"][0]["ofree"] = ps.free

            def finish(tok):
                to[h] = copy(o2[:, h, :], ps.ap[:, 0:S], [tok] + lat_read)
                ps.free = [to[h]]
                if h % 2:
                    heads[h // 2]["hb"].free = [tok]
            if job["i"] == 1:
                job["done"] = finish
            attend(job)

        lat_read = [lq[-1], lk[-1]]
        jobs = []
        for h in range(16):
            ps = PO.next()
            for i in range(2):
                jobs.append({"h": h, "i": i, "ps": ps, "scale": 192.0 ** -0.5})
        go(project(0))
        go(recurrent(3))
        go(project(1))
        todo = []
        for p in range(6):
            todo += [(recurrent(4 + 2 * p), 4), (project(2 + p), 7, 4 * p + 3, 4 * p + 8), (recurrent(5 + 2 * p), 4)]
        weave(jobs, mla_front, mla_back, PB, todo)
        fence()
        st2.close()
        st2 = ExitStack()
        al = allocator(st2)
        OQ = tiles(al(16 * S, f32r)), tiles(al(16 * S, f32r))
        YQ = tiles(al(16 * S, f32r)), tiles(al(16 * S, f32r))
        GB = Ring([Buf(nrm[:, i * S:(i + 1) * S]) for i in range(3)])
        tos, tys, tm = [None] * 16, [None] * 16, [None] * 16
        M = o2

        def f_sig(g, col):
            def f(_, o, tok):
                g.free = [act(g.ap, o, ACT.Sigmoid, [tok, t_vec] + g.free, bias=vcol("b_gate_2", col))]
                return g.free
            return f
        for n in range(16):
            tos[n] = halves(OQ[0][:, n, :], OQ[1][:, n, :], o2[:, n, :], [to[n]])
        for n in range(16):
            g = GB.next()

            def f_o(m, o, tok):
                tm[m] = tt(M[:, m, :], o, g.ap, ALU.mult, [tok, tos[m]] + g.free)
                g.free = [tm[m]]
                return [tm[m]]
            go(linT(two(D["w_ga"], n), H, n4, n, f_sig(g, n)))
            go(linT(two(D["w_attn_o"], n), OQ, tos, n, f_o))
            tys[n] = halves(YQ[0][:, n, :], YQ[1][:, n, :], Y[:, n, :], [yt[n]])
        oq_read = [P.last()]
        tms = [None] * 16
        for n in range(16):
            g = GB.next()

            def f_y2(m, o, tok):
                t = tt(g.ap, o, g.ap, ALU.mult, [tok] + g.free)
                t1 = tt(M[:, m, :], M[:, m, :], g.ap, ALU.add, [t, tm[m]])
                g.free = [t1]
                tms[m] = halves(OQ[0][:, m, :], OQ[1][:, m, :], M[:, m, :], [t1] + oq_read)
                return [t]
            go(linT(two(D["w_gr"], n), H, n4, n, f_sig(g, 16 + n)))
            go(linT(two(D["w_rnn_o"], n), YQ, tys, n, f_y2))
        for n in range(16):
            go(linT(two(D["w_out_2"], n), OQ, tms, n, residual))
        ends = fence()
        st2.close()
        st.close()

        st = ExitStack()
        al = allocator(st)
        share(4, 0, 4)
        sk = al(2048)
        xn = al(2 * 2048).rearrange("p (i c) -> p i c", i=2)
        acc = al(2048)
        pq = tiles(al(16 * S))
        eidx = al(256).bitcast(i32).rearrange("p (i k) -> p i k", i=2)
        gat = al(256).rearrange("p (i k) -> p i k", i=2)
        actv = al(256).rearrange("p (i k) -> p i k", i=2)
        SC = Ring([Buf(al(256)) for _ in range(2)])
        s2 = Ring([Buf(al(256)) for _ in range(2)])
        cand = al(256).rearrange("p (a b) -> p a b", a=16)
        oh = [al(256).rearrange("p (a b) -> p a b", a=16) for _ in range(2)]
        tvl, tfl = (al(32).rearrange("p (c k) -> p c k", c=2) for _ in range(2))
        til = al(32).bitcast(u32).rearrange("p (c k) -> p c k", c=2)
        bv, bf, e1 = al(16), al(32), al(32)
        bc, bd = al(16).bitcast(u32), al(32).bitcast(u32)
        hsm = al(8)
        n5s = al(16 * S)
        n5 = tiles(n5s)
        more = [al(2048) for _ in range(2)]
        NT = Ring([Buf(pq[:, i, :]) for i in range(5)])
        t_n5 = rmsnorm(XT, "ffn_norm_2", 16, xt, NT, pair=H, dst=n5)
        ch_k = Chan(sem("s_k"))
        t_sk = SP.dma(lambda e: e.dma_start(sk, D["subkeys"]), ch_k, ends)
        tpq = [None] * 16
        pq_free = [P.last()]

        def f_pq(n, o, tok):
            tpq[n] = act(pq[:, n, :], o, ACT.Copy, [tok] + pq_free)
            return [tpq[n]]

        def to_pq(n):
            go(linT(two(D["w_peer_q"], n), H, t_n5, n, f_pq))
        txn = [None, None]

        def natural(i):
            for c in range(4):
                pt = PT.next()
                for k in range(4):
                    tok = tr(pt.ap[:, k * 128:(k + 1) * 128], n5[:, 4 * c + k, i * 128:(i + 1) * 128],
                             [t_n5[4 * c + k]] + pt.free, k == 3)
                txn[i] = act(xn[:, i, 512 * c:512 * c + 512], pt.ap, ACT.Copy, [tok])
                pt.free = [txn[i]]
            return tok

        def top16(vals, idx, src, n, tok):
            b = s2.next()
            w = b.ap[:, 0:n]
            t = V(lambda e: e.max(vals[:, 0:8], src), [tok])
            V(lambda e: e.max_index(idx[:, 0:8], vals[:, 0:8], src), [t])
            t = V(lambda e: e.match_replace(w, vals[:, 0:8], src, LOW), [t] + b.free)
            t = V(lambda e: e.max(vals[:, 8:16], w), [t])
            t = V(lambda e: e.max_index(idx[:, 8:16], vals[:, 8:16], w), [t])
            b.free = [t]
            return t

        tga, tei = {}, {}
        scored = {}

        def score(i, h):
            ps = PP.next()
            for c in range(2):
                n = 2 * h + c
                tok = mm(ps.ap[:, c * 128:(c + 1) * 128], pq[:, n, i * 128:(i + 1) * 128],
                         sk[:, n * 128:(n + 1) * 128], True, True, [tpq[n], t_sk] + ps.free, c == 1)
            b = SC.next()
            t = act(b.ap, ps.ap[:, 0:256], ACT.Copy, [tok] + b.free)
            ps.free = [t]
            scored[i, h] = (b, t)

        def select(i, h):
            b, t = scored[i, h]
            for c in range(2):
                t2 = top16(tvl[:, c, :], til[:, c, :], b.ap[:, c * 128:(c + 1) * 128], 128, t)
            b.free = [t2]
            t = vcopy(tfl, til, [t2])
            t = tt(cand, tvl[:, 0, :].unsqueeze(2).to_broadcast([128, 16, 16]),
                   tvl[:, 1, :].unsqueeze(1).to_broadcast([128, 16, 16]), ALU.add, [t2])
            t2 = top16(bv, bc, cand.rearrange("p a b -> p (a b)"), 256, t)
            for c, (op, k) in enumerate(((ALU.logical_shift_right, 4), (ALU.bitwise_and, 15))):
                t = ts(bd[:, 16 * c:16 * c + 16], bc, k, None, op, waits=[t2])
            t = vcopy(bf, bd, [t])
            for c in range(2):
                a = tt(oh[c], bf[:, 16 * c:16 * c + 16].unsqueeze(2).to_broadcast([128, 16, 16]),
                       cc("iota").unsqueeze(1).to_broadcast([128, 16, 16]), ALU.is_equal, [t, t_cst])
                a = tt(oh[c], oh[c], tfl[:, c, :].unsqueeze(1).to_broadcast([128, 16, 16]), ALU.mult, [a])
                a = red(e1[:, 16 * c:16 * c + 16], oh[c], ALU.add, [a])
            a = stt(e1[:, 0:16], e1[:, 0:16], 128.0, e1[:, 16:32], ALU.mult, ALU.add, [a])
            tei[i, h] = vcopy(eidx[:, i, 16 * h:16 * h + 16], e1[:, 0:16], [a])
            g = gat[:, i, 16 * h:16 * h + 16]
            t = ts(g, bv, bv[:, 0:1], None, ALU.subtract, waits=[t2])
            t = act(g, g, ACT.Exp, [t], accum_out=hsm[:, 0:1])
            t = recip(hsm[:, 0:1], hsm[:, 0:1], [t])
            tga[i, h] = ts(g, g, hsm[:, 0:1], None, ALU.mult, waits=[t])

        t_nat = [natural(0), natural(1)]
        rows = Ring([Buf(m, Chan(sem(f"s_g{j}"))) for j, m in enumerate(more)]
                    + [Buf(n5s[:, 2048 * j:2048 * j + 2048], Chan(sem(f"s_g{2 + j}"))) for j in range(2)])
        for b in rows.bufs[2:4]:
            b.free = t_nat + [t_n5[-1]]

        def gather(table, i, k):
            s = rows.next()
            ix = eidx[:, i, k:k + 1]
            tok = G.dma(lambda e: e.indirect_dma_start(
                out=s.ap, out_offset=None, in_=D[table],
                in_offset=bass.IndirectOffsetOnAxis(ap=ix, axis=0)), s.chan, [tei[i, k // 16]] + s.free)
            return s, tok

        tco = {}
        last = {"acc": None, "read": []}

        def experts_in(i, h):
            for k in range(16 * h, 16 * h + 16):
                s, ld = gather("peer_u", i, k)
                a, x, ac = s.ap, xn[:, i, :], actv[:, i, k:k + 1]
                t = V(lambda e, a=a, x=x, ac=ac: e.tensor_tensor_reduce(
                    out=a, in0=a, in1=x, scale=1.0, scalar=0.0, op0=ALU.mult, op1=ALU.add, accum_out=ac),
                    [ld, txn[i]])
                s.free = [t]
            a = actv[:, i, 16 * h:16 * h + 16]
            tco[i, h] = act(a, a, ACT.Gelu_apprx_tanh, [t])

        def experts_out(i, h):
            a = actv[:, i, 16 * h:16 * h + 16]
            t = tt(a, a, gat[:, i, 16 * h:16 * h + 16], ALU.mult, [tco[i, h], tga[i, h]])
            for k in range(16 * h, 16 * h + 16):
                s, ld = gather("peer_v", i, k)
                c = actv[:, i, k:k + 1]
                if k == 0:
                    t = ts(acc, s.ap, c, None, ALU.mult, waits=[t, ld] + last["read"])
                else:
                    t = stt(acc, s.ap, c, acc, ALU.mult, ALU.add, [t, ld, last["acc"]])
                s.free = [t]
                last["acc"] = t

        def merge(i):
            for c in range(16):
                pt = PT.next()
                tok = tr(pt.ap[:, 0:128], acc[:, c * 128:(c + 1) * 128], [last["acc"]] + pt.free, True)
                x = XT[:, c, i * 128:(i + 1) * 128]
                xt[c] = tt(x, pt.ap[:, 0:128], x, ALU.add, [tok, xt[c]])
                pt.free = [xt[c]]
            last["read"] = [tok]

        for n in range(18):
            if n < 8:
                to_pq(2 * n)
                to_pq(2 * n + 1)
            if n < 16:
                score(n // 8, n % 8)
                select(n // 8, n % 8)
            if 1 <= n < 17:
                experts_in((n - 1) // 8, (n - 1) % 8)
            if n >= 2:
                experts_out((n - 2) // 8, (n - 2) % 8)
            if n == 9:
                merge(0)
        merge(1)
        fence()
        st.close()

        st = ExitStack()
        al = allocator(st)
        GB = Ring([Buf(al(S)) for _ in range(3)])
        NT = Ring([Buf(al(S)) for _ in range(6)])
        ppT = tiles(al(2 * S))
        pph = tiles(al(2 * S, f32r)), tiles(al(2 * S, f32r))
        fin = tiles(al(16 * S))
        ch_p, ch_o = Chan(sem("s_p")), Chan(sem("s_out"))
        t_pp = SP.dma(lambda e: e.dma_start(ppT, D["pT"].rearrange("(k p) t -> p k t", p=128)), ch_p,
                      [e.last() for e in (P, A, V)])
        n6 = rmsnorm(XT, "ple_norm_2", 16, xt, NT, pair=H)
        tph = [halves(pph[0][:, k, :], pph[1][:, k, :], ppT[:, k, :], [t_pp]) for k in range(2)]
        for n in range(16):
            g = GB.next()

            def f_pg(m, o, tok):
                g.free = [act(g.ap, o, ACT.Sigmoid, [tok] + g.free)]
                return g.free

            def f_pp(m, o, tok):
                t = tt(g.ap, o, g.ap, ALU.mult, [tok] + g.free)
                xt[m] = tt(XT[:, m, :], XT[:, m, :], g.ap, ALU.add, [t, xt[m]])
                g.free = [xt[m]]
                return [t]
            go(linT(two(D["w_ple_gate"], n), H, n6, n, f_pg))
            go(linT([D["w_ple_proj"][n]], pph, tph, n, f_pp))
        t_f = rmsnorm(XT, "final_norm_2", 16, xt, NT, dst=fin)
        for c in range(4):
            t = SP.dma(lambda e, c=c: e.dma_start(
                out[512 * c:512 * c + 512, :].rearrange("(k p) t -> p k t", p=128), fin[:, 4 * c:4 * c + 4, :]),
                ch_o, [t_f[4 * c + 3]])
        SP.wait([t])
        st.close()
        return listed, (P, A, V, G, SP)

    with base:
        listed, _ = walk(None, 0)
        _, (P, A, V, G, SP) = walk(listed, 1)
        block = base.enter_context(nc.Block())

        @block.sync
        def _(eng):
            SP.play(eng)

        @block.tensor
        def _(eng):
            P.play(eng)

        @block.scalar
        def _(eng):
            A.play(eng)

        @block.vector
        def _(eng):
            V.play(eng)

        @block.gpsimd
        def _(eng):
            G.play(eng)


def constants():
    import numpy as np
    import math
    f = np.float32
    p = np.arange(128)
    ident = np.eye(128, dtype=f)
    mask = np.where(np.arange(256)[None, :] <= 128 + p[:, None], 0.0, NEG).astype(f)
    half = 32
    inv = (1.0 / (np.float32(10000.0) ** (np.arange(half, dtype=f) / f(half)))).astype(f)
    ang = np.arange(256, dtype=f)[:, None] * inv[None, :]
    cos, sin = np.cos(ang).astype(f).T, np.sin(ang).astype(f).T
    cos4 = np.concatenate([cos] * 4, 0)
    sin4 = np.concatenate([-sin, sin, -sin, sin], 0)
    end = np.arange(15) * 16 + 31
    ok = np.stack([(end[None, :] <= (128 * i + p)[:, None]) for i in range(2)], 1).reshape(128, 30)
    iota = np.broadcast_to(np.arange(16, dtype=f), (128, 16))
    cst = np.concatenate([ident, ident[:, ::-1], mask, cos4, sin4, ok.astype(f), np.where(ok, 0.0, NEG).astype(f), iota], 1)
    dist = 255 - np.arange(384)
    n = np.maximum(dist, 0)
    nf = np.maximum(n, 1).astype(f)
    large = 16 + (np.log(nf / f(16)) / f(math.log(2048 / 16)) * f(16)).astype(np.int32)
    bucket = np.where(n < 16, n, np.minimum(large, 31))
    oneh = np.zeros((33, 4, 384), f)
    for v, (d, far) in enumerate(((1, 128), (4, 512), (16, 2048), (1, 10 ** 6))):
        good = (dist >= 0) & (dist % d == 0) & (dist <= far)
        oneh[bucket, v, np.arange(384)] = good
        oneh[32, v] = np.where(good, 0.0, NEG)
    return np.ascontiguousarray(cst.astype(f)), np.ascontiguousarray(oneh.reshape(33, 4 * 384))


def layout(inp):
    import numpy as np
    g = {k: np.asarray(v) for k, v in inp.items()}

    def tiles(w, c=128):
        k, n = w.shape
        return np.ascontiguousarray(w.reshape(k // 128, 128, n // c, c).transpose(2, 1, 0, 3)).reshape(
            n // c, 128, (k // 128) * c)

    def cols(v):
        v = v.reshape(-1, v.shape[-1])
        return v.reshape(v.shape[0], -1, 128).transpose(2, 0, 1).reshape(128, -1)

    d = {}
    x = g["x"][0]
    d["xT"] = np.ascontiguousarray(x.T)
    d["pT"] = np.ascontiguousarray(g["p_2"][0, 0].T)
    d["vec"] = np.ascontiguousarray(np.concatenate([cols(g[n]) for n, _ in VEC], 1))
    d["cst"], d["oneh"] = constants()
    d["relT"] = np.ascontiguousarray(np.concatenate(
        [g["rel_table"].T, np.ones((1, 32), np.float32)], 0))
    d["peT"] = np.ascontiguousarray(g["cmp_pe"][0].transpose(2, 0, 1)).reshape(64, 64)
    d["cw2"] = np.ascontiguousarray(g["cmp_w2"][0].transpose(1, 0, 2)).reshape(128, 128)
    d["cw1"] = np.ascontiguousarray(
        g["cmp_w1"][0].reshape(2, 4, 8, 64, 128).transpose(0, 1, 3, 2, 4)).reshape(2, 4, 64, 1024)
    w = g["w_in"][0]
    d["w_in"] = tiles(w[:, :4608])
    kv = w[:, 4608:5760].reshape(2048, 6, 3, 64)
    d["w_cmp"] = tiles(kv[:, 0:2].reshape(2048, 384))
    d["w_kdup"] = tiles(np.stack([kv[:, 2:5:2]] * 2, 3).reshape(2048, 768))
    d["w_vc"] = tiles(kv[:, 3:6:2].reshape(2048, 384))
    d["w_gate"] = tiles(w[:, 5760:], 36)[0]
    d["w_out"] = tiles(g["w_out"][0])
    d["w_up"] = tiles(g["w_up"][0])
    d["w_down"] = tiles(g["w_down"][0])
    w = g["w_in_2"][0]
    at = 0
    for name, n in (("w_cq", 768), ("w_ckv", 512), ("w_kr", 64), ("w_xr", 2048),
                       ("w_yr", 2048), ("w_ga", 2048), ("w_gr", 2048)):
        part = w[:, at:at + n]
        d[name] = tiles(np.concatenate([part, part], 1) if n == 64 else part, 128)
        at += n
    w = g["w_uq_2"][0].reshape(768, 16, 192)
    d["w_qn"] = tiles(np.ascontiguousarray(w[:, :, :128]).reshape(768, 2048))
    d["w_qp"] = tiles(np.ascontiguousarray(w[:, :, 128:]).reshape(768, 1024))
    w = g["w_ukv_2"][0].reshape(512, 16, 256)
    d["w_kn"] = tiles(np.ascontiguousarray(w[:, :, :128]).reshape(512, 2048))
    d["w_v"] = tiles(np.ascontiguousarray(w[:, :, 128:]).reshape(512, 2048), 256)
    d["w_rg"] = np.ascontiguousarray(np.concatenate([g["w_rg_a_2"][0], g["w_rg_x_2"][0]], 2))
    for name in ("w_attn_o", "w_rnn_o", "w_out", "w_peer_q", "w_ple_gate", "w_ple_proj"):
        d[name + ("_2" if name == "w_out" else "")] = tiles(g[name + "_2"][0])
    d["subkeys"] = np.ascontiguousarray(
        g["peer_subkeys_2"][0].reshape(16, 128, 128).transpose(2, 0, 1)).reshape(128, 2048)
    d["peer_u"] = g["peer_u_2"][0]
    d["peer_v"] = g["peer_v_2"][0]
    return d


def kernel(**inputs):
    import numpy as np
    import concourse.bacc as bacc
    from concourse.bass_utils import run_bass_kernel_spmd as run

    nc = bacc.Bacc("TRN2", target_bir_lowering=False, num_devices=1)
    arrays = {f"in_{k}": np.ascontiguousarray(v) for k, v in layout(inputs).items()}
    D = {k[3:]: nc.dram_tensor(k, v.shape, mybir.dt.from_np(v.dtype), kind="ExternalInput").ap()
         for k, v in arrays.items()}
    D["toe"] = nc.dram_tensor("toe_scratch", (32, 384), mybir.dt.float32).ap()
    out = nc.dram_tensor("out_0", (2048, S), mybir.dt.float32, kind="ExternalOutput").ap()
    program(nc, D, out)
    r = run(nc, [arrays], core_ids=[0])
    return np.ascontiguousarray(r.results[0]["out_0"].T)[None]
```

```python
import concourse.bass as bass
from concourse import mybir
from contextlib import ExitStack

S = 256
NRAW = 5
NSPL = 4
COLS = 1024
UD = 1536
NEG = -1e30
LOW = -3.0e38

VEC = [("norm_attn", 16), ("norm_mlp", 16), ("norm_final", 16), ("attn_norm_2", 16), ("q_norm_2", 6),
       ("kv_norm_2", 4), ("ffn_norm_2", 16), ("ple_norm_2", 16), ("final_norm_2", 16), ("conv_w", 264),
       ("conv_b", 88), ("conv_w_2", 64), ("conv_b_2", 16), ("b_rg_a_2", 16), ("b_rg_x_2", 16),
       ("lru_lambda_2", 16), ("b_gate_2", 32)]
CST = [("ident", 128), ("exch", 128), ("mask", 256), ("cos", 256), ("sin", 256), ("cmp01", 30), ("cmpneg", 30), ("iota", 16), ("row", 2)]


def offsets(table):
    at, out = 0, {}
    for name, n in table:
        out[name] = (at, at + n)
        at += n
    return out, at


VOFF, NVEC = offsets(VEC)
COFF, NCST = offsets(CST)


class Engine:

    def __init__(self, sem):
        self.sem, self.q, self.n, self.seen = sem, [], 0, {}

    def __call__(self, fn, waits=(), sig=True):
        self.q.append((self.fresh(waits), fn, (self.sem, 1) if sig else None))
        self.n += 1 if sig else 0
        return (self.sem, self.n) if sig else None

    def dma(self, fn, chan, waits=()):
        chan.n += 16
        self.q.append((self.fresh(waits), fn, (chan.sem, 16)))
        return (chan.sem, chan.n)

    def wait(self, waits):
        self.q.append((self.fresh(waits), None, None))

    def fresh(self, waits):
        out = []
        for t in waits:
            if t is not None and self.seen.get(id(t[0]), 0) < t[1]:
                self.seen[id(t[0])] = t[1]
                out.append(t)
        return out

    def last(self):
        return (self.sem, self.n) if self.n else None

    def play(self, eng):
        for waits, fn, inc in self.q:
            for sem, val in waits:
                eng.wait_ge(sem, val)
            if fn is not None:
                ins = fn(eng)
                if inc is not None:
                    ins.then_inc(*inc)


class Chan:

    def __init__(self, sem):
        self.sem, self.n = sem, 0


class Buf:

    def __init__(self, ap, chan=None):
        self.ap, self.chan, self.free, self.busy = ap, chan, [], False


class Ring:
    def __init__(self, bufs):
        self.bufs, self.i = bufs, 0

    def next(self):
        b = self.bufs[self.i % len(self.bufs)]
        self.i += 1
        return b


def program(nc, D, out):
    fp32, f32r = mybir.dt.float32, mybir.dt.float32r
    u32, i32 = mybir.dt.uint32, mybir.dt.int32
    ALU, ACT, AX = mybir.AluOpType, mybir.ActivationFunctionType, mybir.AxisListType.X
    base = ExitStack()

    def keep(name, cols, dt=fp32):
        return base.enter_context(nc.sbuf_tensor(name, [128, cols], dt))

    def tiled(t):
        return t[:, :].rearrange("p (k t) -> p k t", t=S)

    XT = tiled(keep("XT", 16 * S))
    HH, HL = tiled(keep("HH", 16 * S, f32r)), tiled(keep("HL", 16 * S, f32r))
    raw_sb = keep("raw", NRAW * COLS)
    sph, spl = keep("sph", NSPL * COLS, f32r), keep("spl", NSPL * COLS, f32r)
    vec, cst, ones, nrm, sqs = (
        keep("vec", NVEC), keep("cst", NCST), keep("ones", 128), keep("nrm", 2 * S), keep("sqs", 2 * S))
    banks = [base.enter_context(nc.psum_tensor(f"ps{i}", [128, 512], fp32)) for i in range(8)]
    sems = {}

    def sem(name):
        if name not in sems:
            sems[name] = base.enter_context(nc.semaphore(name))
        return sems[name]

    def walk(plan, run):
        P, A, V, G, SP = (Engine(sem(f"s_{n}")) for n in ("pe", "act", "dve", "pool", "sp"))
        raw = Ring([Buf(raw_sb[:, i * COLS:(i + 1) * COLS], Chan(sem(f"s_w{i}"))) for i in range(NRAW)])
        spr = Ring([Buf((sph[:, i * COLS:(i + 1) * COLS], spl[:, i * COLS:(i + 1) * COLS]))
                    for i in range(NSPL)])
        bank = [Buf(b[:, :]) for b in banks]
        PP, PS, PT, PO = Ring(bank[0:2]), Ring(bank[2:4]), Ring(bank[4:6]), Ring(bank[6:8])
        SQ = Ring([Buf(sqs[:, i * S:(i + 1) * S]) for i in range(2)])
        names = [0]

        def share(pp, sc, pt):
            for ring, a, b in ((PP, 0, pp), (PS, pp, pp + sc), (PT, pp + sc, pp + sc + pt), (PO, pp + sc + pt, 8)):
                ring.bufs, ring.i = bank[a:b], 0

        def vcol(name, i=0, n=1):
            a = VOFF[name][0] + i
            return vec[:, a:a + n]

        def cc(name):
            a, b = COFF[name]
            return cst[:, a:b]

        def allocator(stack):
            def alloc(cols, dt=fp32):
                names[0] += 1
                t = stack.enter_context(nc.sbuf_tensor(f"t{run}_{names[0]}", [128, cols], dt))
                return t[:, :]
            return alloc

        def tiles(ap):
            return ap.rearrange("p (k t) -> p k t", t=S)

        def fence():
            ends = [e.last() for e in (P, A, V, G)]
            for e in (P, A, V, G):
                e.wait(ends)
            return ends

        def mm(o, l, r, start, stop, waits=(), sig=False):
            return P(lambda e: e.matmul(o, lhsT=l, rhs=r, start=start, stop=stop), waits, sig)

        def tr(o, i, waits=(), sig=False):
            idn = cc("ident")
            return P(lambda e: e.transpose(o, i, idn), waits, sig)

        def act(o, i, f, waits=(), **kw):
            return A(lambda e: e.activation(o, i, f, **kw), waits)

        def tt(o, a, b, op, waits=()):
            return V(lambda e: e.tensor_tensor(o, a, b, op), waits)

        def ts(o, a, s1, s2, op0, op1=None, waits=()):
            if op1 is None:
                return V(lambda e: e.tensor_scalar(o, a, s1, None, op0), waits)
            return V(lambda e: e.tensor_scalar(o, a, s1, s2, op0, op1), waits)

        def stt(o, a, s, b, op0, op1, waits=()):
            return V(lambda e: e.scalar_tensor_tensor(out=o, in0=a, scalar=s, in1=b, op0=op0, op1=op1), waits)

        def red(o, i, op, waits=(), **kw):
            return V(lambda e: e.tensor_reduce(o, i, AX, op, **kw), waits)

        def recip(o, i, waits=()):
            return V(lambda e: e.reciprocal(o, i), waits)

        def vcopy(o, i, waits=()):
            return V(lambda e: e.tensor_copy(o, i), waits)

        def vset(o, v, waits=()):
            return V(lambda e: e.memset(o, v), waits)

        flip = [0]

        def copy(o, i, waits):
            flip[0] ^= 1
            if flip[0]:
                return act(o, i, ACT.Copy, waits)
            return vcopy(o, i, waits)

        def halves(hi, lo, src, waits, pool=False):
            t = act(hi, src, ACT.Copy, waits)
            if pool:
                return G(lambda e: e.tensor_tensor(lo, src, hi.bitcast(fp32), ALU.subtract), [t])
            return tt(lo, src, hi.bitcast(fp32), ALU.subtract, [t])

        listed, ready = [], []
        at = {"use": 0, "dma": 0, "split": 0}

        def pump():
            if plan is None:
                return
            moved = True
            while moved:
                moved = False
                if at["dma"] < len(plan):
                    r = raw.bufs[at["dma"] % NRAW]
                    if not r.busy:
                        src, view, after, cut = plan[at["dma"]]
                        dst = view(r.ap)
                        tok = SP.dma(lambda e, d=dst, s=src: e.dma_start(d, s), r.chan, r.free + after)
                        r.busy = True
                        ready.append((r, tok))
                        at["dma"] += 1
                        moved = True
                if at["split"] < at["dma"]:
                    r, tok = ready[at["split"]]
                    cut = plan[at["split"]][3]
                    if not cut:
                        at["split"] += 1
                        moved = True
                    elif not spr.bufs[spr.i % NSPL].busy:
                        b = spr.next()
                        b.busy = True
                        n = plan[at["split"]][0].free_size()
                        t = halves(b.ap[0][:, 0:n], b.ap[1][:, 0:n], r.ap[:, 0:n], [tok] + b.free, cut == 2)
                        r.free, r.busy = [t], False
                        ready[at["split"]] = (b, t)
                        at["split"] += 1
                        moved = True

        def piece(src, cut=True, view=None, after=()):
            n = src.free_size()
            parts = src.shape[0]
            listed.append((src, view or (lambda ap: ap[0:parts, 0:n]), list(after), cut))
            if plan is None:
                return (spr.bufs[0] if cut else raw.bufs[0]), None
            if at["split"] <= at["use"]:
                pump()
            got = ready[at["use"]]
            at["use"] += 1
            return got

        def done(buf, tok):
            pump()
            buf.free, buf.busy = [tok], False

        THREE = ((0, 0), (0, 1), (1, 0))

        def go(gen):
            for _ in gen:
                pass

        def linT(srcs, rhs, rhs_toks, n, evac, ks=None):
            ps = PP.next()
            o = ps.ap[:, 0:S]
            kt = sum(s.free_size() // 128 for s in srcs)
            ks = ks or range(kt)
            k = 0
            for src in srcs:
                b, ld = piece(src)
                for j in range(src.free_size() // 128):
                    last = j == src.free_size() // 128 - 1
                    for a, c in THREE:
                        end = last and (a, c) == THREE[-1]
                        tok = mm(o, b.ap[a][:, j * 128:(j + 1) * 128], rhs[c][:, ks[k], :], k == 0 and a + c == 0,
                                 k == kt - 1 and (a, c) == THREE[-1],
                                 [ld, rhs_toks[ks[k]]] + (ps.free if k == 0 else []), end)
                    k += 1
                done(b, tok)
                if k == kt:
                    ps.free = evac(n, o, tok)
                yield

        def linN(srcs, lhs, lhs_toks, cols, evac, pool=()):
            pss = [PP.next(), PP.next()]
            kt = sum(s.free_size() // cols for s in srcs)
            k0 = 0
            for n, src in enumerate(srcs):
                b, ld = piece(src, 2 if n in pool else True)
                nk = src.free_size() // cols
                for i in range(2):
                    ps = pss[i]
                    for j in range(nk):
                        k = k0 + j
                        for a, c in THREE:
                            tok = mm(ps.ap[:, 0:cols], lhs[c][:, k, i * 128:(i + 1) * 128],
                                     b.ap[a][:, j * cols:(j + 1) * cols], k == 0 and a + c == 0,
                                     k == kt - 1 and (a, c) == THREE[-1],
                                     [ld, lhs_toks[k]] + (ps.free if k == 0 else []),
                                     j == nk - 1 and (a, c) == THREE[-1])
                    if k0 + nk == kt:
                        ps.free = evac(i, ps.ap[:, 0:cols], tok)
                k0 += nk
                done(b, tok)
                yield

        def two(w, n):
            h = w.shape[2] // 2
            return [w[n, :, 0:h], w[n, :, h:2 * h]]

        class Squares:

            def __init__(self, src, nkt, ring=None):
                self.src, self.nkt, self.k, self.ps, self.tok = src, nkt, 0, PS.next(), None
                self.ring = ring or SQ

            def add(self, tok):
                b, k = self.ring.next(), self.k
                t = act(b.ap, self.src[:, k, :], ACT.Square, [tok] + b.free)
                self.tok = mm(self.ps.ap[:, 0:S], ones[:, :], b.ap, k == 0, k == self.nkt - 1,
                              [t, t_ones] + (self.ps.free if k == 0 else []), True)
                b.free = [self.tok]
                self.k += 1

        def rmsnorm(src, gain, nkt, toks, NT, pair=None, dst=None, after=(), first=0, sums=None, then=None):
            sums = sums or Squares(src, nkt, NT)
            for k in range(sums.k, nkt):
                sums.add(toks[k])
            ps, t = sums.ps, sums.tok
            dev, inv = (nrm[:, i * S:(i + 1) * S] for i in range(2))
            t = ts(dev, ps.ap[:, 0:S], 1.0 / (nkt * 128), 1e-6, ALU.mult, ALU.add, [t])
            ps.free = [t]
            t = act(dev, dev, ACT.Sqrt, [t])
            t = recip(inv, dev, [t])
            out_t, wait = [None] * nkt, []

            def second_half():
                k, o, b, th = wait.pop(0)
                out_t[k] = tt(pair[1][:, k, :], o, pair[0][:, k, :].bitcast(fp32), ALU.subtract, [th])
                if b is not None:
                    b.free = [out_t[k]]
            for k in range(nkt):
                b, free = None, []
                if dst is not None and k >= first:
                    o = dst[:, k - first, :]
                else:
                    b = NT.next()
                    o, free = b.ap, b.free
                out_t[k] = stt(o, src[:, k, :], vcol(gain, k), inv, ALU.mult, ALU.mult, [t, toks[k], t_vec] + free)
                if pair is not None:
                    wait.append((k, o, b, act(pair[0][:, k, :], o, ACT.Copy, [out_t[k]] + list(after))))
                    if len(wait) > 2:
                        second_half()
                if then is not None:
                    then.add(out_t[k])
            while wait:
                second_half()
            return out_t

        def residual(n, o, tok):
            xt[n] = tt(XT[:, n, :], o, XT[:, n, :], ALU.add, [tok, xt[n]])
            return [xt[n]]

        def smalls(tile, n):
            return Ring([Buf(tile[:, 8 * i:8 * i + 8]) for i in range(n)])

        def softmax(job, SB, small):
            nk = (job["i"] + 1) * 128
            c = small.next()
            parts, scale = job["parts"], job.get("scale", 1.0)
            for n, u in enumerate(parts):
                ps = PS.next()
                for j, (l, r) in enumerate(u["qk"]):
                    tok = mm(ps.ap[:, 0:nk], l, r, j == 0, j == len(u["qk"]) - 1,
                             u["toks"] + (ps.free if j == 0 else []), j == len(u["qk"]) - 1)
                b = u["buf"] = SB.next()
                o, i0, i1, ac = b.ap[:, 0:nk], ps.ap[:, 0:nk], u["bias"], c.ap[:, n:n + 1]
                t = V(lambda e, o=o, i0=i0, i1=i1, ac=ac: e.tensor_tensor_reduce(
                    out=o, in0=i0, in1=i1, scale=1.0, scalar=LOW, op0=ALU.add, op1=ALU.max, accum_out=ac),
                    [tok] + u["btoks"] + b.free + c.free)
                ps.free = [t]
            if len(parts) == 1:
                t = ts(c.ap[:, 3:4], c.ap[:, 0:1], -scale, None, ALU.mult, waits=[t])
            else:
                t = red(c.ap[:, 3:4], c.ap[:, 0:len(parts)], ALU.max, [t], negate=True)
            for n, u in enumerate(parts):
                o = u["buf"].ap[:, 0:nk]
                t2 = act(o, o, ACT.Exp, [t], bias=c.ap[:, 3:4], scale=scale, accum_out=c.ap[:, 4 + n:5 + n])
            if len(parts) > 1:
                t2 = red(c.ap[:, 7:8], c.ap[:, 4:4 + len(parts)], ALU.add, [t2])
                t2 = recip(c.ap[:, 7:8], c.ap[:, 7:8], [t2])
            else:
                t2 = recip(c.ap[:, 7:8], c.ap[:, 4:5], [t2])
            for u in parts:
                o = u["buf"].ap[:, 0:nk]
                if job.get("gate") is not None:
                    u["p"] = ts(o, o, c.ap[:, 7:8], job["gate"], ALU.mult, ALU.mult, [t2] + job["gtoks"])
                else:
                    u["p"] = ts(o, o, c.ap[:, 7:8], None, ALU.mult, waits=[t2])
            c.free = [u["p"]]

        def transposed(job, PB):
            i = job["i"]
            for u in job["parts"]:
                pt = PT.next()
                for b in range(i + 1):
                    tok = tr(pt.ap[:, b * 128:(b + 1) * 128], u["buf"].ap[:, b * 128:(b + 1) * 128],
                             [u["p"]] + pt.free, b == i)
                u["buf"].free = [tok]
                pb = u["pb"] = PB.next()
                u["pT"] = copy(pb.ap[:, 0:(i + 1) * 128], pt.ap[:, 0:(i + 1) * 128], [tok] + pb.free)
                pt.free = [u["pT"]]

        def attend(job):
            i = job["i"]
            for u in job["parts"]:
                pb, o = u["pb"], u["out"]
                for b in range(i + 1):
                    tok = mm(o, u["v"](b), pb.ap[:, b * 128:(b + 1) * 128], u["start"] and b == 0,
                             u["stop"] and b == i, [u["pT"]] + u["vtoks"] + u["ofree"], b == i)
                pb.free = [tok]
            if job.get("done"):
                job["done"](tok)

        def weave(jobs, front, back, PB, fillers, lag=2):
            todo = [list(f) + [0, None][len(f) - 2:] for f in fillers]
            steps = len(jobs) + lag + 1
            now = [None]

            def advance(n, most, due):
                while most > 0 and (todo or now[0]):
                    if now[0] is None:
                        free = [f for f in todo if f[2] <= n]
                        if not free:
                            return
                        soon = [f for f in free if f[3] is not None]
                        now[0] = soon[0] if soon and (due or soon[0][3] <= n + 8) else free[0]
                        todo.remove(now[0])
                    if next(now[0][0], True):
                        now[0] = None
                    else:
                        now[0][1] -= 1
                        most -= 1
            for n in range(steps):
                if n > lag:
                    back(jobs[n - lag - 1])
                if lag <= n < len(jobs) + lag:
                    transposed(jobs[n - lag], PB)
                if n < len(jobs):
                    while any(f[3] is not None and f[3] <= n for f in todo + [now[0]] * (now[0] is not None)):
                        advance(n, 1, True)
                    front(jobs[n])
                left = sum(f[1] for f in todo) + (now[0][1] if now[0] else 0)
                advance(n, -(-left // (steps - n)), False)
            while todo or now[0]:
                advance(steps, 1, False)

        ch_c, ch_v, ch_b, ch_t, *ch_x = (Chan(sem(f"s_{n}")) for n in ("c", "v", "b", "t", "x0", "x1", "x2", "x3"))
        xt = []
        for c, ch in enumerate(ch_x):
            xt += [SP.dma(lambda e, c=c: e.dma_start(
                XT[:, 4 * c:4 * c + 4, :], D["xT"][512 * c:512 * c + 512].rearrange("(k p) t -> p k t", p=128)), ch)] * 4
        t_cst = SP.dma(lambda e: e.dma_start(cst[:, :], D["cst"]), ch_c)
        t_vec = SP.dma(lambda e: e.dma_start(vec[:, :], D["vec"]), ch_v)
        t_ones = vset(ones[:, :], 1.0)
        H = (HH, HL)

        st = ExitStack()
        al = allocator(st)
        share(2, 1, 2)
        qT, kT = tiles(al(12 * S)), tiles(al(12 * S))
        vN = al(2 * 1280).rearrange("p (i c) -> p i c", i=2)
        gts = al(72).rearrange("p (i c) -> p i c", i=2)
        bias = tiles(al(24 * S))
        ots = al(16 * S)
        oT = tiles(ots)
        SB = Ring([Buf(al(S)) for _ in range(7)])
        PB = Ring([Buf(al(S)) for _ in range(3)])
        NT = Ring(PB.bufs + SB.bufs[0:2])
        small = smalls(al(64), 8)
        peT = al(64).rearrange("p (b l) -> p b l", b=2)
        hid = al(45)
        hidR = al(3 * 128).rearrange("p (k g n) -> p k g n", k=3, g=4)
        kcT = al(45)
        vcR = al(3 * 64).rearrange("p (k d) -> p k d", k=3)
        w2 = al(128).rearrange("p (b d) -> p b d", b=2)
        pcs = al(1536)
        Pc = pcs[:, 0:768].rearrange("p (i h n) -> p i h n", i=2, h=12)
        PcT = pcs[:, 768:1536].rearrange("p (k i t) -> p k i t", k=3, i=2)
        csm = al(64)
        relT = al(32)
        oneh = ots[:, 0:1536].rearrange("p (v j) -> p v j", v=4)
        toe = pcs.rearrange("p (v j) -> p v j", v=4)
        tpe = ots[:, 1536:1536 + 1440].rearrange("p (l k n) -> p l k n", l=32, k=3)
        kst = ots[:, 3072:3072 + S]

        SP.dma(lambda e: e.dma_start(oneh[0:33], D["oneh"].rearrange("b (v j) -> b v j", v=4)), ch_b)
        SP.dma(lambda e: e.dma_start(relT[0:33, :], D["relT"]), ch_b)
        SP.dma(lambda e: e.dma_start(peT[0:64], D["peT"].rearrange("d (b l) -> d b l", b=2)), ch_b)
        t_b = SP.dma(lambda e: e.dma_start(w2[:, :, :], D["cw2"].rearrange("p (b d) -> p b d", b=2)), ch_b)
        for v, (a, b) in enumerate([(0, 4), (4, 8), (8, 12), (12, 32)]):
            ps = PP.next()
            tok = mm(ps.ap[0:b - a, 0:384], relT[0:33, a:b], oneh[0:33, v, :], True, True, [t_b] + ps.free, True)
            t = vcopy(toe[0:b - a, v, :], ps.ap[0:b - a, 0:384], [tok])
            ps.free = [t]
            td = SP.dma(lambda e, v=v, a=a, b=b: e.dma_start(D["toe"][a:b, :], toe[0:b - a, v, :]), ch_t, [t])
        tb = [None] * 24

        def make_bias(head, slot, after=()):
            src = bass.AP(D["toe"].tensor, head * 384, [[1, 128], [384, 4], [1, 256]])
            s, ld = piece(src, False, lambda ap: ap.rearrange("p (h t) -> p h t", h=4), [td])
            for c in range(2):
                ps = PP.next()
                tok = mm(ps.ap, cc("exch"), s.ap[:, 512 * c:512 * c + 512], True, True,
                         [ld, t_cst] + ps.free, True)
                h = slot + 2 * c
                t = copy(bias[:, h:h + 2, :].rearrange("p h t -> p (h t)"), ps.ap, [tok] + list(after))
                tb[h] = tb[h + 1] = t
                ps.free = [t]
            done(s, tok)
            yield

        ht = rmsnorm(XT, "norm_attn", 16, xt, NT, pair=H)
        tq, tk, tv = [None] * 12, [None] * 12, {}

        def to_q(n, slot, after=()):
            def f(_, o, tok):
                tq[slot] = act(qT[:, slot, :], o, ACT.Copy, [tok] + list(after), scale=0.125)
                return [tq[slot]]
            return linT(two(D["w_in"], n), H, ht, 0, f)

        def to_k(w, n, slot, after=()):
            def f(_, o, tok):
                tk[slot] = vcopy(kT[:, slot, :], o, [tok] + list(after))
                return [tk[slot]]
            return linT(two(w, n), H, ht, 0, f)

        def to_v(n, at, after=()):
            def f(i, o, tok):
                tv[at, i] = tv[at + 128, i] = copy(vN[:, i, at:at + 256], o, [tok] + list(after))
                return [tv[at, i]]
            return linN([D["w_v1"][n, :, j:j + COLS] for j in range(0, 4096, COLS)], H, ht, 256, f)

        for j in range(6):
            go(to_q(30 + j, j))
        unit_t = {}
        tpe_free, hid_free, kst_free = [], [], []
        cmp_t = {}

        def window(what, src, tok):
            kind, kv = what // 3, what % 3
            v = src.rearrange("p (n r) -> p r n", r=16)
            for a in range(2):
                pe = peT[0:64, kind, 16 * a:16 * a + 16].unsqueeze(2).to_broadcast([64, 16, 15])
                t = tt(tpe[0:64, 16 * a:16 * a + 16, kv, :], v[:, :, a:a + 15], pe, ALU.add, [tok, t_b] + tpe_free)
            unit_t[what] = t
            return t

        def compress(br):
            ps = PP.next()
            for p in range(4):
                s, ld = piece(D["cw1"][br, p], False)
                for l in range(8):
                    tok = mm(ps.ap[:, 0:45], s.ap[0:64, l * 128:(l + 1) * 128],
                             tpe[0:64, 8 * p + l].rearrange("p k n -> p (k n)"), p + l == 0, p == 3 and l == 7,
                             [ld] + [unit_t[3 * br + kv] for kv in range(3)] + (ps.free if p + l == 0 else []),
                             l == 7)
                done(s, tok)
            tpe_free[:] = [tok]
            t = act(hid[:, :], ps.ap[:, 0:45], ACT.Gelu_apprx_tanh, [tok] + hid_free)
            ps.free = [t]
            po = PP.next()
            if br == 0:
                for b in (0, 64):
                    tok = mm(po.ap[b:b + 64, 0:45], w2[:, 0, :], hid[:, :], True, True, [t, t_b] + po.free, True)
                hid_free[:] = [tok]
                cmp_t["k"] = vcopy(kcT[:, :], po.ap[:, 0:45], [tok])
                po.free = [cmp_t["k"]]
            else:
                t0 = vset(hidR[:, :, :, :], 0.0)
                h3 = hid.rearrange("p (k n) -> p k n", k=3)
                for g in range(4):
                    t1 = vcopy(hidR[:, :, g, 0:15], h3, [t, t0])
                for kv in range(3):
                    tok = mm(po.ap[:, 64 * kv:64 * kv + 64], hidR[:, kv, :, :].rearrange("p g n -> p (g n)"),
                             w2[:, 1, :], True, True, [t1, t_b] + po.free, kv == 2)
                cmp_t["v"] = vcopy(vcR[:, :, :].rearrange("p k d -> p (k d)"), po.ap[:, 0:192], [tok])
                po.free = [cmp_t["v"]]

        for n in range(3):
            def f_kv(n, o, tok):
                t = window(2 * n, o[0:64, :], tok)
                t2 = act(kst[0:64, :], o[64:128, :], ACT.Copy, [t] + kst_free)
                if n == 1:
                    late.append(t2)
                else:
                    kst_free[:] = [window(2 * n + 1, kst[0:64, :], t2)]
                return [t2]
            late = []
            go(linT(two(D["w_cmp"], n), H, ht, n, f_kv))
            if n == 1:
                compress(0)
                kst_free[:] = [window(3, kst[0:64, :], late[0])]
        for q in range(3):
            go(make_bias(20 + 4 * q, 4 * q))
        for j in range(6):
            go(to_k(D["w_kdup"], j, j))
        compress(1)
        tg = [None, None]

        def f_vg(i, o, tok):
            t = act(vN[:, i, 0:384], o[:, 0:384], ACT.Copy, [tok])
            for at in (0, 128, 256):
                tv[at, i] = t
            tg[i] = act(gts[:, i, 0:36], o[:, 384:420], ACT.Sigmoid, [tok])
            return [tg[i]]
        go(linN([D["w_vcg"][0, :, j:j + 840] for j in range(0, 6720, 840)], H, ht, 420, f_vg))

        t_pz = vset(Pc[:, :, :, :], 0.0, [td])

        def compressed(i):
            pc = Pc[:, i, :, 0:15]
            ng = cc("cmpneg")[:, 15 * i:15 * i + 15].unsqueeze(1).to_broadcast([128, 6, 15])
            ok = cc("cmp01")[:, 15 * i:15 * i + 15].unsqueeze(1).to_broadcast([128, 12, 15])
            for odd in range(2):
                ps = PP.next()
                sc = ps.ap[:, 0:192].rearrange("p (h n) -> p h n", h=6)[:, :, 0:15]
                for m in range(6):
                    b, h = 64 * odd, 2 * m + odd
                    tok = mm(ps.ap[:, 32 * m:32 * m + 15], qT[b:b + 64, m, i * 128:(i + 1) * 128],
                             kcT[b:b + 64, 15 * (h // 4):15 * (h // 4) + 15], True, True,
                             [tq[m], cmp_t["k"]] + ps.free, m == 5)
                t = tt(pc[:, odd:12:2, :], sc, ng, ALU.add, [tok, t_cst, t_pz])
                ps.free = [t]
            mx, dn = csm[:, 24 * i:24 * i + 12], csm[:, 24 * i + 12:24 * i + 24]
            t = red(mx, pc, ALU.max, [t])
            t = tt(pc, pc, mx.unsqueeze(2).to_broadcast([128, 12, 15]), ALU.subtract, [t])
            t = act(pc, pc, ACT.Exp, [t])
            t = tt(pc, pc, ok, ALU.mult, [t])
            t = red(dn, pc, ALU.add, [t])
            t = ts(dn, dn, 1e-30, None, ALU.max, waits=[t])
            t = recip(dn, dn, [t])
            t = tt(dn, dn, gts[:, i, 0:36].rearrange("p (h b) -> p h b", b=3)[:, :, 0], ALU.mult, [t, tg[i]])
            return tt(pc, pc, dn.unsqueeze(2).to_broadcast([128, 12, 15]), ALU.mult, [t])

        def compressed_T(i, t):
            pt = PT.next()
            for kv in range(3):
                tok = tr(pt.ap[:, kv * 128:(kv + 1) * 128],
                         Pc[:, i, 4 * kv:4 * kv + 4, :].rearrange("p h n -> p (h n)"), [t, t_cst] + pt.free, kv == 2)
            t = vcopy(PcT[:, :, i, :], pt.ap[:, 0:384].rearrange("p (k t) -> p k t", k=3), [tok])
            pt.free = [t]
            return t

        tcp = [compressed(0), compressed(1)]
        for j in range(2):
            go(to_q(j, 6 + j))
        t_pct = [compressed_T(i, tcp[i]) for i in range(2)]
        ot = [None] * 16

        def front(job):
            i, nk = job["i"], (job["i"] + 1) * 128
            parts = []
            for q, k, base, bi, at, n in job["parts"]:
                a = at // 128 * 128
                parts.append({
                    "qk": [(qT[base:base + 64, q, i * 128:(i + 1) * 128], kT[base:base + 64, k, 0:nk])],
                    "toks": [tq[q], tk[k]], "bias": bias[:, bi, 128 - 128 * i:S], "btoks": [tb[bi]],
                    "v": lambda b, at=at: vN[:, b, at:at + 64], "vtoks": [tv[a, 0], tv[a, 1]],
                    "out": job["ps"][n].ap[base:base + 64, i * 128:(i + 1) * 128], "start": True, "stop": True})
            job["parts"] = parts
            softmax(job, SB, small)

        def back(job):
            i = job["i"]
            for n, u in enumerate(job["parts"]):
                u["ofree"] = job["ps"][n].free
            if "c" in job:
                h, br = job["c"]
                u = job["parts"][0]
                if br == 0:
                    g = h % 4
                    mm(u["out"], vcR[32 * g:32 * g + 32, h // 4, :], PcT[32 * g:32 * g + 32, h // 4, i, :],
                       True, False, [t_pct[i], cmp_t["v"]] + u["ofree"])
                    u["start"], u["stop"] = False, False
                else:
                    u["start"] = False

            def finish(tok):
                for n, tile in enumerate(job["tiles"]):
                    ot[tile] = copy(oT[:, tile, :], job["ps"][n].ap[:, 0:S], [tok])
                    job["ps"][n].free = [ot[tile]]
                    if job.get("split"):
                        job["split"](tile)
            if job.get("last"):
                job["done"] = finish
            attend(job)

        jobs = []
        for hp in range(6):
            ps = [PO.next()]
            for h in (2 * hp, 2 * hp + 1):
                kv = h // 4
                for i in range(2):
                    for br in range(2):
                        jobs.append({"i": i, "ps": ps, "tiles": [10 + hp], "c": (h, br),
                                     "gate": gts[:, i, 3 * h + 1 + br:3 * h + 2 + br], "gtoks": [tg[i]],
                                     "parts": [(hp, 3 * br + kv, 64 * (h % 2), h, 192 * br + 64 * kv, 0)]})
            jobs[-1]["last"] = True
        todo = []
        for g in range(3):
            for j in range(2):
                if g:
                    todo.append((to_q(6 * g + j, 6 + 2 * g + j), 2))
                todo.append((to_k(D["w_in"], 6 * g + 2 + j, 6 + 2 * g + j), 2))
            todo.append((to_v(g, 512 + g * 256), 4))
            todo.append((make_bias(4 * g, 12 + 4 * g), 1))
        weave(jobs, front, back, PB, todo, 3)
        jobs = []
        for jp in range(2):
            ps = [PO.next() for _ in range(3)]
            for j in (2 * jp, 2 * jp + 1):
                for i in range(2):
                    jobs.append({"i": i, "ps": ps, "tiles": [2 * g + jp for g in range(3)], "parts": [
                        (6 + 2 * g + jp, 6 + 2 * g + jp, 64 * (j % 2), 12 + 4 * g + j, 512 + g * 256 + 64 * j, g)
                        for g in range(3)]})
            jobs[-1]["last"] = True
        room = [P.last(), V.last()]
        todo = [(make_bias(12 + 4 * q, 4 * q, room), 1) for q in range(2)]
        for j in range(4):
            todo.append((to_q(18 + j, j, room), 2))
            todo.append((to_k(D["w_in"], 22 + j, j, room), 2))
            if j % 2:
                todo.append((to_v(3 + j // 2, 128 * (j - 1), room), 4))
        weave(jobs, front, back, PB, todo, 1)
        h_read = [P.last()]
        os_ = [None] * 16

        def split_o(tile):
            os_[tile] = halves(HH[:, tile, :], HL[:, tile, :], oT[:, tile, :], [ot[tile]] + h_read)
        jobs = []
        for hp in range(4):
            ps = [PO.next()]
            for h in (2 * hp, 2 * hp + 1):
                for i in range(2):
                    jobs.append({"i": i, "ps": ps, "tiles": [6 + hp], "split": split_o,
                                 "parts": [(hp, hp, 64 * (h % 2), h, 64 * h, 0)]})
            jobs[-1]["last"] = True
        early = (0, 1, 2, 3, 4, 5, 10, 11, 12, 13, 14, 15)
        for n in early:
            split_o(n)
        todo = [(linT([D["w_out"][n, :, 0:768], D["w_out"][n, :, 1280:2048]], H, os_, n, residual, early), 2)
                for n in range(16)]
        weave(jobs, front, back, PB, todo, 3)
        sums = Squares(XT, 16)
        for n in range(16):
            go(linT([D["w_out"][n, :, 768:1280]], H, os_, n, residual, (6, 7, 8, 9)))
            if n:
                sums.add(xt[n - 1])
        fence()
        st.close()

        st = ExitStack()
        al = allocator(st)
        share(5, 2, 1)
        FF = Ring([Buf((tiles(al(8 * S, f32r)), tiles(al(8 * S, f32r)))) for _ in range(2)])
        CA = Ring([Buf(al(S)) for _ in range(6)])
        NT = Ring([Buf(al(S)) for _ in range(5)])
        h2 = rmsnorm(XT, "norm_mlp", 16, xt, NT, pair=H, sums=sums)

        def conv3(n, o, tok):
            b = CA.next()
            t = act(b.ap, o, ACT.Identity, [tok, t_vec] + b.free, bias=vcol("conv_b", n), scale=vcol("conv_w", n))
            for j in (1, 2):
                t = stt(b.ap[:, j:S], o[:, 0:S - j], vcol("conv_w", 88 * j + n), b.ap[:, j:S], ALU.mult, ALU.add, [t])
            return b, t

        def up(n, ffb, k, ft):
            got = []

            def f_up(m, o, tok):
                got.append(conv3(m, o, tok))
                return [got[-1][1]]
            go(linT(two(D["w_up"], n), H, h2, n, f_up))
            go(linT(two(D["w_up"], 44 + n), H, h2, 44 + n, f_up))
            (ba, ta), (bg, tgg) = got
            t = act(bg.ap, bg.ap, ACT.Silu, [tgg])
            t = tt(ba.ap, ba.ap, bg.ap, ALU.mult, [t, ta])
            bg.free = [t]
            ft.append(halves(ffb.ap[0][:, k, :], ffb.ap[1][:, k, :], ba.ap, [t] + ffb.free))
            ba.free = [ft[-1]]

        def down(c, ffb, ft, sums=None):
            m = len(ft)
            for n in range(16):
                go(linT([D["w_down"][n, :, c * COLS:c * COLS + m * 128]], ffb.ap, ft, n, residual))
                if sums and n:
                    sums.add(xt[n - 1])
            ffb.free = [P.last()]

        before = None
        for c in range(6):
            ffb, ft = FF.next(), []
            for k in range(8 if c < 5 else 4):
                up(8 * c + k, ffb, k, ft)
                if k == 1 and before:
                    down(*before)
            before = (c, ffb, ft)
        sums = Squares(XT, 16)
        down(*before, sums)
        again = Squares(XT, 16, NT)
        xt = rmsnorm(XT, "norm_final", 16, xt, NT, dst=XT, sums=sums, then=again)
        ends = fence()
        st.close()

        st = ExitStack()
        al = allocator(st)
        ots = al(16 * S)
        share(3, 1, 2)
        o2, Y = tiles(ots), tiles(al(16 * S))
        st2 = ExitStack()
        al = allocator(st2)
        LH, LL = tiles(al(10 * S, f32r)), tiles(al(10 * S, f32r))
        lat = o2
        HB = Ring([Buf([tiles(al(2 * S)), tiles(al(2 * S)), al(S),
                        al(512).rearrange("p (i c) -> p i c", i=2)]) for _ in range(3)])
        kp = al(S)
        SB = Ring([Buf(al(S)) for _ in range(4)])
        PB = Ring([Buf(al(S)) for _ in range(3)])
        small = smalls(al(64), 8)
        RW = Ring([Buf(al(S), Chan(sem(f"s_r{i}"))) for i in range(2)])
        for b in RW.bufs:
            b.free = ends
        RS = Ring([Buf([al(S) for _ in range(4)]) for i in range(2)])
        RO = Ring([Buf(al(S)) for _ in range(2)])
        NT = Ring([Buf(Y[:, i, :]) for i in range(10, 16)])
        sp = [al(16) for _ in range(4)]
        n4 = rmsnorm(XT, "attn_norm_2", 16, xt, NT, pair=H, sums=again)
        lt = [None] * 10

        def f_lat(base):
            def f(n, o, tok):
                lt[base + n] = copy(lat[:, base + n, :], o, [tok])
                return [lt[base + n]]
            return f
        for n in range(6):
            go(linT(two(D["w_cq"], n), H, n4, n, f_lat(0)))
        for n in range(4):
            go(linT(two(D["w_ckv"], n), H, n4, n, f_lat(6)))

        def rope(o, dst, waits):
            sw = RO.next()
            for b in (0, 64):
                for x, y in ((b, b + 32), (b + 32, b)):
                    t = act(sw.ap[x:x + 32, :], o[y:y + 32, :], ACT.Copy, waits + sw.free)
            t2 = tt(dst, o, cc("cos"), ALU.mult, [t, t_cst])
            t = tt(sw.ap, sw.ap, cc("sin"), ALU.mult, [t])
            t = tt(dst, dst, sw.ap, ALU.add, [t, t2])
            sw.free = [t]
            return t

        kpt = []

        def f_kr(_, o, tok):
            kpt.append(rope(o, kp, [tok]))
            return [kpt[0]]
        go(linT(two(D["w_kr"], 0), H, n4, 0, f_kr))
        Lq, Lk = (LH[:, 0:6, :], LL[:, 0:6, :]), (LH[:, 6:10, :], LL[:, 6:10, :])

        lam = vcol("lru_lambda_2", 0, 16)
        t = act(sp[0], lam, ACT.Abs, [t_vec])
        t = act(sp[0], sp[0], ACT.Exp, [t], scale=-1.0)
        t1 = ts(sp[1], sp[0], 2.0, None, ALU.add, waits=[t])
        t1 = recip(sp[1], sp[1], [t1])
        t1 = tt(sp[1], sp[1], sp[0], ALU.mult, [t1])
        t2 = tt(sp[2], sp[1], sp[1], ALU.mult, [t1])
        t2 = ts(sp[3], sp[2], 1.0 / 19, 1.0 / 17, ALU.mult, ALU.add, [t2])
        for d in (15, 13, 11, 9, 7, 5, 3, 1):
            t2 = tt(sp[3], sp[3], sp[2], ALU.mult, [t2])
            t2 = ts(sp[3], sp[3], 1.0 / d, None, ALU.add, waits=[t2])
        t2 = tt(sp[3], sp[3], sp[1], ALU.mult, [t2])
        t2 = ts(sp[3], sp[3], 16.0, None, ALU.mult, waits=[t2])
        t2 = ts(sp[0], lam, -1.0, 0.0, ALU.mult, ALU.max, [t2])
        t2 = stt(sp[3], sp[0], 8.0, sp[3], ALU.mult, ALU.add, [t2])
        t_sp = ts(sp[2], sp[3], -1.0, None, ALU.mult, waits=[t2])
        for v in (sp[2], sp[3]):
            t_sp = ts(v, v, 0.5, None, ALU.mult, waits=[t_sp])
        for v, name in zip(sp[0:2], ("b_rg_a_2", "b_rg_x_2")):
            t_sp = ts(v, vcol(name, 0, 16), 0.5, None, ALU.mult, waits=[t_sp])

        yt = [None] * 16

        def recurrent(j):
            sr = RS.next()
            xc, r, w, z = sr.ap
            rw = RW.next()
            t_rw = SP.dma(lambda e: e.dma_start(rw.ap, D["w_rg"][j]), rw.chan, rw.free)
            got = []

            def f_x(n, o, tok):
                t = act(xc, o, ACT.Identity, [tok, t_vec] + sr.free, bias=vcol("conv_b_2", n),
                        scale=vcol("conv_w_2", 48 + n))
                for k in (1, 2, 3):
                    t = stt(xc[:, k:S], o[:, 0:S - k], vcol("conv_w_2", 16 * (3 - k) + n), xc[:, k:S],
                            ALU.mult, ALU.add, [t])
                got.append(t)
                return [t]

            def f_y(n, o, tok):
                y = Y[:, n, :]
                t = act(y, o, ACT.Square, [tok] + nt_read)
                t = ts(y, y, 0.044715, 1.0, ALU.mult, ALU.add, [t])
                t = tt(y, y, o, ALU.mult, [t])
                t = act(y, y, ACT.Tanh, [t], scale=0.7978845608028654)
                got.append(stt(y, y, 1.0, o, ALU.add, ALU.mult, [t]))
                return [got[-1]]
            yield from linT(two(D["w_xr"], j), H, n4, j, f_x)
            yield from linT(two(D["w_yr"], j), H, n4, j, f_y)
            t_xc, t_y = got
            ps = PP.next()
            mm(ps.ap[:, 0:S], rw.ap[:, 0:128], xc, True, True, [t_rw, t_xc] + ps.free)
            tok = mm(ps.ap[:, S:2 * S], rw.ap[:, 128:256], xc, True, True, [], True)
            rw.free = [tok]
            t_i = act(w, ps.ap[:, S:2 * S], ACT.Tanh, [tok, t_sp] + sr.free, bias=sp[1][:, j:j + 1], scale=0.5)
            t_r = act(r, ps.ap[:, 0:S], ACT.Tanh, [], bias=sp[0][:, j:j + 1], scale=0.5)
            ps.free = [t_r]
            t_g = stt(xc, w, 1.0, xc, ALU.add, ALU.mult, [t_i, tok])
            t_t = act(w, r, ACT.Tanh, [t_r, t_g], bias=sp[3][:, j:j + 1], scale=sp[3][:, j:j + 1])
            t_a = act(r, r, ACT.Exp, [t_t], bias=sp[2][:, j:j + 1], scale=sp[2][:, j:j + 1])
            t = ts(z, w, 1.0, None, ALU.add, waits=[t_t])
            t = recip(z, z, [t])
            t = stt(w, w, 0.5, z, ALU.mult, ALU.mult, [t])
            t = act(w, w, ACT.Sqrt, [t])
            t = vset(w[:, 0:1], 0.5, [t])
            t = tt(w, w, xc, ALU.mult, [t])
            t = V(lambda e: e.tensor_tensor_scan(z, r, w, 0.0, ALU.mult, ALU.add), [t, t_a])
            yt[j] = stt(Y[:, j, :], Y[:, j, :], 0.5, z, ALU.mult, ALU.mult, [t, t_y])
            sr.free = [yt[j]]

        nt_read = []
        go(recurrent(0))
        lq = rmsnorm(lat[:, 0:6, :], "q_norm_2", 6, lt[0:6], NT, pair=Lq)
        go(recurrent(1))
        lk = rmsnorm(lat[:, 6:10, :], "kv_norm_2", 4, lt[6:10], NT, pair=Lk)
        nt_read = [P.last(), V.last()]
        go(recurrent(2))
        to = [None] * 16
        heads = {}

        def project(p):
            hb = HB.next()
            qn, kn, qp, mv = hb.ap
            d = {"hb": hb, "t": []}

            def put(dst):
                def f(_, o, tok):
                    d["t"].append(copy(dst, o, [tok] + hb.free))
                    return [d["t"][-1]]
                return f

            def f_qp(_, o, tok):
                d["t"].append(rope(o, qp, [tok] + hb.free))
                return [d["t"][-1]]

            def f_v(i, o, tok):
                d["t"].append(copy(mv[:, i, :], o, [tok] + hb.free))
                return [d["t"][-1]]
            for j in range(2):
                yield from linT([D["w_qn"][2 * p + j]], Lq, lq, 0, put(qn[:, j, :]))
            yield from linT([D["w_qp"][p]], Lq, lq, 0, f_qp)
            for j in range(2):
                yield from linT([D["w_kn"][2 * p + j]], Lk, lk, 0, put(kn[:, j, :]))
            yield from linN([D["w_v"][p]], Lk, lk, 256, f_v)
            heads[p] = d

        def mla_front(job):
            h, i = job["h"], job["i"]
            d = heads[h // 2]
            qn, kn, qp, mv = d["hb"].ap
            j, b, nk = h % 2, 64 * (h % 2), (i + 1) * 128
            job["parts"] = [{
                "qk": [(qn[:, j, i * 128:(i + 1) * 128], kn[:, j, 0:nk]),
                       (qp[b:b + 64, i * 128:(i + 1) * 128], kp[b:b + 64, 0:nk])],
                "toks": d["t"] + [kpt[0]], "bias": cc("mask")[:, 128 - 128 * i:S], "btoks": [t_cst],
                "v": lambda b, j=j, mv=mv: mv[:, b, 128 * j:128 * j + 128], "vtoks": d["t"],
                "out": job["ps"].ap[:, i * 128:(i + 1) * 128], "start": True, "stop": True}]
            softmax(job, SB, small)

        def mla_back(job):
            h, ps = job["h"], job["ps"]
            job["parts"][0]["ofree"] = ps.free

            def finish(tok):
                to[h] = copy(o2[:, h, :], ps.ap[:, 0:S], [tok] + lat_read)
                ps.free = [to[h]]
                if h % 2:
                    heads[h // 2]["hb"].free = [tok]
            if job["i"] == 1:
                job["done"] = finish
            attend(job)

        lat_read = [lq[-1], lk[-1]]
        jobs = []
        for h in range(16):
            ps = PO.next()
            for i in range(2):
                jobs.append({"h": h, "i": i, "ps": ps, "scale": 192.0 ** -0.5})
        go(project(0))
        go(recurrent(3))
        go(project(1))
        todo = []
        for p in range(6):
            todo += [(recurrent(4 + 2 * p), 4), (project(2 + p), 7, 4 * p + 3, 4 * p + 8), (recurrent(5 + 2 * p), 4)]
        weave(jobs, mla_front, mla_back, PB, todo, 2)
        fence()
        st2.close()
        st2 = ExitStack()
        al = allocator(st2)
        OQ = tiles(al(16 * S, f32r)), tiles(al(16 * S, f32r))
        YQ = tiles(al(16 * S, f32r)), tiles(al(16 * S, f32r))
        GB = Ring([Buf(nrm[:, i * S:(i + 1) * S]) for i in range(2)])
        tos, tys, tm = [None] * 16, [None] * 16, [None] * 16
        M = o2

        def f_sig(g, col):
            def f(_, o, tok):
                g.free = [act(g.ap, o, ACT.Sigmoid, [tok, t_vec] + g.free, bias=vcol("b_gate_2", col))]
                return g.free
            return f
        for n in range(16):
            tos[n] = halves(OQ[0][:, n, :], OQ[1][:, n, :], o2[:, n, :], [to[n]])
        for n in range(16):
            g = GB.next()

            def f_o(m, o, tok):
                tm[m] = tt(M[:, m, :], o, g.ap, ALU.mult, [tok, tos[m]] + g.free)
                g.free = [tm[m]]
                return [tm[m]]
            go(linT(two(D["w_ga"], n), H, n4, n, f_sig(g, n)))
            go(linT(two(D["w_attn_o"], n), OQ, tos, n, f_o))
            tys[n] = halves(YQ[0][:, n, :], YQ[1][:, n, :], Y[:, n, :], [yt[n]])
        oq_read = [P.last()]
        tms = [None] * 16
        for n in range(16):
            g = GB.next()

            def f_y2(m, o, tok):
                t = tt(g.ap, o, g.ap, ALU.mult, [tok] + g.free)
                t1 = tt(M[:, m, :], M[:, m, :], g.ap, ALU.add, [t, tm[m]])
                g.free = [t1]
                tms[m] = halves(OQ[0][:, m, :], OQ[1][:, m, :], M[:, m, :], [t1] + oq_read)
                return [t]
            go(linT(two(D["w_gr"], n), H, n4, n, f_sig(g, 16 + n)))
            go(linT(two(D["w_rnn_o"], n), YQ, tys, n, f_y2))
        sums = Squares(XT, 16)
        for n in range(16):
            go(linT(two(D["w_out_2"], n), OQ, tms, n, residual))
            if n:
                sums.add(xt[n - 1])
        ends = fence()
        st2.close()
        st.close()

        outer, st = ExitStack(), ExitStack()
        emb = tiles(allocator(outer)(16 * S))
        al = allocator(st)
        share(4, 1, 3)
        sk = al(2048)
        UT = 2048 - UD
        xn = al(2 * UT).rearrange("p (i c) -> p i c", i=2)
        acc = al(2048)
        pqs = al(16 * S)
        pq = tiles(pqs)
        eidx, epos = (al(256).bitcast(i32).rearrange("p (i k) -> p i k", i=2) for _ in range(2))
        gat, actv, elem = (al(256).rearrange("p (i k) -> p i k", i=2) for _ in range(3))
        SC = Ring([Buf(al(256))])
        s2 = Ring([Buf(al(256)) for _ in range(2)])
        ST = Ring([Buf(al(512), Chan(sem(f"s_a{i}"))) for i in range(2)])
        cand = al(256).rearrange("p (a b) -> p a b", a=16)
        oh = [al(256).rearrange("p (a b) -> p a b", a=16) for _ in range(2)]
        tvl, tfl = (al(32).rearrange("p (c k) -> p c k", c=2) for _ in range(2))
        til = al(32).bitcast(u32).rearrange("p (c k) -> p c k", c=2)
        bv, bf, e1 = al(16), al(32), al(32)
        bc, bd = al(16).bitcast(u32), al(32).bitcast(u32)
        hsm = al(8)
        n5 = tiles(al(UT // 128 * S))
        big = [al(2048) for _ in range(3)]
        NT = Ring([Buf(pq[:, i, :]) for i in range(5)])
        t_n5 = rmsnorm(XT, "ffn_norm_2", 16, xt, NT, pair=H, dst=n5, first=UD // 128, sums=sums)
        ch_k = Chan(sem("s_k"))
        t_sk = SP.dma(lambda e: e.dma_start(sk, D["subkeys"]), ch_k, ends)
        tpq = [None] * 16
        pq_free = [P.last(), V.last()]

        def f_pq(n, o, tok):
            tpq[n] = act(pq[:, n, :], o, ACT.Copy, [tok] + pq_free)
            return [tpq[n]]

        def to_pq(n):
            return linT(two(D["w_peer_q"], n), H, t_n5, n, f_pq)
        stored = {}

        def dense(c):
            def f(i, o, tok):
                b = ST.next()
                t = act(b.ap, o, ACT.Copy, [tok] + b.free)
                dst = D["dense"][i * 128:(i + 1) * 128, 512 * c:512 * c + 512]
                b.free = [SP.dma(lambda e: e.dma_start(dst, b.ap), b.chan, [t])]
                stored[b] = b.free[0]
                return [t]
            return linN([D["u_dense"][c, :, j:j + COLS] for j in range(0, 4 * UD, COLS)], H, t_n5, 512, f, (2,))
        txn = [None, None]

        def natural(i):
            pt = PT.next()
            for k in range(UT // 128):
                tok = tr(pt.ap[:, k * 128:(k + 1) * 128], n5[:, k, i * 128:(i + 1) * 128],
                         [t_n5[UD // 128 + k]] + pt.free, k == UT // 128 - 1)
            txn[i] = act(xn[:, i, :], pt.ap[:, 0:UT], ACT.Copy, [tok])
            pt.free = [txn[i]]

        def top16(vals, idx, src, n, tok):
            b = s2.next()
            w = b.ap[:, 0:n]
            t = V(lambda e: e.max(vals[:, 0:8], src), [tok])
            V(lambda e: e.max_index(idx[:, 0:8], vals[:, 0:8], src), [t])
            t = V(lambda e: e.match_replace(w, vals[:, 0:8], src, LOW), [t] + b.free)
            yield 3 * n
            t = V(lambda e: e.max(vals[:, 8:16], w), [t])
            t = V(lambda e: e.max_index(idx[:, 8:16], vals[:, 8:16], w), [t])
            b.free = [t]
            yield 2 * n
            return t

        tga, tei, tep, scored, tpart, tco = {}, {}, {}, {}, {}, {}

        def score(i, h):
            ps = PS.next()
            for c in range(2):
                n = 2 * h + c
                tok = mm(ps.ap[:, c * 128:(c + 1) * 128], pq[:, n, i * 128:(i + 1) * 128],
                         sk[:, n * 128:(n + 1) * 128], True, True, [tpq[n], t_sk] + ps.free, c == 1)
            b = SC.next()
            t = act(b.ap, ps.ap[:, 0:256], ACT.Copy, [tok] + b.free)
            ps.free = [t]
            scored[i, h] = (b, t)
            return tok

        def select(i, h):
            b, t = scored[i, h]
            for c in range(2):
                t2 = yield from top16(tvl[:, c, :], til[:, c, :], b.ap[:, c * 128:(c + 1) * 128], 128, t)
            b.free = [t2]
            t = vcopy(tfl, til, [t2])
            t = tt(cand, tvl[:, 0, :].unsqueeze(2).to_broadcast([128, 16, 16]),
                   tvl[:, 1, :].unsqueeze(1).to_broadcast([128, 16, 16]), ALU.add, [t2])
            t2 = yield from top16(bv, bc, cand.rearrange("p a b -> p (a b)"), 256, t)
            for c, (op, k) in enumerate(((ALU.logical_shift_right, 4), (ALU.bitwise_and, 15))):
                t = ts(bd[:, 16 * c:16 * c + 16], bc, k, None, op, waits=[t2])
            t = vcopy(bf, bd, [t])
            for c in range(2):
                a = tt(oh[c], bf[:, 16 * c:16 * c + 16].unsqueeze(2).to_broadcast([128, 16, 16]),
                       cc("iota").unsqueeze(1).to_broadcast([128, 16, 16]), ALU.is_equal, [t, t_cst])
                a = tt(oh[c], oh[c], tfl[:, c, :].unsqueeze(1).to_broadcast([128, 16, 16]), ALU.mult, [a])
                a = red(e1[:, 16 * c:16 * c + 16], oh[c], ALU.add, [a])
                yield 768
            a = stt(e1[:, 0:16], e1[:, 0:16], 128.0, e1[:, 16:32], ALU.mult, ALU.add, [a])
            tei[i, h] = vcopy(eidx[:, i, 16 * h:16 * h + 16], e1[:, 0:16], [a])
            a = ts(e1[:, 16:32], e1[:, 0:16], cc("row")[:, i:i + 1], None, ALU.add, waits=[a])
            tep[i, h] = vcopy(epos[:, i, 16 * h:16 * h + 16], e1[:, 16:32], [a])
            g = gat[:, i, 16 * h:16 * h + 16]
            t = ts(g, bv, bv[:, 0:1], None, ALU.subtract, waits=[t2])
            t = act(g, g, ACT.Exp, [t], accum_out=hsm[:, 0:1])
            t = recip(hsm[:, 0:1], hsm[:, 0:1], [t])
            tga[i, h] = ts(g, g, hsm[:, 0:1], None, ALU.mult, waits=[t])
            yield 768

        per = 2048 // UT
        rows_u = Ring([Buf(b[:, j * UT:(j + 1) * UT], Chan(sem(f"s_u{n}_{j}")))
                       for n, b in enumerate(big + [acc]) for j in range(per)])
        ch_e = [Chan(sem(f"s_e{j}")) for j in range(6)]
        got = {}

        def gather(table, dst, chan, ix, waits):
            return G.dma(lambda e: e.indirect_dma_start(
                out=dst, out_offset=None, in_=D[table],
                in_offset=bass.IndirectOffsetOnAxis(ap=ix, axis=0)), chan, waits)

        def experts_in(n):
            for k in range(16):
                if 0 <= n < 16:
                    i, h = todo[n]
                    s, ld = got[n, k]
                    a, x, ac = s.ap, xn[:, i, :], actv[:, i, 16 * h + k:16 * h + k + 1]
                    tpart[i, h] = V(lambda e, a=a, x=x, ac=ac: e.tensor_tensor_reduce(
                        out=a, in0=a, in1=x, scale=1.0, scalar=0.0, op0=ALU.mult, op1=ALU.add, accum_out=ac),
                        [ld, txn[i]])
                    s.free = [tpart[i, h]]
                if 0 <= n + 1 < 16:
                    i, h = todo[n + 1]
                    s = rows_u.next()
                    got[n + 1, k] = s, gather("u_rest", s.ap, s.chan, eidx[:, i, 16 * h + k:16 * h + k + 1],
                                              [tei[i, h]] + s.free)
                yield UT if n >= 0 else 0

        def together(main, side):
            spent, n = 0, 0
            total = 256 * UT + 16 * (5 * 512 + 3 * 768)
            pieces = sum(m[1] for m in main)
            for gen, _ in main:
                for _ in gen:
                    n += 1
                    while spent * pieces < total * n:
                        step = next(side, None)
                        if step is None:
                            break
                        spent += step
            go(side)

        go(to_pq(0))
        go(to_pq(1))
        for i in range(2):
            natural(i)
        todo = [(i, h) for i in range(2) for h in range(8)]
        read = []

        def heads_in():
            for n in range(18):
                if n < 16:
                    read[:] = [score(*todo[n])]
                if n:
                    yield from experts_in(n - 2)
                if n < 16:
                    yield from select(*todo[n])
        main = [(to_pq(n), 2) for n in (2, 3)]
        for n in range(7):
            main += [(to_pq(2 * n + j), 2) for j in (4, 5) if n < 6] + [(dense(n), UD // 256)]
        main += [(dense(n), UD // 256) for n in range(7, 32)]
        together(main, heads_in())
        written = list(stored.values())
        rows_v = Ring([Buf(b, Chan(sem(f"s_v{j}"))) for j, b in enumerate(
            [pqs[:, 0:2048], pqs[:, 2048:4096]] + big)])
        for n, b in enumerate(rows_v.bufs):
            b.free = read if n < 2 else [tpart[1, 7]]
        last = {"acc": None, "read": [tpart[1, 7]]}

        def pick(n, k):
            i, h = todo[n]
            c = ch_e[2 + k // 4 if n == 0 else n % 2]
            got[n, k // 4] = gather("dense_flat", elem[:, i, 16 * h + k:16 * h + k + 1], c,
                                    epos[:, i, 16 * h + k:16 * h + k + 1], [tep[i, h]] + written)

        row = {}

        def fetch(g):
            if g < 256:
                i, h = todo[g // 16]
                k = 16 * h + g % 16
                s = rows_v.next()
                row[g] = s, gather("peer_v", s.ap, s.chan, eidx[:, i, k:k + 1], [tei[i, h]] + s.free)

        def coefficients(n, parts):
            i, h = todo[n]
            w = 16 // parts
            for c in range(parts):
                a = actv[:, i, 16 * h + c * w:16 * h + c * w + w]
                t = tt(a, a, elem[:, i, 16 * h + c * w:16 * h + c * w + w], ALU.add,
                       [got[n, c if parts == 4 else 3], tpart[i, h]])
                t = act(a, a, ACT.Gelu_apprx_tanh, [t])
                t = tt(a, a, gat[:, i, 16 * h + c * w:16 * h + c * w + w], ALU.mult, [t, tga[i, h]])
                for k in range(c * w, c * w + w):
                    tco[n, k] = t
                yield

        def experts_out(n):
            i, h = todo[n]
            co = coefficients(n, 1 if n else 4)
            for k in range(16):
                if k % 4 == 0:
                    next(co, None)
                s, ld = row[16 * n + k]
                c = actv[:, i, 16 * h + k:16 * h + k + 1]
                if h == 0 and k == 0:
                    t = ts(acc, s.ap, c, None, ALU.mult, waits=[tco[n, k], ld] + last["read"])
                else:
                    t = stt(acc, s.ap, c, acc, ALU.mult, ALU.add, [tco[n, k], ld, last["acc"]])
                s.free = [t]
                last["acc"] = t
                fetch(16 * n + k + len(rows_v.bufs))
                if n < 15 and k < 8:
                    pick(n + 1, 2 * k)
                    pick(n + 1, 2 * k + 1)

        ch_p = Chan(sem("s_p"))
        ppT = [o.rearrange("p a b -> p (a b)") for o in oh]
        read_h = [P.last()]
        tpe = [None] * 16

        def embedding():
            for k in range(2):
                t_pp = SP.dma(lambda e, k=k: e.dma_start(ppT[k], D["pT"][128 * k:128 * k + 128]), ch_p, [tga[1, 7]])
            tph = [halves(HH[:, k, :], HL[:, k, :], ppT[k], [t_pp] + read_h) for k in range(2)]
            for c in range(4):
                b, ld = piece(D["w_ple_proj"][c])
                for j in range(4):
                    ps = PP.next()
                    for k in range(2):
                        for x, y in THREE:
                            w = b.ap[x][:, j * 256 + k * 128:j * 256 + k * 128 + 128]
                            tok = mm(ps.ap[:, 0:S], w, H[y][:, k, :], k + x + y == 0, k == 1 and (x, y) == THREE[-1],
                                     [ld, tph[k]] + ps.free, k == 1 and (x, y) == THREE[-1])
                    tpe[4 * c + j] = act(emb[:, 4 * c + j, :], ps.ap[:, 0:S], ACT.Copy, [tok])
                    ps.free = [tpe[4 * c + j]]
                done(b, tok)

        def merge(i):
            sums = Squares(XT, 16) if i else None
            for c in range(16):
                pt = PT.next()
                tok = tr(pt.ap[:, 0:128], acc[:, c * 128:(c + 1) * 128], [last["acc"]] + pt.free, True)
                x = XT[:, c, i * 128:(i + 1) * 128]
                xt[c] = tt(x, pt.ap[:, 0:128], x, ALU.add, [tok, xt[c]])
                pt.free = [xt[c]]
                if i and c:
                    sums.add(xt[c - 1])
            last["read"] = [tok]
            return sums

        for k in range(len(rows_v.bufs)):
            fetch(k)
        for k in range(16):
            pick(0, k)
        for n in range(16):
            experts_out(n)
            if n == 0:
                embedding()
            if n % 8 == 7:
                sums = merge(n // 8)
        fence()
        st.close()

        st = ExitStack()
        al = allocator(st)
        GB = Ring([Buf(al(S)) for _ in range(3)])
        NT = Ring([Buf(al(S)) for _ in range(6)])
        fin = tiles(al(16 * S))
        ch_o = Chan(sem("s_out"))
        n6 = rmsnorm(XT, "ple_norm_2", 16, xt, NT, pair=H, sums=sums)
        sums = Squares(XT, 16)
        for n in range(16):
            g = GB.next()

            def f_pg(m, o, tok):
                t = act(g.ap, o, ACT.Sigmoid, [tok] + g.free)
                t1 = tt(g.ap, g.ap, emb[:, m, :], ALU.mult, [t, tpe[m]])
                xt[m] = tt(XT[:, m, :], XT[:, m, :], g.ap, ALU.add, [t1, xt[m]])
                g.free = [xt[m]]
                return [t]
            go(linT(two(D["w_ple_gate"], n), H, n6, n, f_pg))
            if n:
                sums.add(xt[n - 1])
        t_f = rmsnorm(XT, "final_norm_2", 16, xt, NT, dst=fin, sums=sums)
        for c in range(4):
            t = SP.dma(lambda e, c=c: e.dma_start(
                out[512 * c:512 * c + 512, :].rearrange("(k p) t -> p k t", p=128), fin[:, 4 * c:4 * c + 4, :]),
                ch_o, [t_f[4 * c + 3]])
        SP.wait([t])
        st.close()
        outer.close()
        return listed, (P, A, V, G, SP)

    with base:
        listed, _ = walk(None, 0)
        _, (P, A, V, G, SP) = walk(listed, 1)
        block = base.enter_context(nc.Block())

        @block.sync
        def _(eng):
            SP.play(eng)

        @block.tensor
        def _(eng):
            P.play(eng)

        @block.scalar
        def _(eng):
            A.play(eng)

        @block.vector
        def _(eng):
            V.play(eng)

        @block.gpsimd
        def _(eng):
            G.play(eng)


def constants():
    import numpy as np
    import math
    f = np.float32
    p = np.arange(128)
    ident = np.eye(128, dtype=f)
    mask = np.where(np.arange(256)[None, :] <= 128 + p[:, None], 0.0, NEG).astype(f)
    half = 32
    inv = (1.0 / (np.float32(10000.0) ** (np.arange(half, dtype=f) / f(half)))).astype(f)
    ang = np.arange(256, dtype=f)[:, None] * inv[None, :]
    cos, sin = np.cos(ang).astype(f).T, np.sin(ang).astype(f).T
    cos4 = np.concatenate([cos] * 4, 0)
    sin4 = np.concatenate([-sin, sin, -sin, sin], 0)
    end = np.arange(15) * 16 + 31
    ok = np.stack([(end[None, :] <= (128 * i + p)[:, None]) for i in range(2)], 1).reshape(128, 30)
    iota = np.broadcast_to(np.arange(16, dtype=f), (128, 16))
    cst = np.concatenate([ident, ident[:, ::-1], mask, cos4, sin4, ok.astype(f), np.where(ok, 0.0, NEG).astype(f), iota,
                          np.stack([p * 16384, (p + 128) * 16384], 1).astype(f)], 1)
    dist = 255 - np.arange(384)
    n = np.maximum(dist, 0)
    nf = np.maximum(n, 1).astype(f)
    large = 16 + (np.log(nf / f(16)) / f(math.log(2048 / 16)) * f(16)).astype(np.int32)
    bucket = np.where(n < 16, n, np.minimum(large, 31))
    oneh = np.zeros((33, 4, 384), f)
    for v, (d, far) in enumerate(((1, 128), (4, 512), (16, 2048), (1, 10 ** 6))):
        good = (dist >= 0) & (dist % d == 0) & (dist <= far)
        oneh[bucket, v, np.arange(384)] = good
        oneh[32, v] = np.where(good, 0.0, NEG)
    return np.ascontiguousarray(cst.astype(f)), np.ascontiguousarray(oneh.reshape(33, 4 * 384))


def layout(inp):
    import numpy as np
    g = {k: np.asarray(v) for k, v in inp.items()}

    def tiles(w, c=128):
        k, n = w.shape
        return np.ascontiguousarray(w.reshape(k // 128, 128, n // c, c).transpose(2, 1, 0, 3)).reshape(
            n // c, 128, (k // 128) * c)

    def cols(v):
        v = v.reshape(-1, v.shape[-1])
        return v.reshape(v.shape[0], -1, 128).transpose(2, 0, 1).reshape(128, -1)

    d = {}
    x = g["x"][0]
    d["xT"] = np.ascontiguousarray(x.T)
    d["pT"] = np.ascontiguousarray(g["p_2"][0, 0].T)
    d["vec"] = np.ascontiguousarray(np.concatenate([cols(g[n]) for n, _ in VEC], 1))
    d["cst"], d["oneh"] = constants()
    d["relT"] = np.ascontiguousarray(np.concatenate(
        [g["rel_table"].T, np.ones((1, 32), np.float32)], 0))
    d["peT"] = np.ascontiguousarray(g["cmp_pe"][0].transpose(2, 0, 1)).reshape(64, 64)
    d["cw2"] = np.ascontiguousarray(g["cmp_w2"][0].transpose(1, 0, 2)).reshape(128, 128)
    d["cw1"] = np.ascontiguousarray(
        g["cmp_w1"][0].reshape(2, 4, 8, 64, 128).transpose(0, 1, 3, 2, 4)).reshape(2, 4, 64, 1024)
    w = g["w_in"][0]
    d["w_in"] = tiles(w[:, :4608])
    kv = w[:, 4608:5760].reshape(2048, 6, 3, 64)
    d["w_cmp"] = tiles(kv[:, 0:2].reshape(2048, 384))
    d["w_kdup"] = tiles(np.stack([kv[:, 2:5:2]] * 2, 3).reshape(2048, 768))
    d["w_vcg"] = tiles(np.concatenate([kv[:, 3:6:2].reshape(2048, 384), w[:, 5760:]], 1), 420)
    d["w_v1"] = tiles(np.concatenate([w[:, 128 * c:128 * c + 256] for c in (4, 10, 16, 26, 28)], 1), 256)
    d["w_out"] = tiles(g["w_out"][0])
    d["w_up"] = tiles(g["w_up"][0])
    d["w_down"] = tiles(g["w_down"][0])
    w = g["w_in_2"][0]
    at = 0
    for name, n in (("w_cq", 768), ("w_ckv", 512), ("w_kr", 64), ("w_xr", 2048),
                       ("w_yr", 2048), ("w_ga", 2048), ("w_gr", 2048)):
        part = w[:, at:at + n]
        d[name] = tiles(np.concatenate([part, part], 1) if n == 64 else part, 128)
        at += n
    w = g["w_uq_2"][0].reshape(768, 16, 192)
    d["w_qn"] = tiles(np.ascontiguousarray(w[:, :, :128]).reshape(768, 2048))
    d["w_qp"] = tiles(np.ascontiguousarray(w[:, :, 128:]).reshape(768, 1024))
    w = g["w_ukv_2"][0].reshape(512, 16, 256)
    d["w_kn"] = tiles(np.ascontiguousarray(w[:, :, :128]).reshape(512, 2048))
    d["w_v"] = tiles(np.ascontiguousarray(w[:, :, 128:]).reshape(512, 2048), 256)
    d["w_rg"] = np.ascontiguousarray(np.concatenate([g["w_rg_a_2"][0], g["w_rg_x_2"][0]], 2))
    for name in ("w_attn_o", "w_rnn_o", "w_out", "w_peer_q", "w_ple_gate", "w_ple_proj"):
        d[name + ("_2" if name == "w_out" else "")] = tiles(g[name + "_2"][0])
    d["w_ple_proj"] = np.ascontiguousarray(
        d["w_ple_proj"].reshape(4, 4, 128, 256).transpose(0, 2, 1, 3)).reshape(4, 128, 1024)
    d["subkeys"] = np.ascontiguousarray(
        g["peer_subkeys_2"][0].reshape(16, 128, 128).transpose(2, 0, 1)).reshape(128, 2048)
    u = g["peer_u_2"][0]
    d["u_dense"] = np.ascontiguousarray(
        u[:, :UD].reshape(32, 512, UD // 128, 128).transpose(0, 3, 2, 1)).reshape(32, 128, 4 * UD)
    d["u_rest"] = np.ascontiguousarray(u[:, UD:])
    d["peer_v"] = g["peer_v_2"][0]
    return d


def kernel(**inputs):
    import numpy as np
    import concourse.bacc as bacc
    from concourse.bass_utils import run_bass_kernel_spmd as run

    nc = bacc.Bacc("TRN2", target_bir_lowering=False, num_devices=1)
    arrays = {f"in_{k}": np.ascontiguousarray(v) for k, v in layout(inputs).items()}
    D = {k[3:]: nc.dram_tensor(k, v.shape, mybir.dt.from_np(v.dtype), kind="ExternalInput").ap()
         for k, v in arrays.items()}
    D["dense"] = nc.dram_tensor("dense_scratch", (256, 16384), mybir.dt.float32).ap()
    D["dense_flat"] = D["dense"].rearrange("t (e o) -> (t e) o", o=1)
    D["toe"] = nc.dram_tensor("toe_scratch", (32, 384), mybir.dt.float32).ap()
    out = nc.dram_tensor("out_0", (2048, S), mybir.dt.float32, kind="ExternalOutput").ap()
    program(nc, D, out)
    r = run(nc, [arrays], core_ids=[0])
    return np.ascontiguousarray(r.results[0]["out_0"].T)[None]
```
